# Optimizing a Trainium2 kernel written in Bass

```python
import jax, jax.numpy as jnp
from jax import lax
import numpy as np
import math

D_MODEL = 1024
BATCH = 1
SEQ = 256
DEPTH = 1

CHUNK = 64
D_MIX = D_MODEL
C_CONV = D_MIX // 4
CONV_WIDTH = 31
N_HEADS = 8
HEAD_DIM = 64
D_ATT = N_HEADS * HEAD_DIM
D_Q_LAT = 256
D_KV_LAT = 128
IDX_HEADS = 8
IDX_DIM = 64
TOPK_MAX = 256
Q_BLOCK = 128
C_POOL = D_MIX // 4
POOL_WINDOWS = (2, 4, 8, 16)
POOL_GROUP = C_POOL // 4
N_GROUPS = 4
EXPERTS_PER_GROUP = 8
N_EXPERTS = N_GROUPS * EXPERTS_PER_GROUP
D_EXPERT = 512
MOE_BLOCK = 128
EPS = 1e-6
IN_SPLITS = (C_CONV, C_CONV, D_Q_LAT, D_KV_LAT, IDX_HEADS * IDX_DIM, IDX_DIM, IDX_HEADS, C_POOL)
N_IN = sum(IN_SPLITS)


def _rmsnorm(x, g):
    xf = x.astype(jnp.float32)
    y = xf * lax.rsqrt(jnp.mean(xf * xf, axis=-1, keepdims=True) + EPS)
    return y.astype(x.dtype) * g

def _layernorm(x, g, b):
    xf = x.astype(jnp.float32)
    mu = jnp.mean(xf, axis=-1, keepdims=True)
    var = jnp.mean(jnp.square(xf - mu), axis=-1, keepdims=True)
    return ((xf - mu) * lax.rsqrt(var + EPS)).astype(x.dtype) * g + b

def _conv_module(a_val, a_gate, conv_k, conv_b, ln_g, ln_b):
    u = a_val * jax.nn.sigmoid(a_gate)
    u = lax.conv_general_dilated(
        u, conv_k[:, None, :].astype(u.dtype), window_strides=(1,),
        padding=[(CONV_WIDTH - 1, 0)], dimension_numbers=('NWC', 'WIO', 'NWC'),
        feature_group_count=C_CONV) + conv_b
    return jax.nn.silu(_layernorm(u, ln_g, ln_b))

def _dsa_attention(cq, ckv, qi, ki, wi, q_norm_g, kv_norm_g, w_uq, w_uk, w_uv):
    B, S, _ = ckv.shape
    topk = min(TOPK_MAX, S // 4)
    nb = S // Q_BLOCK
    cq = _rmsnorm(cq, q_norm_g)
    ckv = _rmsnorm(ckv, kv_norm_g)
    q = jnp.einsum('btc,chd->bthd', cq, w_uq)
    q_abs = jnp.einsum('bthd,khd->bthk', q, w_uk)
    qi = qi.reshape(B, S, IDX_HEADS, IDX_DIM)
    key_chunk = jnp.arange(S) // CHUNK
    idx_scale = (IDX_HEADS * IDX_DIM) ** -0.5
    att_scale = HEAD_DIM ** -0.5

    def to_blocks(a):
        return jnp.moveaxis(a.reshape(B, nb, Q_BLOCK, *a.shape[2:]), 1, 0)

    def block(args):
        qa, qib, wib, bi = args
        qchunk = (bi * Q_BLOCK + jnp.arange(Q_BLOCK)) // CHUNK
        allowed = key_chunk[None, :] <= qchunk[:, None]
        rel = jax.nn.relu(jnp.einsum('bqhd,bsd->bqhs', qib, ki).astype(jnp.float32))
        score = jnp.einsum('bqhs,bqh->bqs', rel, wib.astype(jnp.float32)) * idx_scale
        score = jnp.where(allowed[None], score, -jnp.inf)
        _, idx = lax.top_k(score, topk)
        kv_sel = jax.vmap(lambda a, i: a[i])(ckv, idx)
        logits = jnp.einsum('bqhc,bqkc->bqhk', qa, kv_sel).astype(jnp.float32) * att_scale
        valid = (idx // CHUNK) <= qchunk[None, :, None]
        logits = jnp.where(valid[:, :, None, :], logits, -jnp.inf)
        p = jax.nn.softmax(logits, axis=-1).astype(kv_sel.dtype)
        return jnp.einsum('bqhk,bqkc->bqhc', p, kv_sel)

    ctx = lax.map(block, (to_blocks(q_abs), to_blocks(qi), to_blocks(wi), jnp.arange(nb)))
    ctx = jnp.moveaxis(ctx, 0, 1).reshape(B, S, N_HEADS, D_KV_LAT)
    o = jnp.einsum('bthc,chd->bthd', ctx, w_uv)
    return o.reshape(B, S, D_ATT)

def _pool_mixer(u, pool_w, pool_scale):
    B, S, _ = u.shape
    n_pos = jnp.arange(1, S + 1, dtype=jnp.float32)
    outs = []
    for g, w in enumerate(POOL_WINDOWS):
        ug = u[..., g * POOL_GROUP:(g + 1) * POOL_GROUP]
        ugf = ug.astype(jnp.float32)
        cs = jnp.cumsum(ugf, axis=1)
        prev = jnp.pad(cs, ((0, 0), (w, 0), (0, 0)))[:, :S]
        mean = (cs - prev) / jnp.minimum(n_pos, w)[None, :, None]
        outs.append((mean - ugf).astype(u.dtype) @ pool_w[g])
    return jnp.concatenate(outs, axis=-1) * pool_scale

def _hier_moe(h, rg_w, rg_b, re_w, re_b, w1, w3, w2):
    B, S, D = h.shape
    T = B * S
    A = 2 * T
    hf = h.reshape(T, D)
    g_prob = jax.nn.softmax((hf @ rg_w).astype(jnp.float32) + rg_b, axis=-1)
    g_p, g_idx = lax.top_k(g_prob, 1)
    e_logits = jnp.einsum('td,dge->tge', hf, re_w).astype(jnp.float32) + re_b
    e_sel = jnp.take_along_axis(e_logits, g_idx[:, :, None], axis=1)[:, 0]
    e_p, e_idx = lax.top_k(jax.nn.softmax(e_sel, axis=-1), 2)
    e_p = e_p / jnp.sum(e_p, axis=-1, keepdims=True)
    gates = (g_p * e_p).reshape(A)
    a_exp = (g_idx * EXPERTS_PER_GROUP + e_idx).reshape(A).astype(jnp.int32)
    a_tok = jnp.repeat(jnp.arange(T, dtype=jnp.int32), 2)
    order = jnp.argsort(a_exp)
    s_exp = a_exp[order]
    counts = jnp.bincount(a_exp, length=N_EXPERTS)
    starts = jnp.cumsum(counts) - counts
    pcounts = (counts + MOE_BLOCK - 1) // MOE_BLOCK * MOE_BLOCK
    pends = jnp.cumsum(pcounts)
    pstarts = pends - pcounts
    dst = pstarts[s_exp] + jnp.arange(A) - starts[s_exp]
    n_blk = -(-(A + N_EXPERTS * (MOE_BLOCK - 1)) // MOE_BLOCK)
    P = n_blk * MOE_BLOCK
    slot_tok = jnp.zeros((P,), jnp.int32).at[dst].set(a_tok[order])
    slot_gate = jnp.zeros((P,), jnp.float32).at[dst].set(gates[order])
    blk_exp = jnp.minimum(jnp.searchsorted(pends, jnp.arange(n_blk) * MOE_BLOCK, side='right'), N_EXPERTS - 1)

    def run(args):
        tok, e = args
        hb = hf[tok]
        return (jax.nn.silu(hb @ w1[e]) * (hb @ w3[e])) @ w2[e]

    y = lax.map(run, (slot_tok.reshape(n_blk, MOE_BLOCK), blk_exp)).reshape(P, D)
    out = jnp.zeros((T, D), h.dtype).at[slot_tok].add(y * slot_gate[:, None].astype(y.dtype))
    return out.reshape(B, S, D)

def first_inputs(seed: int = 0) -> dict:
    key = jax.random.key(seed)
    ks = jax.random.split(key, 27)

    def nrm(k, shape, scale):
        return jax.random.normal(k, shape, jnp.float32) * scale

    L = DEPTH
    return {
        'x': nrm(ks[0], (BATCH, SEQ, D_MODEL), 1.0),
        'c': nrm(ks[1], (BATCH, D_MODEL), 1.0),
        'mod_w': nrm(ks[2], (L, D_MODEL, 6 * D_MODEL), 0.5 * D_MODEL ** -0.5),
        'mod_b': nrm(ks[3], (L, 6 * D_MODEL), 0.1),
        'norm1_g': 1.0 + nrm(ks[4], (L, D_MODEL), 0.05),
        'w_in': nrm(ks[5], (L, D_MODEL, N_IN), D_MODEL ** -0.5),
        'conv_k': nrm(ks[6], (L, CONV_WIDTH, C_CONV), CONV_WIDTH ** -0.5),
        'conv_b': nrm(ks[7], (L, C_CONV), 0.02),
        'conv_ln_g': 1.0 + nrm(ks[8], (L, C_CONV), 0.05),
        'conv_ln_b': nrm(ks[9], (L, C_CONV), 0.02),
        'q_norm_g': 1.0 + nrm(ks[10], (L, D_Q_LAT), 0.05),
        'kv_norm_g': 1.0 + nrm(ks[11], (L, D_KV_LAT), 0.05),
        'w_uq': nrm(ks[12], (L, D_Q_LAT, N_HEADS, HEAD_DIM), D_Q_LAT ** -0.5),
        'w_uk': nrm(ks[13], (L, D_KV_LAT, N_HEADS, HEAD_DIM), D_KV_LAT ** -0.5),
        'w_uv': nrm(ks[14], (L, D_KV_LAT, N_HEADS, HEAD_DIM), D_KV_LAT ** -0.5),
        'pool_w': nrm(ks[15], (L, len(POOL_WINDOWS), POOL_GROUP, POOL_GROUP), POOL_GROUP ** -0.5),
        'pool_scale': 1.0 + nrm(ks[16], (L, C_POOL), 0.1),
        'w_out': nrm(ks[17], (L, D_MIX, D_MODEL), D_MIX ** -0.5),
        'norm2_g': 1.0 + nrm(ks[18], (L, D_MODEL), 0.05),
        'router_g_w': nrm(ks[19], (L, D_MODEL, N_GROUPS), D_MODEL ** -0.5),
        'router_g_b': nrm(ks[20], (L, N_GROUPS), 0.01),
        'router_e_w': nrm(ks[21], (L, D_MODEL, N_GROUPS, EXPERTS_PER_GROUP), D_MODEL ** -0.5),
        'router_e_b': nrm(ks[22], (L, N_GROUPS, EXPERTS_PER_GROUP), 0.01),
        'exp_w1': nrm(ks[23], (L, N_EXPERTS, D_MODEL, D_EXPERT), D_MODEL ** -0.5),
        'exp_w3': nrm(ks[24], (L, N_EXPERTS, D_MODEL, D_EXPERT), D_MODEL ** -0.5),
        'exp_w2': nrm(ks[25], (L, N_EXPERTS, D_EXPERT, D_MODEL), D_EXPERT ** -0.5),
        'final_g': 1.0 + nrm(ks[26], (D_MODEL,), 0.05),
    }

def first_block(x, c, mod_w, mod_b, norm1_g, w_in, conv_k, conv_b, conv_ln_g, conv_ln_b,
              q_norm_g, kv_norm_g, w_uq, w_uk, w_uv, pool_w, pool_scale, w_out, norm2_g,
              router_g_w, router_g_b, router_e_w, router_e_b, exp_w1, exp_w3, exp_w2, final_g):
    cond = jax.nn.silu(c)
    split_at = np.cumsum(IN_SPLITS)[:-1].tolist()
    for l in range(DEPTH):
        mod = cond @ mod_w[l] + mod_b[l]
        sh1, sc1, g1, sh2, sc2, g2 = [m[:, None, :] for m in jnp.split(mod, 6, axis=-1)]
        h = _rmsnorm(x, norm1_g[l]) * (1 + sc1) + sh1
        z = h @ w_in[l]
        a_val, a_gate, cq, ckv, qi, ki, wi, u_pool = jnp.split(z, split_at, axis=-1)
        y_conv = _conv_module(a_val, a_gate, conv_k[l], conv_b[l], conv_ln_g[l], conv_ln_b[l])
        y_att = _dsa_attention(cq, ckv, qi, ki, wi, q_norm_g[l], kv_norm_g[l], w_uq[l], w_uk[l], w_uv[l])
        y_pool = _pool_mixer(u_pool, pool_w[l], pool_scale[l])
        mix = jnp.concatenate([y_conv, y_att, y_pool], axis=-1) @ w_out[l]
        x = x + g1 * mix
        h = _rmsnorm(x, norm2_g[l]) * (1 + sc2) + sh2
        x = x + g2 * _hier_moe(h, router_g_w[l], router_g_b[l], router_e_w[l], router_e_b[l],
                               exp_w1[l], exp_w3[l], exp_w2[l])
    return _rmsnorm(x, final_g)


D_MIX_2 = D_MODEL
GDN_HEADS = 4
GDN_HEAD_DIM = 128
GDN_WIDTH = GDN_HEADS * GDN_HEAD_DIM
SC_WIDTH = D_MIX_2 - GDN_WIDTH
SC_GROUPS = 8
GDN_CONV = 4
SC_CONV = 3
D_FF = -(-8 * D_MODEL // (3 * 256)) * 256
RMS_EPS = 1e-6
L2_EPS = 1e-6

Q_OFF = 0
K_OFF = GDN_WIDTH
V_OFF = 2 * GDN_WIDTH
Z_OFF = 3 * GDN_WIDTH
A_OFF = 4 * GDN_WIDTH
BETA_OFF = A_OFF + GDN_HEADS
SCB_OFF = BETA_OFF + GDN_HEADS
SCC_OFF = SCB_OFF + SC_WIDTH
SCH_OFF = SCC_OFF + SC_WIDTH
D_IN = SCH_OFF + SC_WIDTH


def rms_norm(x, w):
    x32 = x.astype(jnp.float32)
    y = x32 * lax.rsqrt(jnp.mean(x32 * x32, axis=-1, keepdims=True) + RMS_EPS)
    return (y * w.astype(jnp.float32)).astype(x.dtype)

def l2_normalize(x):
    x32 = x.astype(jnp.float32)
    return x32 * lax.rsqrt(jnp.sum(x32 * x32, axis=-1, keepdims=True) + L2_EPS)

def causal_depthwise_conv(x, w):
    k_width = w.shape[0]
    s = x.shape[1]
    xp = jnp.pad(x, ((0, 0), (k_width - 1, 0), (0, 0)))
    out = xp[:, 0:s] * w[0]
    for j in range(1, k_width):
        out = out + xp[:, j:j + s] * w[j]
    return out

def gated_delta_rule_chunked(q, k, v, g, beta):
    bsz, s, h, dk = q.shape
    dv = v.shape[-1]
    n = s // CHUNK
    f32 = jnp.float32

    def to_chunks(t):
        return t.astype(f32).reshape(bsz, n, CHUNK, h, -1).transpose(0, 3, 1, 2, 4)

    q = to_chunks(q) * (dk ** -0.5)
    k = to_chunks(k)
    v = to_chunks(v)
    g = g.astype(f32).reshape(bsz, n, CHUNK, h).transpose(0, 3, 1, 2)
    beta = beta.astype(f32).reshape(bsz, n, CHUNK, h).transpose(0, 3, 1, 2)
    g = jnp.cumsum(g, axis=-1)

    k_beta = k * beta[..., None]
    v_beta = v * beta[..., None]
    tril = jnp.tril(jnp.ones((CHUNK, CHUNK), dtype=bool))
    strict = jnp.tril(jnp.ones((CHUNK, CHUNK), dtype=bool), -1)
    decay = jnp.exp(jnp.where(tril, g[..., :, None] - g[..., None, :], -jnp.inf))

    lmat = jnp.where(strict, jnp.einsum('bhncd,bhnmd->bhncm', k_beta, k) * decay, 0.0)
    eye = jnp.broadcast_to(jnp.eye(CHUNK, dtype=f32), lmat.shape)
    tmat = lax.linalg.triangular_solve(lmat, eye, left_side=True, lower=True, unit_diagonal=True)

    u = jnp.einsum('bhncm,bhnme->bhnce', tmat, v_beta)
    w = jnp.einsum('bhncm,bhnmd->bhncd', tmat, k_beta * jnp.exp(g)[..., None])
    attn = jnp.where(tril, jnp.einsum('bhncd,bhnmd->bhncm', q, k) * decay, 0.0)
    g_last = g[..., -1]
    k_dec = k * jnp.exp(g_last[..., None] - g)[..., None]
    q_dec = q * jnp.exp(g)[..., None]

    def step(state, inp):
        qd, wi, ui, ai, kd, gl = inp
        v_new = ui - jnp.einsum('bhcd,bhde->bhce', wi, state)
        out = jnp.einsum('bhcd,bhde->bhce', qd, state) + jnp.einsum('bhcm,bhme->bhce', ai, v_new)
        state = state * jnp.exp(gl)[..., None, None] + jnp.einsum('bhcd,bhce->bhde', kd, v_new)
        return state, out

    xs = tuple(jnp.moveaxis(t, 2, 0) for t in (q_dec, w, u, attn, k_dec, g_last))
    state0 = jnp.zeros((bsz, h, dk, dv), dtype=f32)
    _, outs = lax.scan(step, state0, xs)
    return outs.transpose(1, 0, 3, 2, 4).reshape(bsz, s, h, dv)

def hybrid_mixer(h, w_in, conv_qkv_w, a_log, dt_bias, gdn_norm_w, conv_short_w, w_out):
    bsz, s, _ = h.shape
    p = h @ w_in
    qkv = jax.nn.silu(causal_depthwise_conv(p[..., Q_OFF:Z_OFF], conv_qkv_w))
    q = qkv[..., 0:GDN_WIDTH].reshape(bsz, s, GDN_HEADS, GDN_HEAD_DIM)
    k = qkv[..., GDN_WIDTH:2 * GDN_WIDTH].reshape(bsz, s, GDN_HEADS, GDN_HEAD_DIM)
    v = qkv[..., 2 * GDN_WIDTH:3 * GDN_WIDTH].reshape(bsz, s, GDN_HEADS, GDN_HEAD_DIM)
    z = p[..., Z_OFF:A_OFF].reshape(bsz, s, GDN_HEADS, GDN_HEAD_DIM)
    a = p[..., A_OFF:BETA_OFF].astype(jnp.float32)
    b = p[..., BETA_OFF:SCB_OFF].astype(jnp.float32)
    g = -jnp.exp(a_log.astype(jnp.float32)) * jax.nn.softplus(a + dt_bias.astype(jnp.float32))
    beta = jax.nn.sigmoid(b)
    o = gated_delta_rule_chunked(l2_normalize(q), l2_normalize(k), v, g, beta)
    o = rms_norm(o, gdn_norm_w) * jax.nn.silu(z.astype(jnp.float32))
    y_gdn = o.reshape(bsz, s, GDN_WIDTH).astype(h.dtype)
    sc_b = p[..., SCB_OFF:SCC_OFF]
    sc_c = p[..., SCC_OFF:SCH_OFF]
    sc_h = p[..., SCH_OFF:D_IN]
    y_sc = sc_b * causal_depthwise_conv(sc_c * sc_h, conv_short_w)
    return jnp.concatenate([y_gdn, y_sc], axis=-1) @ w_out

def swiglu(h, w_gate, w_up, w_down):
    return (jax.nn.silu(h @ w_gate) * (h @ w_up)) @ w_down

def second_inputs(seed: int = 0) -> dict:
    key = jax.random.key(seed)
    ks = jax.random.split(key, 20)
    f32 = jnp.float32
    nrm = lambda k, shape, scale: jax.random.normal(k, shape, f32) * scale
    dt = jnp.exp(jax.random.uniform(ks[8], (DEPTH, GDN_HEADS), f32, math.log(1e-3), math.log(1e-1)))
    return {
        "x": nrm(ks[0], (BATCH, SEQ, D_MODEL), 1.0),
        "c": nrm(ks[1], (BATCH, D_MODEL), 1.0),
        "w_ada": nrm(ks[2], (DEPTH, D_MODEL, 6 * D_MODEL), 0.5 * D_MODEL ** -0.5),
        "b_ada": nrm(ks[3], (DEPTH, 6 * D_MODEL), 0.02),
        "norm1_w": 1.0 + nrm(ks[4], (DEPTH, D_MODEL), 0.02),
        "w_in": nrm(ks[5], (DEPTH, D_MODEL, D_IN), D_MODEL ** -0.5),
        "conv_qkv_w": nrm(ks[6], (DEPTH, GDN_CONV, 3 * GDN_WIDTH), GDN_CONV ** -0.5),
        "A_log": jnp.log(jax.random.uniform(ks[7], (DEPTH, GDN_HEADS), f32, 1.0, 16.0)),
        "dt_bias": dt + jnp.log(-jnp.expm1(-dt)),
        "gdn_norm_w": 1.0 + nrm(ks[9], (DEPTH, GDN_HEAD_DIM), 0.02),
        "conv_short_w": nrm(ks[10], (DEPTH, SC_CONV, SC_WIDTH), SC_CONV ** -0.5),
        "w_out": nrm(ks[11], (DEPTH, D_MIX_2, D_MODEL), D_MIX_2 ** -0.5),
        "norm2_w": 1.0 + nrm(ks[12], (DEPTH, D_MODEL), 0.02),
        "w_gate": nrm(ks[13], (DEPTH, D_MODEL, D_FF), D_MODEL ** -0.5),
        "w_up": nrm(ks[14], (DEPTH, D_MODEL, D_FF), D_MODEL ** -0.5),
        "w_down": nrm(ks[15], (DEPTH, D_FF, D_MODEL), D_FF ** -0.5),
        "norm_f_w": 1.0 + nrm(ks[16], (D_MODEL,), 0.02),
    }

def second_block(x, c, w_ada, b_ada, norm1_w, w_in, conv_qkv_w, A_log, dt_bias, gdn_norm_w,
              conv_short_w, w_out, norm2_w, w_gate, w_up, w_down, norm_f_w):
    c_act = jax.nn.silu(c)
    for l in range(DEPTH):
        mod = (c_act @ w_ada[l] + b_ada[l])[:, None, :]
        shift1, scale1, gate1, shift2, scale2, gate2 = jnp.split(mod, 6, axis=-1)
        h = rms_norm(x, norm1_w[l]) * (1.0 + scale1) + shift1
        x = x + gate1 * hybrid_mixer(h, w_in[l], conv_qkv_w[l], A_log[l], dt_bias[l],
                                     gdn_norm_w[l], conv_short_w[l], w_out[l])
        h = rms_norm(x, norm2_w[l]) * (1.0 + scale2) + shift2
        x = x + gate2 * swiglu(h, w_gate[l], w_up[l], w_down[l])
    return rms_norm(x, norm_f_w)


def setup_inputs(seed=0):
    out = dict(first_inputs(seed))
    for name, value in second_inputs(seed + 1).items():
        if name != "x":
            out[name + "_2"] = value
    return out


def reference(
    x, c, mod_w, mod_b, norm1_g, w_in, conv_k, conv_b, conv_ln_g, conv_ln_b, q_norm_g,
    kv_norm_g, w_uq, w_uk, w_uv, pool_w, pool_scale, w_out, norm2_g, router_g_w, router_g_b,
    router_e_w, router_e_b, exp_w1, exp_w3, exp_w2, final_g, c_2, w_ada_2, b_ada_2, norm1_w_2,
    w_in_2, conv_qkv_w_2, A_log_2, dt_bias_2, gdn_norm_w_2, conv_short_w_2, w_out_2, norm2_w_2,
    w_gate_2, w_up_2, w_down_2, norm_f_w_2,
):
    x = first_block(
        x, c, mod_w, mod_b, norm1_g, w_in, conv_k, conv_b, conv_ln_g, conv_ln_b, q_norm_g,
        kv_norm_g, w_uq, w_uk, w_uv, pool_w, pool_scale, w_out, norm2_g, router_g_w, router_g_b,
        router_e_w, router_e_b, exp_w1, exp_w3, exp_w2, final_g,
    )
    return second_block(
        x, c_2, w_ada_2, b_ada_2, norm1_w_2, w_in_2, conv_qkv_w_2, A_log_2, dt_bias_2,
        gdn_norm_w_2, conv_short_w_2, w_out_2, norm2_w_2, w_gate_2, w_up_2, w_down_2,
        norm_f_w_2,
    )


_drawn_inputs = setup_inputs


def setup_inputs(seed=0):
    import zlib

    import numpy as np

    out = dict(_drawn_inputs(seed))
    spreads = {}
    factors = {'norm1_g': 3.602,
     'conv_b': 8.0,
     'conv_ln_g': 7.347,
     'conv_ln_b': 28.91,
     'q_norm_g': 8.0,
     'kv_norm_g': 5.277,
     'pool_scale': 3.126,
     'router_g_b': 64.0,
     'router_e_b': 38.137,
     'norm1_w_2': 5.738,
     'A_log_2': 2.834,
     'gdn_norm_w_2': 194.545,
     'norm2_w_2': 46.238,
     'norm_f_w_2': 7.767,
     'norm2_g': 4.396,
     'dt_bias_2': 3.642}
    for name, (base, spread) in spreads.items():
        noise = np.random.default_rng([zlib.crc32(name.encode()), seed]).standard_normal(out[name].shape)
        drawn = base * np.exp(spread * noise) if base else spread * noise
        out[name] = __import__('jax').numpy.asarray(drawn.astype(out[name].dtype))
    for name, factor in factors.items():
        out[name] = (out[name] * factor).astype(out[name].dtype)
    return out
```

```python
from contextlib import ExitStack

import concourse.bass as bass
import numpy as np
from concourse import mybir

P = 128
D = 1024
KD = D // P
T = 256
TT = T // P
EPS = 1e-6
CONV_W = 31
HEADS, HD = 8, 64
TOPK = 64
IDX_SCALE = float((8 * 64) ** -0.5)
ATT_SCALE = float(HD ** -0.5)
CHUNK = 64
E, EG, F = 32, 8, 512
KF = F // P
CAP = 64
MASKED = -1.0e30
TAKEN = -3.0e38
GH = 4
NCH = T // CHUNK
FF = 2816
NFF = FF // P
LEVELS = 6

SLOTS, SLOT = 4, 8192
PRE_LOADS = 15
PRE = [(PRE_LOADS - s + SLOTS - 1) // SLOTS for s in range(SLOTS)]

COLS = {}
_n = 0
for _name, _w in (("c", 8), ("c2", 8), ("mod_b", 48), ("ada_b", 48), ("n1", 8), ("n2", 8), ("nf", 8),
                  ("n1b", 8), ("n2b", 8), ("nfb", 8), ("conv_b", 2), ("ln_g", 2), ("ln_b", 2),
                  ("q_g", 2), ("kv_g", 1), ("pool_s", 2), ("conv_k", 2 * CONV_W), ("gconv", 48),
                  ("sconv", 12), ("gnorm", 1), ("rbias", 36), ("a_log", 4), ("dt", 4)):
    COLS[_name] = (_n, _n + _w)
    _n += _w
NCOL = _n
SMALL = {}
_n = 0
for _name, _w in (("uq", 1024), ("uk", 512), ("uv", 512), ("pw", 128), ("rw", 288)):
    SMALL[_name] = (_n, _n + _w)
    _n += _w
NSMALL = _n
CONST = {}
_n = 0
for _name, _w in (("ident", 128), ("tri", 128), ("iota", 64), ("prio", 8)):
    CONST[_name] = (_n, _n + _w)
    _n += _w
NCONST = _n
NACONST = 1024
NGCONST = 128 * (3 + LEVELS)


def program(nc, xT, mod_w, ada_w, winA, winB, wout, ew1, ew3, ew2, w2A, w2B, w2C, w2D, wout2,
            ffu, ffu_last, ffd, ffd_last, cols_d, small_d, const_d, aconst_d, gconst_d, out):
    fp32 = mybir.dt.float32
    i32 = mybir.dt.int32
    ACT = mybir.ActivationFunctionType
    ALU = mybir.AluOpType
    AX = mybir.AxisListType.X

    with ExitStack() as ctx:
        def sb(name, shape, dt=fp32):
            return ctx.enter_context(nc.sbuf_tensor(name, shape, dt))

        sems, count = {}, {}

        def S(name):
            if name not in sems:
                sems[name] = ctx.enter_context(nc.semaphore(name))
                count[name] = 0
            return sems[name]

        for s in range(SLOTS):
            S(f"loaded{s}"), S(f"loaded_b{s}")

        ring = sb("ring", [P, SLOTS, SLOT])
        x = sb("x_res", [P, KD, T])
        cols = sb("cols", [P, NCOL])
        const = sb("const", [P, NCONST])
        ones = sb("ones", [P, P])
        zero = sb("zero", [P, 1])
        one = sb("one", [P, 1])
        eps = sb("eps", [P, 1])
        mod1 = sb("mod1", [P, 48])
        mod2 = sb("mod2", [P, 48])
        gain = sb("gain", [P, 4, KD])
        cact = sb("cact", [P, 2, 8])
        sweeps = sb("sweeps", [P, 1], i32)
        small = sb("smalls", [P, 64])
        rst = sb("rst", [P, 2, T])
        ARENA = 16444
        arena = sb("arena", [P, ARENA])
        psum = [ctx.enter_context(nc.psum_tensor(f"bank{i}", [P, 2, 512], fp32)) for i in range(4)]

        def bank(i):
            return psum[i // 2][:, i % 2, :]

        def view(off, *shape):
            n = 1
            for d in shape:
                n *= d
            assert off + n <= ARENA, (off, shape)
            v = arena[:, off:off + n]
            if len(shape) == 2:
                v = v.rearrange("p (a b) -> p a b", a=shape[0])
            if len(shape) == 3:
                v = v.rearrange("p (a b c) -> p a b c", a=shape[0], b=shape[1])
            return v

        def col(name, i=0, n=1):
            a = COLS[name][0] + i
            return cols[:, a:a + n]

        def cst(name):
            return const[:, CONST[name][0]:CONST[name][1]]

        ident = cst("ident")

        h = view(0, KD, T)
        qabs = view(0, HEADS, T)
        ctxT = view(2048, HEADS, T)
        aval = view(2048, 2, T)
        cgate = view(2560, 2, T)
        smallw = view(4096, NSMALL)
        uq = smallw[:, 0:1024].rearrange("p (k n) -> p k n", k=2)
        uk = smallw[:, 1024:1536].rearrange("p (k n) -> p k n", k=4)
        uv = smallw[:, 1536:2048]
        pw = smallw[:, 2048:2176].rearrange("p (g n) -> p g n", g=2)
        rw = smallw[:, 2176:2464].rearrange("p (k n) -> p k n", k=KD)
        z_att = view(6560, 8, T)
        ki, qi, cq, ckv = z_att[:, 0, :], z_att[:, 1:5, :], z_att[:, 5:7, :], z_att[:, 7, :]
        rel = view(8608, 3, T)
        qT = view(9376, 4, T)
        UPW, PPW = T + CONV_W - 1, T + 16
        psums = view(10400, 2, 2 * PPW)
        upad = view(11488, 2, UPW)
        ppad = view(12060, 2, PPW)
        y = view(12604, KD, T)
        ctok = view(14652, TT, P)
        score = view(14908, TT, T)
        aconst = view(15420, 4, T)
        selb = aconst
        pbuf = [view(6816, 4, T), view(9376, 4, T)]
        pT = view(12604 + 512, 2, 512)
        modrow = view(12604 + 1536, 512)
        sqx = y
        cacc = score
        csq = view(11488, 2, T)
        dpool = cq
        wi = small[:, 0:16].rearrange("p (t h) -> p t h", t=TT)
        top8, mx, ssum, rsum = small[:, 16:24], small[:, 24:28], small[:, 28:36], small[:, 36:40]

        htok = view(0, TT, D)
        s_oh = view(2048, TT, EG * CAP)
        s_gt = view(3072, TT, EG * CAP)
        gT = view(4096, 4, T)
        moe = view(5120, KD, T)
        hsel = view(7168, KD, EG * CAP)
        h2 = view(11264, KD, T)
        sil, hid = view(11264, 512), view(11776, 512)
        hidT = view(12288, KF, P)
        yex = view(12800, D)
        rt = view(13824, 512)
        rank_s = view(14336, TT, 4 * E)
        gate_s = view(14592, TT, 4 * E)
        sq2 = view(0, KD, T)

        g_h = view(0, KD, T)
        g_y = view(2048, KD, T)
        qkv = view(4096, 12, T)
        raw = view(7168, 12, T + 3)
        zg = view(10276, 4, T)
        scb, scc = view(11300, 4, T), view(12324, 4, T)
        scp = view(13348, 4, T + 2)
        gcon = view(14380, 3 + LEVELS, P)
        dl = view(15532, 192)
        SCR = (PRE_LOADS + 3) % SLOTS

        def scr(i):
            v = ring[:, SCR, 1024 * i:1024 * (i + 1)]
            return v.rearrange("p (u c) -> p u c", u=8)
        dec, lt, expg, attn_t, tm, ttm, pm, lm = [scr(i) for i in range(8)]
        sq8 = view(0, 8, T)
        ktok, vb, kbe = view(7168, 8, P), view(8192, 8, P), view(9216, 8, P)
        kdec, wtn = view(11300, 8, P), view(12324, 8, P)
        state, vnew = view(13348, GH, P), view(13860, GH, P)
        o_t, o_sq = view(0, GH, T), view(1024, GH, T)
        hff = view(4096, NFF, T)
        sff = view(9728, 2, 2, T)
        f_h = view(0, KD, T)
        U_c, ones_c, mask_c = gcon[:, 0, :], gcon[:, 1, :], gcon[:, 2, :]

        block = ctx.enter_context(nc.Block())

        STEP_WI, STEP_IDX, STEP_B, STEP_Q, STEP_QA, STEP_CT = 8, 9, 25, 31, 35, 43
        STEPS = 44
        AHEAD = 8
        GROW, KTOK, VTOK, KK, BROW, KQ = 0, 2, 4, 6, 8, 10

        @block.sync
        def _(sp):
            sp.dma_start(x[:], xT).then_inc(S("x_in"), 16)

            used = [("gemv_mm", 1)] * 2 + [("proj_mm", STEP_WI), ("proj_mm", STEP_B + 6)]
            used += [("gemv_mm", 2 + i // 2) for i in range(10)] + [("res_mm", KD)]

            def load(n, src, width=SLOT):
                s = n % SLOTS
                if n >= SLOTS:
                    sp.wait_ge(S(used[n - SLOTS][0]), used[n - SLOTS][1])
                sp.dma_start(ring[:, s, 0:width], src).then_inc(S(f"loaded{s}"), 16)

            load(0, mod_w[0])
            load(1, mod_w[1])
            load(2, winA)
            load(3, winB, winB.shape[1])
            for i in range(2, 6):
                load(2 + i, mod_w[i])
            for i in range(6):
                load(8 + i, ada_w[i])
            load(14, wout)

            def expert_used(g8, n):
                if n % 3 < 2:
                    sp.wait_ge(S("up_mm"), g8 + (AHEAD + 2 * (n // 3) + n % 3 + 1))
                else:
                    sp.wait_ge(S("down_mm"), g8 + (AHEAD + 2 * (n // 3) + 2))

            def expert_load(e8, n):
                s = (PRE_LOADS + n) % SLOTS
                w = (ew1, ew3, ew2)[n % 3]
                pair = w[bass.ds(e8 + 2 * (n // 3), 2), :, :]
                sp.dma_start(ring[:, s, :].rearrange("p (a f) -> p a f", a=2),
                             pair.rearrange("a p f -> p a f")).then_inc(S(f"loaded{s}"), 16)

            for n in range(SLOTS):
                sp.wait_ge(S(used[PRE_LOADS + n - SLOTS][0]), used[PRE_LOADS + n - SLOTS][1])
                expert_load(0, n)
            with sp.Fori(0, 3) as g:
                for n in range(SLOTS, 12 + SLOTS):
                    expert_used(g * 8, n - SLOTS)
                    expert_load(g * 8 + 8 * (n // 12), n % 12)
            for n in range(SLOTS, 12):
                expert_used(3 * 8, n - SLOTS)
                expert_load(3 * 8, n)
            sp.wait_ge(S("sweeps_ready"), 1)
            n_sw = sp.value_load(sweeps[0:1, 0:1], min_val=1, max_val=4)
            with sp.If(n_sw > 1):
                with sp.Fori(4, n_sw * 4) as g:
                    for n in range(12):
                        expert_used(g * 8, n - SLOTS)
                        expert_load((g % 4) * 8, n)
            post = [(w2A, SLOT), (w2B, SLOT), (w2C, SLOT), (w2D, w2D.shape[1]), (wout2, SLOT)]
            post += [(ffu[i], SLOT) for i in range(5)] + [(ffu_last, SLOT // 2)]
            post += [(ffd[i], SLOT) for i in range(2)] + [(ffd_last, 6 * D)]
            used_b = [("proj2_mm", 8), ("proj2_mm", 16), ("proj2_mm", 24), ("delta_done", 1), ("res_mm", 2 * KD)]
            used_b += [("ff_up_mm", 4 * i + 4) for i in range(5)]
            for j, (src, width) in enumerate(post):
                s = (PRE_LOADS + j) % SLOTS
                if j < SLOTS:
                    expert_used(n_sw * 32, j - SLOTS)
                else:
                    sp.wait_ge(S(used_b[j - SLOTS][0]), used_b[j - SLOTS][1])
                sp.dma_start(ring[:, s, 0:width], src).then_inc(S(f"loaded_b{s}"), 16)
            for i in range(KD // 2):
                sp.wait_ge(S("out_ready"), i + 1)
                sp.dma_start(out[:, 2 * i:2 * i + 2, :], f_h[:, 2 * i:2 * i + 2, :]).then_inc(S("stored"), 16)
            sp.wait_ge(S("stored"), 16 * (KD // 2))

        @block.gpsimd
        def _(pool):
            def p(ins, name="pool_step"):
                ins.then_inc(S(name), 1)
                count[name] += 1
                pool.wait_ge(S(name), count[name])

            p(nc.gpsimd.memset(ppad[:, :, 0:16], 0.0), "pool_pad")
            pool.wait_ge(S("proj_ev"), STEP_B + 6)
            s_a = psums[:, 0, :].rearrange("p (c t) -> p c t", c=2)
            s_b = psums[:, 1, :].rearrange("p (c t) -> p c t", c=2)
            p(nc.gpsimd.memset(psums, 0.0))
            p(nc.gpsimd.tensor_tensor(s_a[:, :, 1:PPW], ppad[:, :, 1:PPW], ppad[:, :, 0:PPW - 1], ALU.add))
            p(nc.gpsimd.tensor_tensor(s_b[:, :, 3:PPW], s_a[:, :, 3:PPW], s_a[:, :, 1:PPW - 2], ALU.add))
            p(nc.gpsimd.tensor_tensor(s_a[:, 1, 7:PPW], s_b[:, 1, 7:PPW], s_b[:, 1, 3:PPW - 4], ALU.add))
            p(nc.gpsimd.tensor_tensor(s_b[:, 1, 15:PPW], s_a[:, 1, 15:PPW], s_a[:, 1, 7:PPW - 8], ALU.add))
            pool.wait_ge(S("proj_mm"), STEP_QA)
            for c in range(2):
                for half, sums in ((0, s_a), (64, s_b)):
                    q = slice(half, half + 64)
                    p(nc.gpsimd.tensor_tensor(dpool[q, c, :], sums[q, c, 16:PPW], aconst[q, 2 + c, :], ALU.mult))
                    p(nc.gpsimd.tensor_tensor(dpool[q, c, :], dpool[q, c, :], ppad[q, c, 16:PPW], ALU.subtract),
                      "dpool_ready" if (c, half) == (1, 64) else "pool_step")

            for lv in range(1, LEVELS):
                for t in range(TT):
                    pool.wait_ge(S("lt_ready"), 1)
                    if lv > 1:
                        pool.wait_ge(S("merge_p_mm"), TT * (lv - 2) + t + 1)
                    nc.gpsimd.tensor_tensor(lm[:, 4 * t:4 * t + 4, :], lt[:, 4 * t:4 * t + 4, :],
                                            gcon[:, 3 + lv, :].unsqueeze(1).to_broadcast([P, 4, P]),
                                            ALU.mult).then_inc(S("lm_ready"), 1)

        @block.scalar
        def _(act):
            def a(ins, name):
                ins.then_inc(S(name), 1)
                count[name] += 1

            act.dma_start(cols[:], cols_d).then_inc(S("small_in"), 16)
            act.dma_start(const[:], const_d).then_inc(S("small_in"), 16)
            act.dma_start(aconst[:], aconst_d).then_inc(S("small_in"), 16)
            act.dma_start(smallw[:], small_d).then_inc(S("small_in"), 16)
            act.wait_ge(S("small_in"), 64)
            act.wait_ge(S("init"), 1)
            a(nc.scalar.activation(cact[:, 0, :], col("c", 0, 8), ACT.Silu, bias=zero[:]), "cact_ready")
            a(nc.scalar.activation(cact[:, 1, :], col("c2", 0, 8), ACT.Silu, bias=zero[:]), "cact_ready")

            def root(src, dst, n, mm, at, out_name):
                act.wait_ge(S(mm), at)
                a(nc.scalar.activation(dst, src, ACT.Sqrt, scale=1.0 / n, bias=eps[:]), out_name)

            def gemv_row(r):
                act.wait_ge(S("gemv_mm"), r + 1)
                if r > 0:
                    act.wait_ge(S("modT_mm"), r)
                a(nc.scalar.activation(modrow, bank(1), ACT.Copy), "modrow_ready")

            root(bank(0)[:, 0:T], rst[:, 0, :], D, "ms_mm", 1, "root_ready")
            gemv_row(0)

            def step_out(i):
                act.wait_ge(S("proj_mm"), i + 1)
                src = bank(3 + i % 2)
                if i < STEP_WI:
                    ins = nc.scalar.activation(z_att[:, i, :], src[:, 0:T], ACT.Copy)
                elif i == STEP_WI:
                    ins = nc.scalar.activation(small[:, 0:16], src[:, 0:16], ACT.Copy)
                elif i < STEP_B:
                    n = i - STEP_IDX
                    w = P if n < 8 else T
                    if n >= 2:
                        act.wait_ge(S("idx_acc"), n - 1)
                    ins = nc.scalar.activation(rel[:, n % 2, 0:w], src[:, 0:w], ACT.Relu)
                elif i < STEP_B + 2:
                    ins = nc.scalar.activation(aval[:, i - STEP_B, :], src[:, 0:T], ACT.Copy)
                elif i < STEP_B + 4:
                    ins = nc.scalar.activation(cgate[:, i - STEP_B - 2, :], src[:, 0:T], ACT.Exp, scale=-1.0,
                                               bias=zero[:])
                elif i < STEP_Q:
                    if i == STEP_B + 4:
                        act.wait_ge(S("pool_pad"), 1)
                    ins = nc.scalar.activation(ppad[:, i - STEP_B - 4, 16:PPW], src[:, 0:T], ACT.Copy)
                elif i < STEP_QA:
                    ins = nc.scalar.activation(qT[:, i - STEP_Q, :], src[:, 0:T], ACT.Copy)
                elif i < STEP_CT:
                    ins = nc.scalar.activation(qabs[:, i - STEP_QA, :], src[:, 0:T], ACT.Copy)
                else:
                    ins = nc.scalar.activation(ctok[:, :, :], src[:, 0:T].rearrange("p (t c) -> p t c", t=TT), ACT.Copy)
                a(ins, "proj_ev")

            for i in range(STEP_WI + 1):
                step_out(i)
            act.wait_ge(S("lat_mm"), 1)
            a(nc.scalar.activation(rst[:, 0, :], bank(0)[:, 0:T], ACT.Sqrt, scale=1.0 / 256, bias=eps[:]), "lat_root")
            a(nc.scalar.activation(rst[:, 1, :], bank(0)[:, T:2 * T], ACT.Sqrt, scale=1.0 / 128, bias=eps[:]), "lat_root")
            for i in range(STEP_WI + 1, STEPS):
                step_out(i)
            gemv_row(1)
            gemv_row(2)

            def exps(gi):
                w = P if gi < 2 else T
                act.wait_ge(S("max_ready"), gi + 1)
                for j in range(4):
                    a(nc.scalar.activation(pbuf[gi % 2][:, j, 0:w], pbuf[gi % 2][:, j, 0:w], ACT.Exp,
                                           bias=mx[:, j:j + 1], accum_out=ssum[:, 4 * (gi % 2) + j:4 * (gi % 2) + j + 1]), "exp_done")

            def pt_out(gi):
                for st in range(1 if gi < 2 else 2):
                    n = (0, 1, 2, 4)[gi] + st
                    act.wait_ge(S("pT_mm"), n + 1)
                    if gi > 0:
                        act.wait_ge(S("ctx_mm"), gi)
                    a(nc.scalar.activation(pT[:, st, :], bank(5), ACT.Copy), "pT_ready")

            def ctx_out(gi):
                act.wait_ge(S("ctx_mm"), gi + 1)
                if gi == 0:
                    act.wait_ge(S("u_ready"), 1)
                qb, hh = gi // 2, gi % 2
                a(nc.scalar.activation(ctxT[:, 4 * hh:4 * hh + 4, qb * P:qb * P + P],
                                       bank(4).rearrange("p (h q) -> p h q", h=4), ACT.Copy), "ctx_ready")

            for gi in range(4):
                exps(gi)
                if gi > 0:
                    gemv_row(2 + gi)
                pt_out(gi)
                ctx_out(gi)
            for c in range(2):
                act.wait_ge(S("o_mm"), c + 1)
                a(nc.scalar.activation(y[:, 2 + 2 * c:4 + 2 * c, :],
                                       bank(3 + c).rearrange("p (a t) -> p a t", a=2), ACT.Copy), "y1_ready")
            act.wait_ge(S("pool_mm"), 1)
            for c in range(2):
                a(nc.scalar.activation(y[:, 6 + c, :], bank(5)[:, c * T:c * T + T], ACT.Copy, scale=col("pool_s", c)),
                  "y1_ready")
            root(bank(0)[:, T:2 * T], rst[:, 1, :], 256, "cstat_mm", 2, "cvar_root")
            act.wait_ge(S("cnorm_ready"), 1)
            for c in range(2):
                a(nc.scalar.activation(y[:, c, :], cacc[:, c, :], ACT.Silu, scale=col("ln_g", c), bias=col("ln_b", c)),
                  "y1_ready")

            root(bank(0)[:, 0:T], rst[:, 0, :], D, "ms_mm", 2, "root_ready")
            for i in range(4):
                act.wait_ge(S("htok_mm"), i + 1)
                t, half = i // 2, i % 2
                a(nc.scalar.activation(htok[:, t, half * 512:half * 512 + 512], bank(2 + i % 2), ACT.Copy), "htok_ready")
            act.wait_ge(S("router_in"), 1)
            a(nc.scalar.activation(rt[:, 72:80], rt[:, 72:80], ACT.Exp, bias=zero[:]), "router_exp")
            act.wait_ge(S("router_in"), 2)
            a(nc.scalar.activation(rt[:, 160:162], rt[:, 160:162], ACT.Exp, bias=zero[:]), "router_exp")

            def act_group(g):
                for i in range(10):
                    act.wait_ge(S("gath_mm"), g * 10 + (i + 2))
                    src = bank(7 - i % 2)
                    if i < 8:
                        dst = hsel[:, i, :]
                    else:
                        dst = gT[:, 2 * (i - 8):2 * (i - 8) + 2, :]
                        src = src.rearrange("p (j t) -> p j t", j=2)
                    nc.scalar.activation(dst, src, ACT.Copy).then_inc(S("gath_ev"), 1)
                for j in range(4):
                    act.wait_ge(S("up_mm"), g * 8 + (AHEAD + 2 * j + 1))
                    nc.scalar.activation(sil, bank(0), ACT.Silu, bias=zero[:]).then_inc(S("sil_ready"), 1)
                    act.wait_ge(S("hidT_mm"), g * 4 + (j + 1))
                    nc.scalar.activation(hidT[:], bank(6).rearrange("p (k s) -> p k s", k=KF),
                                         ACT.Copy).then_inc(S("hidT_ready"), 1)
                    for half in range(2):
                        act.wait_ge(S("down_mm"), g * 8 + (AHEAD + 2 * j + half + 1))
                        nc.scalar.activation(yex[:, half * 512:half * 512 + 512], bank(2 + half),
                                             ACT.Copy).then_inc(S("y_ready"), 1)

            act.wait_ge(S("sweeps_ready"), 1)
            n_sw = act.value_load(sweeps[0:1, 0:1], min_val=1, max_val=4)
            with act.Fori(0, 4) as g:
                act_group(g)
            with act.If(n_sw > 1):
                with act.Fori(4, n_sw * 4) as g:
                    act_group(g)

            act.wait_ge(S("moe_added"), 1)
            act.dma_start(gcon[:], gconst_d).then_inc(S("gcon_in"), 16)
            root(bank(0)[:, 0:T], rst[:, 0, :], D, "ms_mm", 3, "root_ready")
            root(bank(0)[:, 0:T], rst[:, 0, :], D, "ms_mm", 4, "root_ready")

            def proj_out(i):
                act.wait_ge(S("proj2_mm"), i + 1)
                src = bank(i % 2)[:, 0:T]
                if i < 12:
                    if i == 0:
                        act.wait_ge(S("raw_pad"), 1)
                    ins = nc.scalar.activation(raw[:, i, 3:3 + T], src, ACT.Copy)
                elif i < 16:
                    ins = nc.scalar.activation(zg[:, i - 12, :], src, ACT.Silu, bias=zero[:])
                elif i < 20:
                    ins = nc.scalar.activation(scb[:, i - 16, :], src, ACT.Copy)
                elif i < 24:
                    ins = nc.scalar.activation(scc[:, i - 20, :], src, ACT.Copy)
                else:
                    ins = nc.scalar.activation(scp[:, i - 24, 2:2 + T], src, ACT.Copy)
                a(ins, "proj2_ev")
                if i >= 8 and (i - 8) % 4 == 3 and (i - 8) // 4 < 3:
                    for k in range(4):
                        m = (i - 11) + k
                        act.wait_ge(S("gconv_done"), m + 1)
                        a(nc.scalar.activation(qkv[:, m, :], qkv[:, m, :], ACT.Silu, bias=zero[:]), "qkv_ready")

            for i in range(28):
                proj_out(i)
            act.wait_ge(S("ab_mm"), 1)
            a(nc.scalar.activation(dl[:, 0:16], bank(2)[:, 0:16], ACT.Copy), "ab_ready")
            for i in range(4):
                act.wait_ge(S("l2_mm"), i + 1)
                if i >= 1:
                    act.wait_ge(S("l2_done"), i)
                a(nc.scalar.activation(rst[:], bank(4 + i % 2).rearrange("p (a t) -> p a t", a=2), ACT.Sqrt,
                                       bias=eps[:]), "l2_root")
            act.wait_ge(S("sp_in"), 1)
            a(nc.scalar.activation(dl[:, 24:32], dl[:, 24:32], ACT.Exp, bias=zero[:]), "sp_exp")
            a(nc.scalar.activation(dl[:, 40:48], dl[:, 40:48], ACT.Exp, bias=zero[:], scale=-1.0), "sp_exp")
            a(nc.scalar.activation(dl[:, 48:52], col("a_log", 0, 4), ACT.Exp, bias=zero[:]), "sp_exp")
            act.wait_ge(S("sp_exp"), 3)
            a(nc.scalar.activation(dl[:, 24:32], dl[:, 24:32], ACT.Ln, bias=one[:]), "sp_exp")
            act.wait_ge(S("gcol_ready"), 1)
            a(nc.scalar.activation(dl[:, 80:96], dl[:, 64:80], ACT.Exp, bias=zero[:]), "gexp_ready")
            for t in range(TT):
                act.wait_ge(S("unit_mm"), GROW + t + 1)
                a(nc.scalar.activation(expg[:, 4 * t:4 * t + 4, :], bank(2 + t).rearrange("p (h c) -> p h c", h=4),
                                       ACT.Exp, bias=zero[:]), "expg_ready")
                act.wait_ge(S("dec_arg"), t + 1)
                a(nc.scalar.activation(dec[:, 4 * t:4 * t + 4, :], dec[:, 4 * t:4 * t + 4, :], ACT.Exp,
                                       bias=zero[:]), "dec_ready")
            for t in range(TT):
                act.wait_ge(S("merge0_mm"), t + 1)
                a(nc.scalar.activation(tm[:, 4 * t:4 * t + 4, :], bank(4 + t).rearrange("p (h c) -> p h c", h=4),
                                       ACT.Copy), "tm0_ready")
            for lv in range(1, LEVELS):
                for t in range(TT):
                    act.wait_ge(S("merge_p_mm"), TT * (lv - 1) + t + 1)
                    a(nc.scalar.activation(pm[:, 4 * t:4 * t + 4, :], bank(t).rearrange("p (h c) -> p h c", h=4),
                                           ACT.Copy), "pm_ready")
            for t in range(TT):
                act.wait_ge(S("wt_mm"), t + 1)
                a(nc.scalar.activation(wtn[:, 4 * t:4 * t + 4, :], bank(4 + t).rearrange("p (h c) -> p h c", h=4),
                                       ACT.Copy), "wt_ready")
            for n in range(NCH):
                q = slice(64 * (n % 2), 64 * (n % 2) + 64)
                act.wait_ge(S("vnew_mm"), n + 1)
                if n >= 2:
                    act.wait_ge(S("out_mm"), n - 1)
                    act.wait_ge(S("state_mm"), n - 1)
                a(nc.scalar.activation(vnew[q], bank(n % 2)[q].rearrange("p (h c) -> p h c", h=4), ACT.Copy), "vnew_ready")
                act.wait_ge(S("out_mm"), n + 1)
                a(nc.scalar.activation(o_t[:, :, 64 * n:64 * n + 64],
                                       bank(2 + n % 2)[:, 0:256].rearrange("p (h c) -> p h c", h=4), ACT.Copy), "o_ready")
            for i in range(2):
                act.wait_ge(S("l2_mm"), 4 + i + 1)
                if i:
                    act.wait_ge(S("l2_done"), 5)
                a(nc.scalar.activation(rst[:], bank(4 + i).rearrange("p (a t) -> p a t", a=2), ACT.Sqrt,
                                       scale=1.0 / 128, bias=eps[:]), "l2_root")
            root(bank(0)[:, 0:T], rst[:, 0, :], D, "ms_mm", 5, "root_ready")
            for f in range(NFF):
                act.wait_ge(S("ff_gate_mm"), f + 1)
                if f >= 4:
                    act.wait_ge(S("hff_ready"), f - 3)
                a(nc.scalar.activation(sff[:, (f // 2) % 2, f % 2, :], bank(2 * (f % 2) + 2)[:, 0:T], ACT.Silu,
                                       bias=zero[:]), "sff_ready")
            root(bank(0)[:, 0:T], rst[:, 0, :], D, "ms_mm", 6, "root_ready")

        @block.vector
        def _(dve):
            def v(ins, name="dve_step"):
                ins.then_inc(S(name), 1)
                count[name] += 1
                dve.wait_ge(S(name), count[name])

            tt, stt, ts = nc.vector.tensor_tensor, nc.vector.scalar_tensor_tensor, nc.vector.tensor_scalar

            nc.vector.memset(zero[:], 0.0).then_inc(S("dve_step"), 1)
            nc.vector.memset(one[:], 1.0).then_inc(S("dve_step"), 1)
            nc.vector.memset(eps[:], EPS).then_inc(S("dve_step"), 1)
            nc.vector.memset(ones[:], 1.0).then_inc(S("dve_step"), 1)
            nc.vector.memset(upad[:, :, 0:CONV_W - 1], 0.0).then_inc(S("dve_step"), 1)
            count["dve_step"] += 5
            dve.wait_ge(S("dve_step"), 5)
            v(nc.vector.memset(score[:], 0.0), "init")

            def square_x(sq):
                for i in range(2):
                    k = slice(4 * i, 4 * i + 4)
                    v(tt(sq[:, k, :], x[:, k, :], x[:, k, :], ALU.mult), "sq_ready")

            def normed(dst, n):
                dve.wait_ge(S("root_ready"), n + 1)
                v(nc.vector.reciprocal(rst[:, 0, :], rst[:, 0, :]))
                for i in range(2):
                    k = slice(4 * i, 4 * i + 4)
                    v(tt(dst[:, k, :], x[:, k, :], rst[:, 0, :].unsqueeze(1).to_broadcast([P, 4, T]), ALU.mult))

            def modulated(dst, n, mod, shift):
                for k in range(KD):
                    v(ts(dst[:, k, :], dst[:, k, :], gain[:, n, k:k + 1], mod[:, shift * 8 + k:shift * 8 + k + 1],
                         ALU.mult, ALU.add), "h_ready")

            def gemv_col(r):
                mod, bias, rr = (mod1, "mod_b", r) if r < 3 else (mod2, "ada_b", r - 3)
                dve.wait_ge(S("modT_mm"), r + 1)
                for j in range(4):
                    o = slice(16 * rr + 4 * j, 16 * rr + 4 * j + 4)
                    v(tt(mod[:, o], bank(2).rearrange("p (s q) -> p s q", s=4)[:, :, 32 * j],
                         col(bias, 16 * rr + 4 * j, 4), ALU.add), "mod_ready")
                if rr != 1:
                    n = 2 * (r // 3) + rr // 2
                    sc = mod[:, 8:16] if rr == 0 else mod[:, 32:40]
                    v(stt(gain[:, n, :], sc, 1.0, col(("n1", "n2", "n1b", "n2b")[n], 0, 8), ALU.add, ALU.mult))

            dve.wait_ge(S("x_in"), 16)
            square_x(sqx)
            normed(h, 0)
            dve.wait_ge(S("small_in"), 64)
            gemv_col(0)
            modulated(h, 0, mod1, 0)
            dve.wait_ge(S("proj_ev"), STEP_WI)
            v(tt(rel[:, 0:2, :], cq, cq, ALU.mult))
            v(tt(rel[:, 2, :], ckv, ckv, ALU.mult), "lat_sq")
            dve.wait_ge(S("proj_ev"), STEP_WI + 1)
            dve.wait_ge(S("lat_root"), 2)
            v(nc.vector.reciprocal(rst[:, 0, :], rst[:, 0, :]))
            v(nc.vector.reciprocal(rst[:, 1, :], rst[:, 1, :]))
            for c in range(2):
                v(stt(cq[:, c, :], cq[:, c, :], col("q_g", c), rst[:, 0, :], ALU.mult, ALU.mult), "lat_ready")
            v(stt(ckv, ckv, col("kv_g"), rst[:, 1, :], ALU.mult, ALU.mult), "lat_ready")
            for n in range(16):
                qb, w = n // 8, P if n < 8 else T
                dve.wait_ge(S("proj_ev"), STEP_IDX + n + 1)
                v(stt(score[:, qb, 0:w], rel[:, n % 2, 0:w], wi[:, qb, n % 8:n % 8 + 1], score[:, qb, 0:w],
                      ALU.mult, ALU.add), "idx_acc")
            dve.wait_ge(S("small_in"), 64)
            for qb in range(2):
                w = P if qb == 0 else T
                sc = score[:, qb, 0:w]
                v(stt(sc, sc, IDX_SCALE, aconst[:, qb, 0:w], ALU.mult, ALU.add))
                for _ in range(TOPK // 8):
                    v(nc.vector.max(top8, sc))
                    v(nc.vector.match_replace(sc, top8, sc, TAKEN))
                v(ts(selb[:, qb, 0:w], sc, -2.0e38, MASKED, ALU.is_gt, ALU.mult))
            dve.wait_ge(S("proj_ev"), STEP_B + 4)
            v(nc.vector.tensor_scalar_add(cgate, cgate, 1.0))
            v(nc.vector.reciprocal(cgate, cgate))
            v(tt(upad[:, :, CONV_W - 1:UPW], aval, cgate, ALU.mult), "u_ready")

            def conv(c, lo, hi):
                for j in range(lo, hi):
                    src, k = upad[:, c, j:j + T], col("conv_k", c * CONV_W + j)
                    if j == 0:
                        v(ts(cacc[:, c, :], src, k, col("conv_b", c), ALU.mult, ALU.add))
                    else:
                        v(stt(cacc[:, c, :], src, k, cacc[:, c, :], ALU.mult, ALU.add),
                          "conv_done" if j == CONV_W - 1 else "dve_step")

            gemv_col(1)
            gemv_col(2)
            for gi in range(4):
                qb, w, buf = gi // 2, P if gi < 2 else T, pbuf[gi % 2]
                dve.wait_ge(S("lg_mm"), gi + 1)
                if gi >= 2:
                    dve.wait_ge(S("pT_mm"), (1, 2)[gi - 2])
                v(stt(buf[:, :, 0:w], psum[3][:].rearrange("p a (b s) -> p (a b) s", b=2)[:, :, 0:w], ATT_SCALE,
                      selb[:, qb, 0:w].unsqueeze(1).to_broadcast([P, 4, w]), ALU.mult, ALU.add), "lg_used")
                if gi > 0:
                    dve.wait_ge(S("exp_done"), 4 * gi)
                v(nc.vector.tensor_reduce(mx, buf[:, :, 0:w], AX, ALU.max))
                v(nc.vector.tensor_scalar_mul(mx, mx, -1.0), "max_ready")
                conv(gi // 2, 16 * (gi % 2), (16, CONV_W)[gi % 2])
                dve.wait_ge(S("exp_done"), 4 * (gi + 1))
                v(nc.vector.reciprocal(rsum, ssum[:, 4 * (gi % 2):4 * (gi % 2) + 4]))
                v(tt(buf[:, :, 0:w], buf[:, :, 0:w], rsum.unsqueeze(2).to_broadcast([P, 4, w]), ALU.mult), "p_ready")
                if gi > 0:
                    gemv_col(2 + gi)
            dve.wait_ge(S("cstat_mm"), 1)
            for c in range(2):
                v(stt(cacc[:, c, :], bank(0)[:, 0:T], -1.0 / 256, cacc[:, c, :], ALU.mult, ALU.add))
            v(tt(csq, cacc, cacc, ALU.mult), "csq_ready")
            dve.wait_ge(S("cvar_root"), 1)
            v(nc.vector.reciprocal(rst[:, 1, :], rst[:, 1, :]))
            v(tt(cacc, cacc, rst[:, 1, :].unsqueeze(1).to_broadcast([P, 2, T]), ALU.mult), "cnorm_ready")

            def residual(n, gate):
                for m in range(KD):
                    dve.wait_ge(S("res_mm"), KD * n + m + 1)
                    v(stt(x[:, m, :], bank(6 + m % 2)[:, 0:T], gate[:, m:m + 1], x[:, m, :], ALU.mult, ALU.add),
                      "res_used")

            residual(0, mod1[:, 16:24])

            square_x(sq2)
            normed(h2, 1)
            modulated(h2, 1, mod1, 3)
            lg = rt[:, 0:72].rearrange("p (t e) -> p t e", t=TT)
            glog, elog = lg[:, :, 0:4], lg[:, :, 4:36].rearrange("p t (g e) -> p t g e", g=4)
            gex = rt[:, 72:80].rearrange("p (t g) -> p t g", t=TT)
            goh = rt[:, 80:88].rearrange("p (t g) -> p t g", t=TT)
            gmax, gp, pri = rt[:, 88:90], rt[:, 90:92], rt[:, 92:94]
            esel = rt[:, 96:112].rearrange("p (t e) -> p t e", t=TT)
            oh = [rt[:, 112 + 16 * i:128 + 16 * i].rearrange("p (t e) -> p t e", t=TT) for i in range(2)]
            emax = [rt[:, 144:146], rt[:, 146:148]]
            gap, den, wg = rt[:, 160:162], rt[:, 162:164], [rt[:, 164:166], rt[:, 166:168]]
            tmp8 = rt[:, 176:192].rearrange("p (t e) -> p t e", t=TT)
            asg = rt[:, 192:256].rearrange("p (t g e) -> p t g e", t=TT, g=4)
            gat = rt[:, 256:320].rearrange("p (t g e) -> p t g e", t=TT, g=4)
            tmp32 = rt[:, 320:384].rearrange("p (t g e) -> p t g e", t=TT, g=4)
            cnt = rt[:, 384:416]
            acc1 = rt[:, 416:424]

            def wide(a, n):
                return a.unsqueeze(2).to_broadcast([P, TT, n])

            def first_max(src, top, out_oh, n):
                v(nc.vector.tensor_reduce(top, src, AX, ALU.max))
                v(tt(out_oh, src, wide(top, n), ALU.is_equal))
                v(tt(out_oh, out_oh, cst("prio")[:, 0:n].unsqueeze(1).to_broadcast([P, TT, n]), ALU.mult))
                v(nc.vector.tensor_reduce(pri, out_oh, AX, ALU.max))
                v(tt(out_oh, out_oh, wide(pri, n), ALU.is_equal))

            dve.wait_ge(S("router_mm"), 1)
            v(tt(lg, bank(1)[:, 0:72].rearrange("p (t e) -> p t e", t=TT),
                 col("rbias", 0, 36).unsqueeze(1).to_broadcast([P, TT, 36]), ALU.add))
            first_max(glog, gmax, goh, 4)
            v(tt(gex, glog, wide(gmax, 4), ALU.subtract), "router_in")
            v(tt(tmp32, elog, goh.unsqueeze(3).to_broadcast([P, TT, 4, 8]), ALU.mult))
            v(tt(esel, tmp32[:, :, 0, :], tmp32[:, :, 1, :], ALU.add))
            v(tt(esel, esel, tmp32[:, :, 2, :], ALU.add))
            v(tt(esel, esel, tmp32[:, :, 3, :], ALU.add))
            first_max(esel, emax[0], oh[0], 8)
            v(stt(tmp8, oh[0], MASKED, esel, ALU.mult, ALU.add))
            first_max(tmp8, emax[1], oh[1], 8)
            v(tt(gap, emax[1], emax[0], ALU.subtract), "router_in")
            v(tt(tmp8, oh[0], oh[1], ALU.add))
            v(tt(asg, goh.unsqueeze(3).to_broadcast([P, TT, 4, 8]), tmp8.unsqueeze(2).to_broadcast([P, TT, 4, 8]),
                 ALU.mult), "asg_ready")
            dve.wait_ge(S("router_exp"), 1)
            v(nc.vector.tensor_reduce(gp, gex, AX, ALU.add))
            v(nc.vector.reciprocal(gp, gp))
            dve.wait_ge(S("router_exp"), 2)
            v(nc.vector.tensor_scalar_add(den, gap, 1.0))
            v(nc.vector.reciprocal(den, den))
            v(tt(wg[0], den, gp, ALU.mult))
            v(tt(wg[1], wg[0], gap, ALU.mult))
            v(tt(oh[0], oh[0], wide(wg[0], 8), ALU.mult))
            v(tt(oh[1], oh[1], wide(wg[1], 8), ALU.mult))
            v(tt(oh[0], oh[0], oh[1], ALU.add))
            v(tt(gat, goh.unsqueeze(3).to_broadcast([P, TT, 4, 8]), oh[0].unsqueeze(2).to_broadcast([P, TT, 4, 8]),
                 ALU.mult))
            dve.wait_ge(S("rank_mm"), 1)
            a2, g2 = rt[:, 192:256].rearrange("p (t e) -> p t e", t=TT), rt[:, 256:320].rearrange("p (t e) -> p t e", t=TT)
            rk = rt[:, 320:384].rearrange("p (t e) -> p t e", t=TT)
            v(stt(rk, bank(5)[:, 0:64].rearrange("p (t e) -> p t e", t=TT), 1.0, a2, ALU.add, ALU.mult))
            for s in range(4):
                v(nc.vector.tensor_scalar_add(rank_s[:, :, E * s:E * s + E], rk, -1.0 - CAP * s))
                v(nc.vector.tensor_copy(gate_s[:, :, E * s:E * s + E], g2))
            v(nc.vector.reduce_max(acc1[:, 0:1], bank(5)[:, 64:96], AX))
            for s in range(1, 4):
                v(ts(acc1[:, s:s + 1], acc1[:, 0:1], CAP * s + 0.5, None, ALU.is_gt))
            v(stt(acc1[:, 1:2], acc1[:, 1:2], 1.0, acc1[:, 2:3], ALU.add, ALU.add))
            v(tt(acc1[:, 1:2], acc1[:, 1:2], acc1[:, 3:4], ALU.add))
            v(nc.vector.tensor_copy(sweeps[:], acc1[:, 1:2]), "sweeps_ready")
            v(nc.vector.memset(moe, 0.0))
            dve.sem_inc(S("moe_add"), 2)

            def dve_group(g):
                dve.wait_ge(S("gath_mm"), g * 10 + 1)
                shape = [P, TT, EG, CAP]
                iota = cst("iota").unsqueeze(1).unsqueeze(1).to_broadcast(shape)
                for t in range(TT):
                    nc.vector.tensor_tensor(
                        s_oh[:, t, :].rearrange("p (e s) -> p e s", e=EG),
                        rank_s[:, t, bass.ds(g * 8, 8)].unsqueeze(2).to_broadcast([P, EG, CAP]),
                        cst("iota").unsqueeze(1).to_broadcast([P, EG, CAP]), ALU.is_equal).then_inc(S("onehot"), 1)
                dve.wait_ge(S("onehot"), g * 2 + 2)
                for t in range(TT):
                    nc.vector.tensor_tensor(
                        s_gt[:, t, :].rearrange("p (e s) -> p e s", e=EG),
                        s_oh[:, t, :].rearrange("p (e s) -> p e s", e=EG),
                        gate_s[:, t, bass.ds(g * 8, 8)].unsqueeze(2).to_broadcast([P, EG, CAP]),
                        ALU.mult).then_inc(S("gated"), 1)
                for j in range(4):
                    dve.wait_ge(S("up_mm"), g * 8 + (AHEAD + 2 * j + 2))
                    dve.wait_ge(S("sil_ready"), g * 4 + (j + 1))
                    nc.vector.tensor_tensor(hid, sil, bank(1), ALU.mult).then_inc(S("hid_ready"), 1)
                    for c in range(4):
                        dve.wait_ge(S("comb_mm"), g * 16 + (4 * j + c + 1))
                        dve.wait_ge(S("moe_add"), g * 16 + (4 * j + c + 2))
                        nc.vector.tensor_tensor(moe[:, 2 * c:2 * c + 2, :],
                                                bank(4 + c % 2).rearrange("p (a t) -> p a t", a=2),
                                                moe[:, 2 * c:2 * c + 2, :], ALU.add).then_inc(S("moe_add"), 1)

            n_sw = dve.value_load(sweeps[0:1, 0:1], min_val=1, max_val=4)
            with dve.Fori(0, 4) as g:
                dve_group(g)
            with dve.If(n_sw > 1):
                with dve.Fori(4, n_sw * 4) as g:
                    dve_group(g)
            dve.wait_ge(S("moe_add"), n_sw * 64 + 2)
            for k in range(KD):
                v(stt(x[:, k, :], moe[:, k, :], mod1[:, 40 + k:41 + k], x[:, k, :], ALU.mult, ALU.add),
                  "moe_added" if k == KD - 1 else "dve_step")

            square_x(view(2048, KD, T))
            normed(x, 2)
            for k in range(KD):
                v(nc.vector.tensor_scalar_mul(x[:, k, :], x[:, k, :], col("nf", k)))
            square_x(view(2048, KD, T))
            v(nc.vector.memset(raw[:, :, 0:3], 0.0), "raw_pad")
            v(nc.vector.memset(scp[:, :, 0:2], 0.0))
            normed(g_h, 3)
            modulated(g_h, 2, mod2, 0)
            for m in range(12):
                dve.wait_ge(S("proj2_ev"), m + 1)
                for j in range(4):
                    src, k = raw[:, m, j:j + T], col("gconv", 4 * m + j)
                    if j == 0:
                        v(nc.vector.tensor_scalar_mul(qkv[:, m, :], src, k))
                    else:
                        v(stt(qkv[:, m, :], src, k, qkv[:, m, :], ALU.mult, ALU.add),
                          "gconv_done" if j == 3 else "dve_step")
            for i in range(4):
                dve.wait_ge(S("proj2_ev"), 24 + i + 1)
                v(tt(scp[:, i, 2:2 + T], scp[:, i, 2:2 + T], scc[:, i, :], ALU.mult))
                o = g_y[:, 4 + i, :]
                v(nc.vector.tensor_scalar_mul(o, scp[:, i, 0:T], col("sconv", 3 * i)))
                v(stt(o, scp[:, i, 1:1 + T], col("sconv", 3 * i + 1), o, ALU.mult, ALU.add))
                v(stt(o, scp[:, i, 2:2 + T], col("sconv", 3 * i + 2), o, ALU.mult, ALU.add))
                v(tt(o, o, scb[:, i, :], ALU.mult), "y2_ready")
            dve.wait_ge(S("ab_mm"), 1)
            dve.wait_ge(S("qkv_ready"), 8)
            for i in range(4):
                k = slice(2 * i, 2 * i + 2)
                v(tt(sq8[:, k, :], qkv[:, k, :], qkv[:, k, :], ALU.mult), "sq8_ready")
            for i in range(4):
                k = slice(2 * i, 2 * i + 2)
                dve.wait_ge(S("l2_root"), i + 1)
                v(nc.vector.reciprocal(rst[:], rst[:]))
                if i < 2:
                    v(stt(qkv[:, k, :], qkv[:, k, :], float(128 ** -0.5), rst[:], ALU.mult, ALU.mult), "l2_done")
                else:
                    v(tt(qkv[:, k, :], qkv[:, k, :], rst[:], ALU.mult), "l2_done")
            ab = dl[:, 0:16].rearrange("p (t c) -> p t c", t=TT)
            ap, sp_, am = [dl[:, o:o + 8].rearrange("p (t h) -> p t h", t=TT) for o in (16, 24, 32)]
            be = dl[:, 40:48].rearrange("p (t h) -> p t h", t=TT)
            na = dl[:, 48:52]
            gg = dl[:, 56:64].rearrange("p (t h) -> p t h", t=TT)
            dve.wait_ge(S("ab_ready"), 1)
            v(tt(ap, ab[:, :, 0:4], col("dt", 0, 4).unsqueeze(1).to_broadcast([P, TT, 4]), ALU.add))
            v(nc.vector.tensor_scalar_mul(sp_, ap, -1.0))
            v(tt(sp_, sp_, ap, ALU.min))
            v(nc.vector.tensor_scalar_max(am, ap, 0.0))
            v(nc.vector.tensor_copy(be, ab[:, :, 4:8]), "sp_in")
            dve.wait_ge(S("sp_exp"), 4)
            v(tt(sp_, sp_, am, ALU.add))
            v(nc.vector.tensor_scalar_mul(na, na, -1.0))
            v(tt(gg, sp_, na.unsqueeze(1).to_broadcast([P, TT, 4]), ALU.mult), "g_ready")
            v(nc.vector.tensor_scalar_add(be, be, 1.0))
            v(nc.vector.reciprocal(be, be), "beta_ready")
            dve.wait_ge(S("gcum_mm"), 1)
            G, GL = dl[:, 64:72], dl[:, 72:80]
            v(nc.vector.tensor_copy(G, bank(6)[:, 0:8]))
            v(tt(GL, bank(6)[:, 8:16], G, ALU.subtract), "gcol_ready")
            eG, eGL = dl[:, 80:88], dl[:, 88:96]
            nbe = dl[:, 96:104]
            for t in range(TT):
                dve.wait_ge(S("unit_mm"), GROW + t + 1)
                dve.wait_ge(S("expg_ready"), t + 1)
                for hd in range(GH):
                    u = 4 * t + hd
                    v(stt(dec[:, u, :], bank(2 + t)[:, hd * P:hd * P + P], G[:, u:u + 1], mask_c, ALU.subtract, ALU.add),
                      "dec_arg" if hd == 3 else "dve_step")
            dve.wait_ge(S("gexp_ready"), 1)
            v(tt(nbe, dl[:, 40:48], eG, ALU.mult))
            v(nc.vector.tensor_scalar_mul(nbe, nbe, -1.0))
            for t in range(TT):
                dve.wait_ge(S("unit_mm"), KTOK + t + 1)
                for hd in range(GH):
                    u = 4 * t + hd
                    src = bank(0 + t)[:, hd * P:hd * P + P]
                    v(nc.vector.tensor_scalar_mul(kbe[:, u, :], src, nbe[:, u:u + 1]))
                    v(nc.vector.tensor_scalar_mul(kdec[:, u, :], src, eGL[:, u:u + 1]), "k_used")
            for t in range(TT):
                dve.wait_ge(S("unit_mm"), VTOK + t + 1)
                for hd in range(GH):
                    u = 4 * t + hd
                    v(nc.vector.tensor_scalar_mul(vb[:, u, :], bank(6 + t)[:, hd * P:hd * P + P],
                                                  dl[:, 40 + u:41 + u]), "v_used")
            for t in range(TT):
                us = slice(4 * t, 4 * t + 4)
                dve.wait_ge(S("dec_ready"), t + 1)
                dve.wait_ge(S("unit_mm"), KK + t + 1)
                v(tt(lt[:, us, :], bank(4 + t).rearrange("p (h c) -> p h c", h=4), dec[:, us, :], ALU.mult), "kk_used")
                dve.wait_ge(S("unit_mm"), BROW + t + 1)
                v(tt(lt[:, us, :], lt[:, us, :], bank(2 + t).rearrange("p (h c) -> p h c", h=4), ALU.mult),
                  "lt_ready" if t == 1 else "dve_step")
            for t in range(TT):
                us = slice(4 * t, 4 * t + 4)
                dve.wait_ge(S("unit_mm"), KQ + t + 1)
                v(tt(attn_t[:, us, :], bank(0 + t).rearrange("p (h c) -> p h c", h=4), dec[:, us, :], ALU.mult),
                  "attn_ready")
            for t in range(TT):
                us = slice(4 * t, 4 * t + 4)
                v(tt(ttm[:, us, :], lt[:, us, :], gcon[:, 3, :].unsqueeze(1).to_broadcast([P, 4, P]), ALU.mult))
                v(tt(ttm[:, us, :], ident.unsqueeze(1).to_broadcast([P, 4, P]), ttm[:, us, :], ALU.subtract), "ttm_ready")
            for lv in range(1, LEVELS):
                for t in range(TT):
                    us = slice(4 * t, 4 * t + 4)
                    if lv == 1:
                        dve.wait_ge(S("tm0_ready"), t + 1)
                    if lv < LEVELS - 1:
                        dve.wait_ge(S("merge_t_mm"), TT * (lv - 1) + t + 1)
                        v(tt(tm[:, us, :], tm[:, us, :], bank(4 + t).rearrange("p (h c) -> p h c", h=4), ALU.subtract),
                          "tm_ready")
                    dve.wait_ge(S("merge_tt_mm"), TT * (lv - 1) + t + 1)
                    v(tt(ttm[:, us, :], ttm[:, us, :], bank(2 + t).rearrange("p (h c) -> p h c", h=4), ALU.subtract),
                      "ttm_ready")
            for t in range(TT):
                for hd in range(GH):
                    v(tt(qkv[:, hd, t * P:t * P + P], qkv[:, hd, t * P:t * P + P], expg[:, 4 * t + hd, :], ALU.mult),
                      "qdec_ready")
            for n in range(NCH - 1):
                dve.wait_ge(S("state_mm"), n + 1)
                dve.wait_ge(S("out_mm"), n + 1)
                for hd in range(GH):
                    src = bank(6 + n % 2)[:, hd * P:hd * P + P]
                    if n == 0:
                        v(nc.vector.tensor_copy(state[:, hd, :], src), "state_ready")
                    else:
                        u = 4 * (n // 2) + hd
                        last = 64 * (n % 2) + 63
                        v(stt(state[:, hd, :], state[:, hd, :], expg[:, u, last:last + 1], src, ALU.mult, ALU.add),
                          "state_ready")
            dve.wait_ge(S("o_ready"), NCH)
            v(tt(o_sq, o_t, o_t, ALU.mult), "osq_ready")
            v(nc.vector.memset(dl[:, 128:129], 0.0), "delta_done")
            for i in range(2):
                k = slice(2 * i, 2 * i + 2)
                dve.wait_ge(S("l2_root"), 4 + i + 1)
                v(nc.vector.reciprocal(rst[:], rst[:]))
                v(stt(o_t[:, k, :], o_t[:, k, :], col("gnorm"), rst[:], ALU.mult, ALU.mult), "l2_done")
                v(tt(g_y[:, k, :], o_t[:, k, :], zg[:, k, :], ALU.mult), "y2_ready")
            residual(1, mod2[:, 16:24])
            square_x(view(2048, KD, T))
            normed(f_h, 4)
            modulated(f_h, 3, mod2, 24 // 8)
            for f in range(NFF):
                dve.wait_ge(S("sff_ready"), f + 1)
                dve.wait_ge(S("ff_up_mm"), f + 1)
                v(tt(hff[:, f, :], sff[:, (f // 2) % 2, f % 2, :], bank(2 * (f % 2) + 3)[:, 0:T], ALU.mult), "hff_ready")
            residual(2, mod2[:, 40:48])
            square_x(view(2048, KD, T))
            normed(f_h, 5)
            for k in range(KD):
                ins = nc.vector.tensor_scalar_mul(f_h[:, k, :], f_h[:, k, :], col("nfb", k))
                v(ins, "out_ready" if k % 2 else "dve_step")

        @block.tensor
        def _(pe):
            mm = nc.tensor.matmul

            def ms(sq, n, wait_name="sq_ready"):
                for k in range(KD):
                    if k % 4 == 0:
                        pe.wait_ge(S("sq_ready"), 2 * n + k // 4 + 1)
                    last = mm(bank(0)[:, 0:T], ones[:], sq[:, k, :], start=k == 0, stop=k == KD - 1)
                last.then_inc(S("ms_mm"), 1)

            def gemv(r):
                n = 2 * r if r < 1 else 2 * r + 2
                c = cact[:, r // 3, :]
                pe.wait_ge(S("cact_ready"), 2)
                if r > 0:
                    pe.wait_ge(S("modrow_ready"), r)
                for k in range(KD):
                    s = (n + k // 4) % SLOTS
                    if k % 4 == 0:
                        pe.wait_ge(S(f"loaded{s}"), 16 * ((n + k // 4) // SLOTS + 1))
                    w = ring[:, s, :].rearrange("p (k n) -> p k n", k=4)[:, k % 4, :]
                    for j in range(4):
                        last = mm(bank(1)[32 * j:32 * j + 32, :], c[:, k:k + 1].to_broadcast([P, 32]),
                                  w[:, 512 * j:512 * j + 512], start=k == 0, stop=k == KD - 1)
                last.then_inc(S("gemv_mm"), 1)

            def gemv_t(r):
                pe.wait_ge(S("modrow_ready"), r + 1)
                if r > 0:
                    pe.wait_ge(S("mod_ready"), 4 * r)
                for s in range(4):
                    last = nc.tensor.transpose(bank(2)[:, s * P:s * P + P], modrow[:, s * P:s * P + P], ident)
                last.then_inc(S("modT_mm"), 1)

            ms(sqx, 0)
            gemv(0)
            pe.wait_ge(S("small_in"), 64)
            gemv_t(0)

            def step_begin(i):
                if i >= 2:
                    pe.wait_ge(S("proj_ev"), i - 1)
                return bank(3 + i % 2)

            def z_chunk(i, s, width, at):
                w = ring[:, s, 0:KD * width].rearrange("p (k n) -> p k n", k=KD)
                b = step_begin(i)
                for k in range(KD):
                    last = mm(b[:, 0:T], w[:, k, at:at + P], h[:, k, :], start=k == 0, stop=k == KD - 1)
                last.then_inc(S("proj_mm"), 1)
                return last

            pe.wait_ge(S("h_ready"), KD)
            pe.wait_ge(S("loaded2"), 16)
            for i in range(8):
                last = z_chunk(i, 2, 1024, i * P)
            WB = 776
            pe.wait_ge(S("loaded3"), 16)
            wb = ring[:, 3, 0:KD * WB].rearrange("p (k n) -> p k n", k=KD)
            b = step_begin(STEP_WI)
            for t in range(TT):
                for k in range(KD):
                    last = mm(b[:, 8 * t:8 * t + 8], h[:, k, t * P:t * P + P], wb[:, k, 768:776],
                              start=k == 0, stop=k == KD - 1)
            last.then_inc(S("proj_mm"), 1)
            pe.wait_ge(S("lat_sq"), 1)
            pe.wait_ge(S("root_ready"), 1)
            for c in range(2):
                mm(bank(0)[:, 0:T], ones[:], rel[:, c, :], start=c == 0, stop=c == 1)
            mm(bank(0)[:, T:2 * T], ones[:], rel[:, 2, :], start=True, stop=True).then_inc(S("lat_mm"), 1)
            for n in range(16):
                qb, hd = n // 8, n % 8
                w, q = P if qb == 0 else T, slice(64 * (hd % 2), 64 * (hd % 2) + 64)
                b = step_begin(STEP_IDX + n)
                mm(b[:, 0:w], qi[q, hd // 2, qb * P:qb * P + P], ki[q, 0:w], start=True,
                   stop=True).then_inc(S("proj_mm"), 1)
            for i in range(6):
                last = z_chunk(STEP_B + i, 3, WB, i * P)
            pe.wait_ge(S("small_in"), 64)
            pe.wait_ge(S("lat_ready"), 3)
            for c in range(4):
                b = step_begin(STEP_Q + c)
                for k in range(2):
                    last = mm(b[:, 0:T], uq[:, k, c * P:c * P + P], cq[:, k, :], start=k == 0, stop=k == 1)
                last.then_inc(S("proj_mm"), 1)
            for hd in range(HEADS):
                q = slice(64 * (hd % 2), 64 * (hd % 2) + 64)
                b = step_begin(STEP_QA + hd)
                pe.wait_ge(S("proj_ev"), STEP_Q + hd // 2 + 1)
                mm(b[:, 0:T], uk[q, hd // 2, :], qT[q, hd // 2, :], start=True, stop=True).then_inc(S("proj_mm"), 1)
            b = step_begin(STEP_CT)
            for t in range(TT):
                last = nc.tensor.transpose(b[:, t * P:t * P + P], ckv[:, t * P:t * P + P], ident)
            last.then_inc(S("proj_mm"), 1)

            def logits(gi):
                qb, hh, w = gi // 2, gi % 2, P if gi < 2 else T
                pe.wait_ge(S("proj_ev"), STEPS)
                if gi > 0:
                    pe.wait_ge(S("lg_used"), gi)
                for j in range(4):
                    last = mm(psum[3][:, j // 2, (j % 2) * T:(j % 2) * T + w],
                              qabs[:, 4 * hh + j, qb * P:qb * P + P], ckv[:, 0:w], start=True, stop=True)
                last.then_inc(S("lg_mm"), 1)

            def context(gi):
                nst = 1 if gi < 2 else 2
                pe.wait_ge(S("p_ready"), gi + 1)
                for st in range(nst):
                    n = (0, 1, 2, 4)[gi] + st
                    if n > 0:
                        pe.wait_ge(S("pT_ready"), n)
                    for j in range(4):
                        last = nc.tensor.transpose(bank(5)[:, j * P:j * P + P],
                                                   pbuf[gi % 2][:, j, st * P:st * P + P], ident)
                    last.then_inc(S("pT_mm"), 1)
                if gi > 0:
                    pe.wait_ge(S("ctx_ready"), gi)
                for st in range(nst):
                    pe.wait_ge(S("pT_ready"), (0, 1, 2, 4)[gi] + st + 1)
                    last = mm(bank(4), ctok[:, st, :], pT[:, st, :], start=st == 0, stop=st == nst - 1)
                last.then_inc(S("ctx_mm"), 1)

            gemv(1)
            gemv_t(1)
            gemv(2)
            gemv_t(2)
            logits(0)
            gemv(3)
            for gi in range(4):
                if gi > 0:
                    gemv_t(2 + gi)
                context(gi)
                if gi < 3:
                    logits(gi + 1)
                if gi < 2:
                    gemv(4 + gi)
            pe.wait_ge(S("ctx_ready"), 4)
            for c in range(4):
                for j in range(2):
                    hd = 2 * c + j
                    last = mm(bank(3 + c // 2)[64 * j:64 * j + 64, (c % 2) * T:(c % 2) * T + T],
                              uv[:, 64 * hd:64 * hd + 64], ctxT[:, hd, :], start=True, stop=True)
                if c % 2:
                    last.then_inc(S("o_mm"), 1)
            pe.wait_ge(S("dpool_ready"), 1)
            pe.wait_ge(S("pT_ready"), 6)
            for gq in range(4):
                q = slice(64 * (gq % 2), 64 * (gq % 2) + 64)
                last = mm(bank(5)[q, (gq // 2) * T:(gq // 2) * T + T], pw[q, gq // 2, :], dpool[q, gq // 2, :],
                          start=True, stop=True)
            last.then_inc(S("pool_mm"), 1)
            pe.wait_ge(S("conv_done"), 2)
            for c in range(2):
                last = mm(bank(0)[:, 0:T], ones[:], cacc[:, c, :], start=c == 0, stop=c == 1)
            last.then_inc(S("cstat_mm"), 1)
            pe.wait_ge(S("csq_ready"), 1)
            for c in range(2):
                last = mm(bank(0)[:, T:2 * T], ones[:], csq[:, c, :], start=c == 0, stop=c == 1)
            last.then_inc(S("cstat_mm"), 1)

            def out_product(n, w, src, nk):
                for m in range(KD):
                    if m >= 2:
                        pe.wait_ge(S("res_used"), KD * n + m - 1)
                    for k in range(nk):
                        last = mm(bank(6 + m % 2)[:, 0:T], w(k)[:, m * P:m * P + P], src[:, k, :],
                                  start=k == 0, stop=k == nk - 1)
                    last.then_inc(S("res_mm"), 1)
                return last

            pe.wait_ge(S("loaded2"), 16 * 4)
            pe.wait_ge(S("y1_ready"), 6)
            wo = ring[:, 2, :].rearrange("p (k n) -> p k n", k=KD)
            out_product(0, lambda k: wo[:, k, :], y, KD)

            ms(sq2, 1)
            pe.wait_ge(S("h_ready"), 2 * KD)
            for t in range(TT):
                for k in range(KD):
                    last = mm(bank(1)[:, 36 * t:36 * t + 36], h2[:, k, t * P:t * P + P], rw[:, k, :],
                              start=k == 0, stop=k == KD - 1)
            last.then_inc(S("router_mm"), 1)
            for i in range(4):
                t, half = i // 2, i % 2
                if i >= 2:
                    pe.wait_ge(S("htok_ready"), i - 1)
                for q in range(4):
                    last = nc.tensor.transpose(bank(2 + i % 2)[:, q * P:q * P + P],
                                               h2[:, 4 * half + q, t * P:t * P + P], ident)
                last.then_inc(S("htok_mm"), 1)
            pe.wait_ge(S("asg_ready"), 1)
            asg = [rt[:, 192 + E * t:192 + E * t + E] for t in range(TT)]
            mm(bank(5)[:, 0:32], cst("tri"), asg[0], start=True, stop=True)
            mm(bank(5)[:, 32:64], cst("tri"), asg[1], start=True, stop=False)
            mm(bank(5)[:, 32:64], ones[:], asg[0], start=False, stop=True)
            mm(bank(5)[:, 64:96], ones[:], asg[0], start=True, stop=False)
            mm(bank(5)[:, 64:96], ones[:], asg[1], start=False, stop=True).then_inc(S("rank_mm"), 1)
            pe.wait_ge(S("htok_ready"), 4)
            pe.wait_ge(S("sweeps_ready"), 1)
            pe.sem_inc(S("gath_ev"), 2)
            pe.sem_inc(S("gath_mm"), 1)
            pe.sem_inc(S("up_mm"), AHEAD)
            pe.sem_inc(S("down_mm"), AHEAD)
            n_sw_ap = sweeps[0:1, 0:1]

            def pe_group(g):
                def slot(n):
                    s = (PRE_LOADS + n) % SLOTS
                    return s, g * 48 + 16 * (PRE[s] + n // SLOTS + 1)

                pe.wait_ge(S("onehot"), g * 2 + 2)
                for i in range(8):
                    pe.wait_ge(S("gath_ev"), g * 10 + (i + 1))
                    for t in range(TT):
                        last = mm(bank(7 - i % 2), htok[:, t, i * P:i * P + P], s_oh[:, t, :], start=t == 0, stop=t == 1)
                    last.then_inc(S("gath_mm"), 1)
                pe.wait_ge(S("gated"), g * 2 + 2)
                for i in range(2):
                    pe.wait_ge(S("gath_ev"), g * 10 + (i + 9))
                    for j in range(2):
                        for t in range(TT):
                            last = nc.tensor.transpose(bank(7 - i % 2)[:, j * T + t * P:j * T + t * P + P],
                                                       s_gt[:, t, (2 * i + j) * P:(2 * i + j) * P + P], ident)
                    last.then_inc(S("gath_mm"), 1)
                pe.wait_ge(S("gath_ev"), g * 10 + 12)
                for j in range(4):
                    for i in range(2):
                        s, at = slot(3 * j + i)
                        pe.wait_ge(S(f"loaded{s}"), at)
                        w = ring[:, s, :].rearrange("p (a k f) -> p a k f", a=2, k=KD)
                        for k in range(KD):
                            for e in range(2):
                                lo = (2 * j + e) * CAP
                                last = mm(bank(i)[64 * e:64 * e + 64, :], hsel[:, k, lo:lo + CAP], w[:, e, k, :],
                                          start=k == 0, stop=k == KD - 1)
                        last.then_inc(S("up_mm"), 1)
                    pe.wait_ge(S("hid_ready"), g * 4 + (j + 1))
                    for k in range(KF):
                        last = nc.tensor.transpose(bank(6)[:, k * P:k * P + P], hid[:, k * P:k * P + P], ident)
                    last.then_inc(S("hidT_mm"), 1)
                    s, at = slot(3 * j + 2)
                    pe.wait_ge(S("hidT_ready"), g * 4 + (j + 1))
                    pe.wait_ge(S(f"loaded{s}"), at)
                    w = ring[:, s, :].rearrange("p (a k n) -> p a k n", a=2, k=KF)
                    for half in range(2):
                        for k in range(KF):
                            for e in range(2):
                                last = mm(bank(2 + half)[64 * e:64 * e + 64, :], hidT[:, k, 64 * e:64 * e + 64],
                                          w[:, e, k, half * 512:half * 512 + 512], start=k == 0, stop=k == KF - 1)
                        last.then_inc(S("down_mm"), 1)
                    for c in range(4):
                        pe.wait_ge(S("y_ready"), g * 8 + (2 * j + c // 2 + 1))
                        pe.wait_ge(S("moe_add"), g * 16 + (4 * j + c + 1))
                        for q in range(2):
                            m = 2 * c + q
                            last = mm(bank(4 + c % 2)[:, q * T:q * T + T], yex[:, m * P:m * P + P], gT[:, j, :],
                                      start=True, stop=True)
                        last.then_inc(S("comb_mm"), 1)

            n_sw = pe.value_load(n_sw_ap, min_val=1, max_val=4)
            with pe.Fori(0, 4) as g:
                pe_group(g)
            with pe.If(n_sw > 1):
                with pe.Fori(4, n_sw * 4) as g:
                    pe_group(g)

            def post(j):
                s = (PRE_LOADS + j) % SLOTS
                pe.wait_ge(S(f"loaded_b{s}"), 16 * (j // SLOTS + 1))
                return s, ring[:, s, :]

            ms(view(2048, KD, T), 2)
            pe.wait_ge(S("root_ready"), 3)
            ms(view(2048, KD, T), 3)
            pe.wait_ge(S("h_ready"), 3 * KD)
            for j in range(4):
                s, w = post(j)
                width = 1024 if j < 3 else 520
                w = w[:, 0:KD * width].rearrange("p (k n) -> p k n", k=KD)
                for i in range(8 if j < 3 else 4):
                    n = 8 * j + i
                    if n >= 2:
                        pe.wait_ge(S("proj2_ev"), n - 1)
                    if n == 0:
                        pe.wait_ge(S("root_ready"), 4)
                    for k in range(KD):
                        last = mm(bank(n % 2)[:, 0:T], w[:, k, i * P:i * P + P], g_h[:, k, :], start=k == 0,
                                  stop=k == KD - 1)
                    last.then_inc(S("proj2_mm"), 1)
            for t in range(TT):
                for k in range(KD):
                    last = mm(bank(2)[:, 8 * t:8 * t + 8], g_h[:, k, t * P:t * P + P], w[:, k, 512:520],
                              start=k == 0, stop=k == KD - 1)
            last.then_inc(S("ab_mm"), 1)
            for i in range(4):
                pe.wait_ge(S("sq8_ready"), i + 1)
                if i >= 2:
                    pe.wait_ge(S("l2_root"), i - 1)
                for q in range(2):
                    last = mm(bank(4 + i % 2)[:, q * T:q * T + T], ones[:], sq8[:, 2 * i + q, :], start=True, stop=True)
                last.then_inc(S("l2_mm"), 1)
            pe.wait_ge(S("g_ready"), 1)
            pe.wait_ge(S("gcon_in"), 16)
            mm(bank(6)[:, 0:8], U_c, dl[:, 56:64], start=True, stop=True)
            mm(bank(6)[:, 8:16], ones_c, dl[:, 56:64], start=True, stop=True).then_inc(S("gcum_mm"), 1)
            pe.wait_ge(S("ab_ready"), 1)
            for t in range(TT):
                for hd in range(GH):
                    u = 4 * t + hd
                    last = mm(bank(2 + t)[:, hd * P:hd * P + P], dl[:, 56 + u:57 + u].to_broadcast([P, P]), U_c,
                              start=True, stop=True)
                last.then_inc(S("unit_mm"), 1)
            pe.wait_ge(S("proj2_ev"), 28)
            pe.wait_ge(S("l2_done"), 4)
            for t in range(TT):
                for hd in range(GH):
                    last = nc.tensor.transpose(bank(0 + t)[:, hd * P:hd * P + P], qkv[:, 4 + hd, t * P:t * P + P], ident)
                last.then_inc(S("unit_mm"), 1)
            pe.wait_ge(S("qkv_ready"), 12)
            pe.wait_ge(S("gcol_ready"), 1)
            for t in range(TT):
                for hd in range(GH):
                    last = nc.tensor.transpose(bank(6 + t)[:, hd * P:hd * P + P], qkv[:, 8 + hd, t * P:t * P + P], ident)
                last.then_inc(S("unit_mm"), 1)
            pe.wait_ge(S("l2_root"), 4)
            for t in range(TT):
                for hd in range(GH):
                    kt = qkv[:, 4 + hd, t * P:t * P + P]
                    last = mm(bank(4 + t)[:, hd * P:hd * P + P], kt, kt, start=True, stop=True)
                last.then_inc(S("unit_mm"), 1)
            pe.wait_ge(S("beta_ready"), 1)
            for t in range(TT):
                pe.wait_ge(S("expg_ready"), t + 1)
                pe.wait_ge(S("dec_arg"), t + 1)
                for hd in range(GH):
                    u = 4 * t + hd
                    last = mm(bank(2 + t)[:, hd * P:hd * P + P], dl[:, 40 + u:41 + u].to_broadcast([P, P]), ident,
                              start=True, stop=True)
                last.then_inc(S("unit_mm"), 1)
            pe.wait_ge(S("k_used"), 8)
            for t in range(TT):
                for hd in range(GH):
                    last = mm(bank(0 + t)[:, hd * P:hd * P + P], qkv[:, 4 + hd, t * P:t * P + P],
                              qkv[:, hd, t * P:t * P + P], start=True, stop=True)
                last.then_inc(S("unit_mm"), 1)
            pe.wait_ge(S("kk_used"), 2)
            for t in range(TT):
                pe.wait_ge(S("ttm_ready"), t + 1)
                for hd in range(GH):
                    last = nc.tensor.transpose(bank(4 + t)[:, hd * P:hd * P + P], ttm[:, 4 * t + hd, :], ident)
                last.then_inc(S("merge0_mm"), 1)
            pe.wait_ge(S("attn_ready"), 2)
            for lv in range(1, LEVELS):
                for t in range(TT):
                    pe.wait_ge(S("lm_ready"), TT * (lv - 1) + t + 1)
                    if lv == 1:
                        pe.wait_ge(S("tm0_ready"), t + 1)
                    else:
                        pe.wait_ge(S("tm_ready"), TT * (lv - 2) + t + 1)
                    for hd in range(GH):
                        u = 4 * t + hd
                        last = mm(bank(t)[:, hd * P:hd * P + P], lm[:, u, :], tm[:, u, :], start=True, stop=True)
                    last.then_inc(S("merge_p_mm"), 1)
                for t in range(TT):
                    pe.wait_ge(S("pm_ready"), TT * (lv - 1) + t + 1)
                    pe.wait_ge(S("ttm_ready"), TT * (lv - 1) + t + 1)
                    if lv < LEVELS - 1:
                        for hd in range(GH):
                            u = 4 * t + hd
                            last = mm(bank(4 + t)[:, hd * P:hd * P + P], ttm[:, u, :], pm[:, u, :], start=True,
                                      stop=True)
                        last.then_inc(S("merge_t_mm"), 1)
                    for hd in range(GH):
                        u = 4 * t + hd
                        last = mm(bank(2 + t)[:, hd * P:hd * P + P], pm[:, u, :], ttm[:, u, :], start=True, stop=True)
                    last.then_inc(S("merge_tt_mm"), 1)
            for t in range(TT):
                pe.wait_ge(S("ttm_ready"), TT * (LEVELS - 1) + t + 1)
                for hd in range(GH):
                    u = 4 * t + hd
                    last = mm(bank(4 + t)[:, hd * P:hd * P + P], kbe[:, u, :], ttm[:, u, :], start=True, stop=True)
                last.then_inc(S("wt_mm"), 1)
            pe.wait_ge(S("v_used"), 8)
            pe.wait_ge(S("wt_ready"), 2)
            pe.wait_ge(S("qdec_ready"), 8)
            for n in range(NCH):
                t, o = n // 2, 64 * (n % 2)
                q = slice(o, o + 64)
                if n >= 1:
                    pe.wait_ge(S("state_ready"), 4 * n)
                if n >= 2:
                    pe.wait_ge(S("o_ready"), n - 1)
                for hd in range(GH):
                    u = 4 * t + hd
                    dst = bank(n % 2)[q, hd * P:hd * P + P]
                    last = mm(dst, ttm[q, u, o:o + 64], vb[q, u, :], start=True, stop=n == 0)
                    if n > 0:
                        last = mm(dst, wtn[:, u, o:o + 64], state[:, hd, :], start=False, stop=True)
                last.then_inc(S("vnew_mm"), 1)
                pe.wait_ge(S("vnew_ready"), n + 1)
                if n < NCH - 1:
                    for hd in range(GH):
                        u = 4 * t + hd
                        last = mm(bank(6 + n % 2)[:, hd * P:hd * P + P], kdec[q, u, :], vnew[q, hd, :], start=True,
                                  stop=True)
                    last.then_inc(S("state_mm"), 1)
                for hd in range(GH):
                    u = 4 * t + hd
                    dst = bank(2 + n % 2)[:, 64 * hd:64 * hd + 64]
                    last = mm(dst, vnew[q, hd, :], attn_t[q, u, o:o + 64], start=True, stop=n == 0)
                    if n > 0:
                        last = mm(dst, state[:, hd, :], qkv[:, hd, 64 * n:64 * n + 64], start=False, stop=True)
                last.then_inc(S("out_mm"), 1)
            pe.wait_ge(S("osq_ready"), 1)
            for i in range(2):
                for q in range(2):
                    last = mm(bank(4 + i)[:, q * T:q * T + T], ones[:], o_sq[:, 2 * i + q, :], start=True, stop=True)
                last.then_inc(S("l2_mm"), 1)
            pe.wait_ge(S("y2_ready"), 6)
            s, w = post(4)
            wo2 = w.rearrange("p (k n) -> p k n", k=KD)
            out_product(1, lambda k: wo2[:, k, :], g_y, KD)
            ms(view(2048, KD, T), 4)
            pe.wait_ge(S("h_ready"), 4 * KD)
            for f in range(NFF):
                j, i = 5 + f // 4, f % 4
                half = 512 if j < 10 else 256
                if i == 0:
                    s, w = post(j)
                    w = w[:, 0:KD * 2 * half].rearrange("p (k n) -> p k n", k=KD)
                if f >= 2:
                    pe.wait_ge(S("hff_ready"), f - 1)
                for b, off, name in ((2 * (f % 2) + 2, 0, "ff_gate_mm"), (2 * (f % 2) + 3, half, "ff_up_mm")):
                    for k in range(KD):
                        last = mm(bank(b)[:, 0:T], w[:, k, off + i * P:off + i * P + P], f_h[:, k, :], start=k == 0,
                                  stop=k == KD - 1)
                    last.then_inc(S(name), 1)
            down = [post(11 + j)[1].rearrange("p (k n) -> p k n", k=KD) for j in range(3)]
            pe.wait_ge(S("hff_ready"), NFF)
            out_product(2, lambda k: down[k // 8][:, k % 8, :], hff, NFF)
            ms(view(2048, KD, T), 5)


def _tiles(w):
    r, n = w.shape
    return np.ascontiguousarray(w.reshape(r // P, P, n).transpose(1, 0, 2)).reshape(P, (r // P) * n)


def _cols(v):
    return v.reshape(-1, P).T


def _constants():
    i = np.arange(P)
    const = np.zeros((P, NCONST), np.float32)
    const[:, CONST["ident"][0]:CONST["ident"][1]] = np.eye(P)
    const[:, CONST["tri"][0]:CONST["tri"][1]] = i[:, None] < i[None, :]
    const[:, CONST["iota"][0]:CONST["iota"][1]] = np.arange(CAP)
    const[:, CONST["prio"][0]:CONST["prio"][1]] = 8 - np.arange(8)
    aconst = np.zeros((P, 4, T), np.float32)
    s = np.arange(T)
    for qb in range(2):
        aconst[:, qb] = np.where((s[None, :] // CHUNK) <= ((qb * P + i[:, None]) // CHUNK), 0.0, MASKED)
    for c in range(2):
        for half in range(2):
            w = (2, 4, 8, 16)[2 * c + half]
            aconst[64 * half:64 * half + 64, 2 + c] = 1.0 / np.minimum(s + 1, w)
    g = np.zeros((P, 3 + LEVELS, P), np.float32)
    same = (i[:, None] // CHUNK) == (i[None, :] // CHUNK)
    g[:, 0] = same & (i[:, None] <= i[None, :])
    g[:, 1] = same
    g[:, 2] = np.where(same & (i[:, None] <= i[None, :]), 0.0, MASKED)
    for lv in range(LEVELS):
        b = 1 << lv
        pair = (i[:, None] // (2 * b)) == (i[None, :] // (2 * b))
        g[:, 3 + lv] = pair & ((i[:, None] // b) % 2 == 0) & ((i[None, :] // b) % 2 == 1)
    return const, aconst, g


def kernel(**inp):
    from concourse import bacc
    from concourse.bass_utils import run_bass_kernel_spmd

    inp = {k: np.asarray(v) for k, v in inp.items()}
    C = np.ascontiguousarray

    def passes(w):
        return C(w.reshape(2, 4, P, 3, 2048).transpose(3, 0, 2, 1, 4)).reshape(6, P, SLOT)

    win = inp["w_in"][0]
    ki = win[:, 1408:1472]
    wa = np.concatenate([ki, ki, win[:, 896:1408], win[:, 512:896]], axis=1)
    wb = np.concatenate([win[:, 0:512], win[:, 1480:1736], win[:, 1472:1480]], axis=1)
    w2 = inp["w_in_2"][0]
    gate, up, down = inp["w_gate_2"][0], inp["w_up_2"][0], inp["w_down_2"][0]
    ffu = np.stack([_tiles(np.concatenate([gate[:, 512 * i:512 * i + 512], up[:, 512 * i:512 * i + 512]], axis=1))
                    for i in range(5)])
    vectors = [_cols(inp["c"][0]), _cols(inp["c_2"][0]), _cols(inp["mod_b"][0]), _cols(inp["b_ada_2"][0]),
               _cols(inp["norm1_g"][0]), _cols(inp["norm2_g"][0]), _cols(inp["final_g"]), _cols(inp["norm1_w_2"][0]),
               _cols(inp["norm2_w_2"][0]), _cols(inp["norm_f_w_2"]), _cols(inp["conv_b"][0]),
               _cols(inp["conv_ln_g"][0]), _cols(inp["conv_ln_b"][0]), _cols(inp["q_norm_g"][0]),
               _cols(inp["kv_norm_g"][0]), _cols(inp["pool_scale"][0]),
               inp["conv_k"][0].reshape(CONV_W, 2, P).transpose(2, 1, 0).reshape(P, 2 * CONV_W),
               inp["conv_qkv_w_2"][0].reshape(4, 12, P).transpose(2, 1, 0).reshape(P, 48),
               inp["conv_short_w_2"][0].reshape(3, 4, P).transpose(2, 1, 0).reshape(P, 12),
               _cols(inp["gdn_norm_w_2"][0]),
               np.broadcast_to(inp["router_g_b"][0].reshape(1, 4), (P, 4)),
               np.broadcast_to(inp["router_e_b"][0].reshape(1, 32), (P, 32)),
               np.broadcast_to(inp["A_log_2"][0].reshape(1, 4), (P, 4)),
               np.broadcast_to(inp["dt_bias_2"][0].reshape(1, 4), (P, 4))]
    pool_w = inp["pool_w"][0].reshape(2, 2, 64, 64).transpose(1, 2, 0, 3).reshape(P, 128)
    router = np.concatenate([inp["router_g_w"][0], inp["router_e_w"][0].reshape(D, E)], axis=1)
    uk = inp["w_uk"][0].transpose(1, 2, 0).reshape(4, P, P).transpose(1, 0, 2).reshape(P, 512)
    smallw = [_tiles(inp["w_uq"][0].reshape(256, 512)), uk, inp["w_uv"][0].reshape(P, 512), pool_w, _tiles(router)]
    const, aconst, gconst = _constants()

    def experts(w):
        e, r, n = w.shape
        return C(w.reshape(e, r // P, P, n).transpose(0, 2, 1, 3)).reshape(e, P, (r // P) * n)

    arrays = {
        "xT": C(inp["x"][0].T.reshape(KD, P, T).transpose(1, 0, 2)),
        "mod_w": passes(inp["mod_w"][0]), "ada_w": passes(inp["w_ada_2"][0]),
        "winA": _tiles(wa), "winB": _tiles(wb), "wout": _tiles(inp["w_out"][0]),
        "ew1": experts(inp["exp_w1"][0]), "ew3": experts(inp["exp_w3"][0]), "ew2": experts(inp["exp_w2"][0]),
        "w2A": _tiles(w2[:, 0:1024]), "w2B": _tiles(w2[:, 1024:2048]), "w2C": _tiles(w2[:, 2056:3080]),
        "w2D": _tiles(np.concatenate([w2[:, 3080:3592], w2[:, 2048:2056]], axis=1)),
        "wout2": _tiles(inp["w_out_2"][0]),
        "ffu": ffu, "ffu_last": _tiles(np.concatenate([gate[:, 2560:], up[:, 2560:]], axis=1)),
        "ffd": np.stack([_tiles(down[0:1024]), _tiles(down[1024:2048])]), "ffd_last": _tiles(down[2048:]),
        "cols_d": C(np.concatenate(vectors, axis=1)), "small_d": C(np.concatenate(smallw, axis=1)),
        "const_d": const, "aconst_d": aconst, "gconst_d": gconst,
    }
    nc = bacc.Bacc("TRN2", target_bir_lowering=False, num_devices=1)
    aps = {k: nc.dram_tensor("in_" + k, a.shape, mybir.dt.from_np(a.dtype), kind="ExternalInput").ap()
           for k, a in arrays.items()}
    out = nc.dram_tensor("out_dram", (P, KD, T), mybir.dt.float32, kind="ExternalOutput").ap()
    program(nc, out=out, **aps)
    r = run_bass_kernel_spmd(nc, [{"in_" + k: a for k, a in arrays.items()}], core_ids=[0])
    got = r.results[0]["out_dram"]
    return np.ascontiguousarray(got.transpose(1, 0, 2).reshape(D, T).T).reshape(1, T, D)
```

```python
from contextlib import ExitStack

import concourse.bass as bass
import numpy as np
from concourse import mybir

P = 128
D = 1024
KD = D // P
T = 256
TT = T // P
EPS = 1e-6
CONV_W = 31
HEADS, HD = 8, 64
TOPK = 64
IDX_SCALE = float((8 * 64) ** -0.5)
ATT_SCALE = float(HD ** -0.5)
CHUNK = 64
E, EG, F = 32, 8, 512
KF = F // P
CAP = 64
MASKED = -1.0e30
TAKEN = -3.0e38
GH = 4
NCH = T // CHUNK
FF = 2816
NFF = FF // P
LEVELS = 6

SLOTS, SLOT = 4, 8192
PRE_LOADS = 15
PRE = [(PRE_LOADS - s + SLOTS - 1) // SLOTS for s in range(SLOTS)]

COLS = {}
_n = 0
for _name, _w in (("c", 8), ("c2", 8), ("mod_b", 48), ("ada_b", 48), ("n1", 8), ("n2", 8), ("nf", 8),
                  ("n1b", 8), ("n2b", 8), ("nfb", 8), ("conv_b", 2), ("ln_g", 2), ("ln_b", 2),
                  ("q_g", 2), ("kv_g", 1), ("pool_s", 2), ("conv_k", 2 * CONV_W), ("gconv", 48),
                  ("sconv", 12), ("gnorm", 1), ("rbias", 36), ("a_log", 4), ("dt", 4), ("abw", 64)):
    COLS[_name] = (_n, _n + _w)
    _n += _w
NCOL = _n
SMALL = {}
_n = 0
for _name, _w in (("uq", 1024), ("uk", 512), ("uv", 512), ("pw", 128), ("rw", 288)):
    SMALL[_name] = (_n, _n + _w)
    _n += _w
NSMALL = _n
CONST = {}
_n = 0
for _name, _w in (("ident", 128), ("tri", 128), ("iota", 64), ("prio", 8)):
    CONST[_name] = (_n, _n + _w)
    _n += _w
NCONST = _n
NACONST = 1024
NGCONST = 128 * (3 + LEVELS)


def program(nc, xT, mod_w, ada_w, winA, winB, wout, ew1, ew3, ew2, w2A, w2B, w2C, w2D, wout2,
            ffu, ffu_last, ffd, ffd_last, cols_d, small_d, const_d, aconst_d, gconst_d, out):
    fp32 = mybir.dt.float32
    i32 = mybir.dt.int32
    ACT = mybir.ActivationFunctionType
    ALU = mybir.AluOpType
    AX = mybir.AxisListType.X

    with ExitStack() as ctx:
        def sb(name, shape, dt=fp32):
            return ctx.enter_context(nc.sbuf_tensor(name, shape, dt))

        sems, count = {}, {}

        def S(name):
            if name not in sems:
                sems[name] = ctx.enter_context(nc.semaphore(name))
                count[name] = 0
            return sems[name]

        for s in range(SLOTS):
            S(f"loaded{s}"), S(f"loaded_b{s}")

        ring = sb("ring", [P, SLOTS, SLOT])
        x = sb("x_res", [P, KD, T])
        cols = sb("cols", [P, NCOL])
        const = sb("const", [P, NCONST])
        ones = sb("ones", [P, P])
        zero = sb("zero", [P, 1])
        one = sb("one", [P, 1])
        eps = sb("eps", [P, 1])
        mod1 = sb("mod1", [P, 48])
        mod2 = sb("mod2", [P, 48])
        gain = sb("gain", [P, 4, KD])
        cact = sb("cact", [P, 2, 8])
        sweeps = sb("sweeps", [P, 1], i32)
        small = sb("smalls", [P, 64])
        rst = sb("rst", [P, 2, T])
        ARENA = 16444
        arena = sb("arena", [P, ARENA])
        psum = [ctx.enter_context(nc.psum_tensor(f"bank{i}", [P, 2, 512], fp32)) for i in range(4)]

        def bank(i):
            return psum[i // 2][:, i % 2, :]

        def view(off, *shape):
            n = 1
            for d in shape:
                n *= d
            assert off + n <= ARENA, (off, shape)
            v = arena[:, off:off + n]
            if len(shape) == 2:
                v = v.rearrange("p (a b) -> p a b", a=shape[0])
            if len(shape) == 3:
                v = v.rearrange("p (a b c) -> p a b c", a=shape[0], b=shape[1])
            return v

        def col(name, i=0, n=1):
            a = COLS[name][0] + i
            return cols[:, a:a + n]

        def cst(name):
            return const[:, CONST[name][0]:CONST[name][1]]

        ident = cst("ident")

        PRE_SLOT = [0, 1, 2, 3, 0, 1, 2, 0, 1, 3, 2, 0, 3, 2, 0]
        EXP_SLOT = [3, 2, 0, 1]
        POST_SLOT = [3, 2, 0, 1, 2, 0, 1, 3, 2, 0, 1, 3, 2, 0]
        PRE = [PRE_SLOT.count(s) for s in range(SLOTS)]
        PASS = [(0, 1), (4, 5), (6, 7), (9, 10), (11, 12), (13, 14)]

        def landed(n):
            return 16 * PRE_SLOT[:n + 1].count(PRE_SLOT[n])

        h = view(0, KD, T)
        qabs = view(0, HEADS, T)
        ctxT = view(2048, HEADS, T)
        aval = view(2048, 2, T)
        cgate = view(2560, 2, T)
        smallw = view(4096, NSMALL)
        uq = smallw[:, 0:1024].rearrange("p (k n) -> p k n", k=2)
        uk = smallw[:, 1024:1536].rearrange("p (k n) -> p k n", k=4)
        uv = smallw[:, 1536:2048]
        pw = smallw[:, 2048:2176].rearrange("p (g n) -> p g n", g=2)
        rw = smallw[:, 2176:2464].rearrange("p (k n) -> p k n", k=KD)
        z_att = view(6560, 8, T)
        ki, qi, cq, ckv = z_att[:, 0, :], z_att[:, 1:5, :], z_att[:, 5:7, :], z_att[:, 7, :]
        rel = view(8608, 3, T)
        qT = view(9376, 4, T)
        UPW, PPW = T + CONV_W - 1, T + 16
        psums = view(10400, 2, 2 * PPW)
        upad = view(11488, 2, UPW)
        ppad = view(12060, 2, PPW)
        y = view(12604, KD, T)
        ctok = view(14652, TT, P)
        score = view(14908, TT, T)
        aconst = view(15420, 4, T)
        selb = aconst
        pbuf = [view(6816, 4, T), view(9376, 4, T)]
        pT = view(12604 + 512, 2, 512)
        modrow = [view(12604 + 1536, 512)] * 4 + [view(8608, 512)] * 2
        cacc = y[:, 0:2, :]
        csq = view(11488, 2, T)
        dpool = cq
        wi = small[:, 0:16].rearrange("p (t h) -> p t h", t=TT)
        top8, ssum, rsum = small[:, 16:24], small[:, 28:36], small[:, 36:40]
        mx = [small[:, 24:28], small[:, 40:44]]

        htok = view(0, TT, D)
        s_oh = view(2048, TT, EG * CAP)
        s_gt = view(3072, TT, EG * CAP)
        gT = view(4096, 4, T)
        hsel = view(7168, KD, EG * CAP)
        h2 = view(11264, KD, T)
        sil, hid = view(11264, 512), view(11776, 512)
        hidT = view(12288, KF, P)
        yex = view(12800, D)
        rt = view(13824, 512)
        rank_s = view(14336, TT, 4 * E)
        gate_s = view(14592, TT, 4 * E)
        sq_xn = view(0, KD, 2, T)

        g_h = view(0, KD, T)
        g_y = view(2048, KD, T)
        qkv = view(4096, 12, T)
        raw = view(7168, 12, T + 3)
        zg = view(10276, 4, T)
        scb, scc = view(11300, 4, T), view(12324, 4, T)
        scp = view(13348, 4, T + 2)
        gcon = view(14380, 3 + LEVELS, P)
        dl = view(15532, 144)
        SCR = POST_SLOT[0]

        def scr(i):
            v = ring[:, SCR, 1024 * i:1024 * (i + 1)]
            return v.rearrange("p (u c) -> p u c", u=8)
        dec, lt, expg, attn_t, tm, ttm, pm, lm = [scr(i) for i in range(8)]
        sq8 = view(7168, 8, T)
        kdec, vb, kbe = view(7168, 8, P), view(8192, 8, P), view(12324, 8, P)
        wtn = lm
        state, vnew = tm[:, 0:4, :], tm[:, 4:8, :]
        o_t, o_sq = [ring[:, SCR, 1024 * i:1024 * (i + 1)].rearrange("p (h c) -> p h c", h=GH) for i in range(2)]
        hff = view(4096, NFF, T)
        sff = view(9728, 2, 2, T)
        f_h = view(0, KD, T)
        U_c, ones_c, mask_c = gcon[:, 0, :], gcon[:, 1, :], gcon[:, 2, :]

        rcol = small[:, 44:52]
        gnf = small[:, 52:60]
        xsq = [view(12604, 3, T)] + [view(15676, 3, T)] * 4
        GATH = (7, 3)
        STAT = (0, 5)

        block = ctx.enter_context(nc.Block())

        SERIES = [("a", 0), ("a", 1), ("g", 0), ("g", 1), ("p", 0), ("p", 1), ("wi", 0)]
        SERIES += [("lat", i) for i in range(3)] + [("ki", 0)] + [("qi", i) for i in range(4)]
        SERIES += [("ix", 0), ("ix", 1), ("q", 0), ("ix", 2), ("q", 1), ("ix", 3), ("q", 2), ("ix", 4), ("q", 3)]
        SERIES += [("ix", 5), ("ix", 6), ("ix", 7), ("ct", 0)]
        SERIES += [(kind, i + d) for i in range(8) for kind, d in (("qa", 0), ("ix", 8))]
        AFTER = {step: i + 1 for i, step in enumerate(SERIES)}
        AHEAD = 8
        GROW, KTOK, KK, BROW, VTOK, KQ = 0, 2, 4, 6, 8, 10
        PROJ2 = [(kind, i) for kind in "qkvz" for i in range(4)] + [(kind, i) for i in range(4) for kind in "bch"]
        PROJ2_BANK = [i % 2 for i in range(16)] + [7] + [4 + i % 2 for i in range(17, 28)]

        @block.sync
        def _(sp):
            sp.dma_start(x[:], xT).then_inc(S("x_in"), 16)
            sp.dma_start(cols[:], cols_d).then_inc(S("small_in"), 16)
            sp.dma_start(const[:], const_d).then_inc(S("small_in"), 16)
            pre = [(mod_w[0], SLOT, None), (mod_w[1], SLOT, None), (winB, winB.shape[1], None), (winA, SLOT, None),
                   (mod_w[2], SLOT, ("gemv_mm", 1)), (mod_w[3], SLOT, ("gemv_mm", 1)),
                   (mod_w[4], SLOT, ("proj_mm", AFTER["wi", 0])), (mod_w[5], SLOT, ("gemv_mm", 2)),
                   (wout, SLOT, ("gemv_mm", 2)), (ada_w[0], SLOT, ("proj_mm", AFTER["qi", 3])),
                   (ada_w[1], SLOT, ("gemv_mm", 3)), (ada_w[2], SLOT, ("gemv_mm", 3)),
                   (ada_w[3], SLOT, ("gemv_mm", 4)), (ada_w[4], SLOT, ("gemv_mm", 4)),
                   (ada_w[5], SLOT, ("gemv_mm", 5))]
            for n, (src, width, used) in enumerate(pre):
                s = PRE_SLOT[n]
                if used:
                    sp.wait_ge(S(used[0]), used[1])
                sp.dma_start(ring[:, s, 0:width], src).then_inc(S(f"loaded{s}"), 16)
                if n == 2:
                    sp.dma_start(aconst[:], aconst_d).then_inc(S("att_in"), 16)
                    sp.dma_start(smallw[:], small_d).then_inc(S("att_in"), 16)

            def expert_used(g8, n):
                if n % 3 < 2:
                    sp.wait_ge(S("up_mm"), g8 + (AHEAD + 2 * (n // 3) + n % 3 + 1))
                else:
                    sp.wait_ge(S("down_mm"), g8 + (AHEAD + 2 * (n // 3) + 2))

            def expert_load(e8, n):
                s = EXP_SLOT[n % SLOTS]
                w = (ew1, ew3, ew2)[n % 3]
                pair = w[bass.ds(e8 + 2 * (n // 3), 2), :, :]
                sp.dma_start(ring[:, s, :].rearrange("p (a f) -> p a f", a=2),
                             pair.rearrange("a p f -> p a f")).then_inc(S(f"loaded{s}"), 16)

            for n, used in enumerate([("gemv_mm", 5), ("gemv_mm", 6), ("gemv_mm", 6), ("res_mm", KD)]):
                sp.wait_ge(S(used[0]), used[1])
                expert_load(0, n)
            with sp.Fori(0, 3) as g:
                for n in range(SLOTS, 12 + SLOTS):
                    expert_used(g * 8, n - SLOTS)
                    expert_load(g * 8 + 8 * (n // 12), n % 12)
            for n in range(SLOTS, 12):
                expert_used(3 * 8, n - SLOTS)
                expert_load(3 * 8, n)
            sp.wait_ge(S("sweeps_ready"), 1)
            n_sw = sp.value_load(sweeps[0:1, 0:1], min_val=1, max_val=4)
            with sp.If(n_sw > 1):
                with sp.Fori(4, n_sw * 4) as g:
                    for n in range(12):
                        expert_used(g * 8, n - SLOTS)
                        expert_load((g % 4) * 8, n)
            post = [(w2A, SLOT), (w2B, SLOT), (w2C, SLOT), (w2D, w2D.shape[1]), (wout2, SLOT)]
            post += [(ffu[i], SLOT) for i in range(5)] + [(ffu_last, SLOT // 2)]
            post += [(ffd[i], SLOT) for i in range(2)] + [(ffd_last, 6 * D)]
            used_b = [("proj2_mm", 16), ("proj2_mm", 27), ("proj2_mm", 28), ("delta_done", 1), ("res_mm", 2 * KD)]
            used_b += [("ff_up_mm", 4 * i + 4) for i in range(5)]
            for j, (src, width) in enumerate(post):
                s = POST_SLOT[j]
                if j < SLOTS:
                    expert_used(n_sw * 32, j - SLOTS)
                else:
                    sp.wait_ge(S(used_b[j - SLOTS][0]), used_b[j - SLOTS][1])
                sp.dma_start(ring[:, s, 0:width], src).then_inc(S(f"loaded_b{s}"), 16)
            for i in range(KD // 2):
                sp.wait_ge(S("out_ready"), 2 * i + 2)
                sp.dma_start(out[:, 2 * i:2 * i + 2, :], f_h[:, 2 * i:2 * i + 2, :]).then_inc(S("stored"), 16)
            sp.wait_ge(S("stored"), 16 * (KD // 2))

        @block.gpsimd
        def _(pool):
            def p(ins, name="pool_step"):
                ins.then_inc(S(name), 1)
                count[name] += 1
                pool.wait_ge(S(name), count[name])

            p(nc.gpsimd.memset(ppad[:, :, 0:16], 0.0), "pool_pad")
            pool.wait_ge(S("proj_ev"), AFTER["p", 1])
            s_a = psums[:, 0, :].rearrange("p (c t) -> p c t", c=2)
            s_b = psums[:, 1, :].rearrange("p (c t) -> p c t", c=2)
            p(nc.gpsimd.memset(psums, 0.0))
            p(nc.gpsimd.tensor_tensor(s_a[:, :, 1:PPW], ppad[:, :, 1:PPW], ppad[:, :, 0:PPW - 1], ALU.add))
            p(nc.gpsimd.tensor_tensor(s_b[:, :, 3:PPW], s_a[:, :, 3:PPW], s_a[:, :, 1:PPW - 2], ALU.add))
            p(nc.gpsimd.tensor_tensor(s_a[:, 1, 7:PPW], s_b[:, 1, 7:PPW], s_b[:, 1, 3:PPW - 4], ALU.add))
            p(nc.gpsimd.tensor_tensor(s_b[:, 1, 15:PPW], s_a[:, 1, 15:PPW], s_a[:, 1, 7:PPW - 8], ALU.add))
            pool.wait_ge(S("proj_mm"), AFTER["q", 3])
            pool.wait_ge(S("att_in"), 32)
            for c in range(2):
                for half, sums in ((0, s_a), (64, s_b)):
                    q = slice(half, half + 64)
                    p(nc.gpsimd.tensor_tensor(dpool[q, c, :], sums[q, c, 16:PPW], aconst[q, 2 + c, :], ALU.mult))
                    p(nc.gpsimd.tensor_tensor(dpool[q, c, :], dpool[q, c, :], ppad[q, c, 16:PPW], ALU.subtract),
                      "dpool_ready" if (c, half) == (1, 64) else "pool_step")

            for lv in range(1, LEVELS):
                for t in range(TT):
                    pool.wait_ge(S("lt_ready"), 1)
                    if lv > 1:
                        pool.wait_ge(S("merge_p_mm"), TT * (lv - 2) + t + 1)
                    nc.gpsimd.tensor_tensor(lm[:, 4 * t:4 * t + 4, :], lt[:, 4 * t:4 * t + 4, :],
                                            gcon[:, 3 + lv, :].unsqueeze(1).to_broadcast([P, 4, P]),
                                            ALU.mult).then_inc(S("lm_ready"), 1)

        @block.scalar
        def _(act):
            def a(ins, name):
                ins.then_inc(S(name), 1)
                count[name] += 1

            act.wait_ge(S("small_in"), 32)
            act.wait_ge(S("init"), 1)
            a(nc.scalar.activation(cact[:, 0, :], col("c", 0, 8), ACT.Silu, bias=zero[:]), "cact_ready")
            a(nc.scalar.activation(cact[:, 1, :], col("c2", 0, 8), ACT.Silu, bias=zero[:]), "cact_ready")

            def root(src, dst, n, mm, at, out_name):
                act.wait_ge(S(mm), at)
                a(nc.scalar.activation(dst, src, ACT.Sqrt, scale=1.0 / n, bias=eps[:]), out_name)

            def norm_root(n):
                act.wait_ge(S("ms_mm"), n + 1)
                for t in range(TT):
                    a(nc.scalar.activation(rcol[:, t:t + 1], bank(STAT[t])[:, 0:1], ACT.Sqrt, scale=1.0 / D,
                                           bias=eps[:]), "root_ready")

            def shifted(dst, n, mod, shift):
                for k in range(KD):
                    act.wait_ge(S("scaled"), 8 * n + k + 1)
                    a(nc.scalar.activation(dst[:, k, :], dst[:, k, :], ACT.Identity,
                                           bias=mod[:, shift * 8 + k:shift * 8 + k + 1]), "h_ready")

            def gemv_row(r):
                act.wait_ge(S("gemv_mm"), r + 1)
                if r > 0:
                    act.wait_ge(S("modT_mm"), r)
                a(nc.scalar.activation(modrow[r], bank(1), ACT.Copy), "modrow_ready")

            norm_root(0)
            gemv_row(0)
            shifted(h, 0, mod1, 0)

            def step_out(i):
                act.wait_ge(S("proj_mm"), i + 1)
                src = bank(3 + i % 2)
                kind, n = SERIES[i]
                func, kw = ACT.Copy, {}
                if kind == "a":
                    dst = aval[:, n, :]
                elif kind == "g":
                    dst, func, kw = cgate[:, n, :], ACT.Sigmoid, {"bias": zero[:]}
                elif kind == "p":
                    act.wait_ge(S("pool_pad"), 1)
                    dst = ppad[:, n, 16:PPW]
                elif kind == "wi":
                    dst = small[:, 0:16]
                elif kind in ("lat", "ki", "qi"):
                    dst = z_att[:, {"lat": 5, "ki": 0, "qi": 1}[kind] + n, :]
                elif kind == "ix":
                    if n >= 2:
                        act.wait_ge(S("idx_acc"), n - 1)
                    dst, func = rel[:, n % 2, 0:P if n < 8 else T], ACT.Relu
                elif kind == "q":
                    dst = qT[:, n, :]
                elif kind == "qa":
                    dst = qabs[:, n, :]
                else:
                    dst = ctok.rearrange("p t c -> p (t c)")
                a(nc.scalar.activation(dst, src[:, 0:dst.shape[1]], func, **kw), "proj_ev")

            for i in range(AFTER["ki", 0]):
                step_out(i)
            act.wait_ge(S("lat_mm"), 1)
            a(nc.scalar.activation(rst[:, 0, :], bank(0)[:, 0:T], ACT.Sqrt, scale=1.0 / 256, bias=eps[:]), "lat_root")
            a(nc.scalar.activation(rst[:, 1, :], bank(0)[:, T:2 * T], ACT.Sqrt, scale=1.0 / 128, bias=eps[:]), "lat_root")
            gemv_row(1)
            for i in range(AFTER["ki", 0], AFTER["ct", 0]):
                step_out(i)
            gemv_row(2)
            for i in range(AFTER["ct", 0], len(SERIES)):
                step_out(i)

            def exps(gi):
                w = P if gi < 2 else T
                act.wait_ge(S("max_ready"), gi + 1)
                for j in range(4):
                    a(nc.scalar.activation(pbuf[gi % 2][:, j, 0:w], pbuf[gi % 2][:, j, 0:w], ACT.Exp,
                                           bias=mx[gi % 2][:, j:j + 1],
                                           accum_out=ssum[:, 4 * (gi % 2) + j:4 * (gi % 2) + j + 1]), "exp_done")

            def pt_out(gi):
                for st in range(1 if gi < 2 else 2):
                    n = (0, 1, 2, 4)[gi] + st
                    act.wait_ge(S("pT_mm"), n + 1)
                    if gi > 0:
                        act.wait_ge(S("ctx_mm"), gi)
                    a(nc.scalar.activation(pT[:, st, :], bank(5), ACT.Copy), "pT_ready")

            def ctx_out(gi):
                act.wait_ge(S("ctx_mm"), gi + 1)
                if gi == 0:
                    act.wait_ge(S("u_ready"), 1)
                qb, hh = gi // 2, gi % 2
                a(nc.scalar.activation(ctxT[:, 4 * hh:4 * hh + 4, qb * P:qb * P + P],
                                       bank(4).rearrange("p (h q) -> p h q", h=4), ACT.Copy), "ctx_ready")

            exps(0)
            for gi in range(4):
                if gi < 3:
                    exps(gi + 1)
                if gi == 2:
                    root(bank(0)[:, T:2 * T], rst[:, 1, :], 256, "cstat_mm", 2, "cvar_root")
                if gi == 1:
                    gemv_row(3)
                pt_out(gi)
                ctx_out(gi)
            for c in range(2):
                act.wait_ge(S("o_mm"), c + 1)
                a(nc.scalar.activation(y[:, 2 + 2 * c:4 + 2 * c, :],
                                       bank(3 + c).rearrange("p (a t) -> p a t", a=2), ACT.Copy), "y1_ready")
            act.wait_ge(S("pool_mm"), 1)
            for c in range(2):
                a(nc.scalar.activation(y[:, 6 + c, :], bank(5)[:, c * T:c * T + T], ACT.Copy, scale=col("pool_s", c)),
                  "y1_ready")
            act.wait_ge(S("cnorm_ready"), 1)
            for c in range(2):
                a(nc.scalar.activation(y[:, c, :], cacc[:, c, :], ACT.Silu, scale=col("ln_g", c), bias=col("ln_b", c)),
                  "y1_ready")

            gemv_row(4)
            gemv_row(5)
            norm_root(1)
            shifted(h2, 1, mod1, 3)
            for i in range(4):
                act.wait_ge(S("htok_mm"), i + 1)
                t, half = i // 2, i % 2
                a(nc.scalar.activation(htok[:, t, half * 512:half * 512 + 512], bank(2 + i % 2), ACT.Copy), "htok_ready")
            act.wait_ge(S("router_in"), 1)
            a(nc.scalar.activation(rt[:, 72:80], rt[:, 72:80], ACT.Exp, bias=zero[:]), "router_exp")
            act.wait_ge(S("router_in"), 2)
            a(nc.scalar.activation(rt[:, 160:162], rt[:, 160:162], ACT.Exp, bias=zero[:]), "router_exp")

            def act_group(g):
                def gathered(i):
                    act.wait_ge(S("gath_mm"), g * 10 + (i + 2))
                    src = bank(GATH[i % 2])
                    if i in (4, 5):
                        dst, src = gT[:, 2 * (i - 4):2 * (i - 4) + 2, :], src.rearrange("p (j t) -> p j t", j=2)
                    else:
                        j = (0, 1, None, 2, 3)[i // 2]
                        dst = hsel[:, 4 * (i % 2):4 * (i % 2) + 4, j * P:j * P + P]
                        src = src.rearrange("p (k s) -> p k s", k=4)
                    nc.scalar.activation(dst, src, ACT.Copy).then_inc(S("gath_ev"), 1)

                for i in range(2):
                    gathered(i)
                for j in range(4):
                    act.wait_ge(S("up_mm"), g * 8 + (AHEAD + 2 * j + 1))
                    nc.scalar.activation(sil, bank(0), ACT.Silu, bias=zero[:]).then_inc(S("sil_ready"), 1)
                    for i in ((2, 3, 4, 5), (6, 7), (8, 9), ())[j]:
                        gathered(i)
                    act.wait_ge(S("hidT_mm"), g * 4 + (j + 1))
                    nc.scalar.activation(hidT[:], bank(6).rearrange("p (k s) -> p k s", k=KF),
                                         ACT.Copy).then_inc(S("hidT_ready"), 1)
                    for half in range(2):
                        act.wait_ge(S("down_mm"), g * 8 + (AHEAD + 2 * j + half + 1))
                        nc.scalar.activation(yex[:, half * 512:half * 512 + 512], bank(2 + half),
                                             ACT.Copy).then_inc(S("y_ready"), 1)

            act.wait_ge(S("sweeps_ready"), 1)
            n_sw = act.value_load(sweeps[0:1, 0:1], min_val=1, max_val=4)
            with act.Fori(0, 4) as g:
                act_group(g)
            with act.If(n_sw > 1):
                with act.Fori(4, n_sw * 4) as g:
                    act_group(g)

            act.dma_start(gcon[:], gconst_d).then_inc(S("gcon_in"), 16)
            for k in range(KD):
                if k % 2 == 0:
                    act.wait_ge(S("moe_add"), n_sw * 64 + (k // 2 + 1))
                a(nc.scalar.activation(sq_xn[:, k, 0, :], x[:, k, :], ACT.Square, bias=zero[:]), "sqx_ready")
                a(nc.scalar.activation(sq_xn[:, k, 1, :], x[:, k, :], ACT.Square, bias=zero[:], scale=col("nf", k)),
                  "sqx_ready")
            norm_root(2)
            act.wait_ge(S("ms3_in"), 1)
            a(nc.scalar.activation(rcol[:, 2:4], rcol[:, 2:4], ACT.Sqrt, scale=1.0 / D, bias=eps[:]), "root3_ready")
            shifted(g_h, 2, mod2, 0)

            def proj_out(i):
                act.wait_ge(S("proj2_mm"), i + 1)
                kind, n = PROJ2[i]
                func, kw = ACT.Copy, {}
                if kind in "qkv":
                    if i == 0:
                        act.wait_ge(S("raw_pad"), 1)
                    dst = raw[:, i, 3:3 + T]
                elif kind == "z":
                    dst, func, kw = zg[:, n, :], ACT.Silu, {"bias": zero[:]}
                elif kind == "b":
                    dst = scb[:, n, :]
                elif kind == "c":
                    dst = scc[:, n, :]
                else:
                    dst = scp[:, n, 2:2 + T]
                a(nc.scalar.activation(dst, bank(PROJ2_BANK[i])[:, 0:T], func, **kw), "proj2_ev")

            def conv_silu(m):
                for i in range(m, m + 4):
                    act.wait_ge(S("gconv_done"), i + 1)
                    a(nc.scalar.activation(qkv[:, i, :], qkv[:, i, :], ACT.Silu, bias=zero[:]), "qkv_ready")

            act.wait_ge(S("ab_mm"), 1)
            a(nc.scalar.activation(dl[:, 0:16], bank(2)[:, 0:16], ACT.Copy), "ab_ready")
            proj_out(0)
            proj_out(1)
            act.wait_ge(S("sp_in"), 1)
            a(nc.scalar.activation(dl[:, 24:32], dl[:, 24:32], ACT.Exp, bias=zero[:]), "sp_exp")
            a(nc.scalar.activation(dl[:, 40:48], dl[:, 40:48], ACT.Exp, bias=zero[:], scale=-1.0), "sp_exp")
            a(nc.scalar.activation(dl[:, 48:52], col("a_log", 0, 4), ACT.Exp, bias=zero[:]), "sp_exp")
            act.wait_ge(S("sp_exp"), 3)
            a(nc.scalar.activation(dl[:, 24:32], dl[:, 24:32], ACT.Ln, bias=one[:]), "sp_exp")
            for i in range(2, 8):
                proj_out(i)
            act.wait_ge(S("gcol_ready"), 1)
            a(nc.scalar.activation(dl[:, 80:96], dl[:, 64:80], ACT.Exp, bias=zero[:]), "gexp_ready")
            for t in range(TT):
                act.wait_ge(S("unit_mm"), GROW + t + 1)
                a(nc.scalar.activation(expg[:, 4 * t:4 * t + 4, :], bank(2 + t).rearrange("p (h c) -> p h c", h=4),
                                       ACT.Exp, bias=zero[:]), "expg_ready")
            for t in range(TT):
                act.wait_ge(S("dec_arg"), t + 1)
                a(nc.scalar.activation(dec[:, 4 * t:4 * t + 4, :], dec[:, 4 * t:4 * t + 4, :], ACT.Exp,
                                       bias=zero[:]), "dec_ready")
            conv_silu(0)
            proj_out(8)
            conv_silu(4)
            proj_out(9)
            act.wait_ge(S("qk_mm"), 1)
            a(nc.scalar.activation(dl[:, 104:120], bank(4)[:, 0:16], ACT.Sqrt, bias=eps[:]), "qk_root")
            proj_out(10)
            proj_out(11)
            conv_silu(8)
            for i in range(12, 16):
                proj_out(i)
            for t in range(TT):
                act.wait_ge(S("merge0_mm"), t + 1)
                a(nc.scalar.activation(tm[:, 4 * t:4 * t + 4, :], bank(4 + t).rearrange("p (h c) -> p h c", h=4),
                                       ACT.Copy), "tm0_ready")
            for lv in range(1, LEVELS):
                for t in range(TT):
                    act.wait_ge(S("merge_p_mm"), TT * (lv - 1) + t + 1)
                    a(nc.scalar.activation(pm[:, 4 * t:4 * t + 4, :], bank(t).rearrange("p (h c) -> p h c", h=4),
                                           ACT.Copy), "pm_ready")
            for t in range(TT):
                act.wait_ge(S("wt_mm"), t + 1)
                a(nc.scalar.activation(wtn[:, 4 * t:4 * t + 4, :], bank(4 + t).rearrange("p (h c) -> p h c", h=4),
                                       ACT.Copy), "wt_ready")
            proj_out(16)
            for n in range(NCH):
                q = slice(64 * (n % 2), 64 * (n % 2) + 64)
                act.wait_ge(S("vnew_mm"), n + 1)
                if n >= 2:
                    act.wait_ge(S("out_mm"), n - 1)
                    act.wait_ge(S("state_mm"), n - 1)
                a(nc.scalar.activation(vnew[q], bank(n % 2)[q].rearrange("p (h c) -> p h c", h=4), ACT.Copy), "vnew_ready")
                proj_out(17 + 2 * n)
                act.wait_ge(S("out_mm"), n + 1)
                a(nc.scalar.activation(o_t[:, :, 64 * n:64 * n + 64],
                                       bank(2 + n % 2)[:, 0:256].rearrange("p (h c) -> p h c", h=4), ACT.Copy), "o_ready")
                proj_out(18 + 2 * n)
            proj_out(25)
            act.wait_ge(S("o_ms"), 1)
            a(nc.scalar.activation(dl[:, 128:136], dl[:, 128:136], ACT.Sqrt, bias=eps[:], scale=1.0 / 128), "o_root")
            proj_out(26)
            proj_out(27)
            norm_root(3)
            shifted(f_h, 3, mod2, 3)
            for f in range(NFF):
                act.wait_ge(S("ff_gate_mm"), f + 1)
                if f >= 4:
                    act.wait_ge(S("hff_ready"), f - 3)
                a(nc.scalar.activation(sff[:, (f // 2) % 2, f % 2, :], bank(2 * (f % 2) + 2)[:, 0:T], ACT.Silu,
                                       bias=zero[:]), "sff_ready")
            norm_root(4)

        @block.vector
        def _(dve):
            def v(ins, name="dve_step"):
                ins.then_inc(S(name), 1)
                count[name] += 1
                dve.wait_ge(S(name), count[name])

            tt, stt, ts = nc.vector.tensor_tensor, nc.vector.scalar_tensor_tensor, nc.vector.tensor_scalar

            nc.vector.memset(zero[:], 0.0).then_inc(S("dve_step"), 1)
            nc.vector.memset(one[:], 1.0).then_inc(S("dve_step"), 1)
            nc.vector.memset(eps[:], EPS).then_inc(S("dve_step"), 1)
            nc.vector.memset(ones[:], 1.0).then_inc(S("dve_step"), 1)
            nc.vector.memset(upad[:, :, 0:CONV_W - 1], 0.0).then_inc(S("dve_step"), 1)
            count["dve_step"] += 5
            dve.wait_ge(S("dve_step"), 5)
            v(nc.vector.memset(score[:], 0.0), "init")

            def d(ins, name):
                ins.then_inc(S(name), 1)
                count[name] += 1

            def add_square(n, k):
                total, sq = xsq[n][:, 0, :], xsq[n][:, 2, :]
                if k == 0:
                    v(tt(total, x[:, k, :], x[:, k, :], ALU.mult))
                else:
                    v(tt(sq, x[:, k, :], x[:, k, :], ALU.mult))
                    v(tt(total, total, sq, ALU.add), "sq_ready" if k == KD - 1 else "dve_step")

            def inverse(n):
                dve.wait_ge(S("root_ready"), 2 * n + 2)
                v(nc.vector.reciprocal(rcol[:, 0:2], rcol[:, 0:2]), "rcol_ready")

            def scaled(dst, n, gains, name="scaled"):
                dve.wait_ge(S("rrow_mm"), n + 1)
                for k in range(KD):
                    d(stt(dst[:, k, :], x[:, k, :], gains[:, k:k + 1], bank(0)[:, 0:T], ALU.mult, ALU.mult), name)

            def gemv_col(r):
                mod, bias, rr = (mod1, "mod_b", r) if r < 3 else (mod2, "ada_b", r - 3)
                dve.wait_ge(S("modT_mm"), r + 1)
                for j in range(4):
                    o = slice(16 * rr + 4 * j, 16 * rr + 4 * j + 4)
                    v(tt(mod[:, o], bank(2).rearrange("p (s q) -> p s q", s=4)[:, :, 32 * j],
                         col(bias, 16 * rr + 4 * j, 4), ALU.add), "mod_ready")
                if rr != 1:
                    n = 2 * (r // 3) + rr // 2
                    sc = mod[:, 8:16] if rr == 0 else mod[:, 32:40]
                    v(stt(gain[:, n, :], sc, 1.0, col(("n1", "n2", "n1b", "n2b")[n], 0, 8), ALU.add, ALU.mult))

            dve.wait_ge(S("x_in"), 16)
            for k in range(KD):
                add_square(0, k)
            inverse(0)
            dve.wait_ge(S("small_in"), 32)
            gemv_col(0)
            scaled(h, 0, gain[:, 0, :])
            dve.wait_ge(S("proj_ev"), AFTER["g", 1])
            v(tt(upad[:, :, CONV_W - 1:UPW], aval, cgate, ALU.mult), "u_ready")

            def conv(lo, hi):
                for j in range(lo, hi):
                    for c in range(2):
                        src, k = upad[:, c, j:j + T], col("conv_k", c * CONV_W + j)
                        if j == 0:
                            d(ts(cacc[:, c, :], src, k, col("conv_b", c), ALU.mult, ALU.add), f"conv_step{c}")
                        else:
                            dve.wait_ge(S(f"conv_step{c}"), j)
                            d(stt(cacc[:, c, :], src, k, cacc[:, c, :], ALU.mult, ALU.add), f"conv_step{c}")

            conv(0, 24)
            dve.wait_ge(S("proj_ev"), AFTER["lat", 2])
            v(tt(rel[:, 0:2, :], cq, cq, ALU.mult))
            v(tt(rel[:, 2, :], ckv, ckv, ALU.mult), "lat_sq")
            conv(24, CONV_W)
            dve.wait_ge(S("lat_root"), 2)
            v(nc.vector.reciprocal(rst[:, 0, :], rst[:, 0, :]))
            v(nc.vector.reciprocal(rst[:, 1, :], rst[:, 1, :]))
            for c in range(2):
                v(stt(cq[:, c, :], cq[:, c, :], col("q_g", c), rst[:, 0, :], ALU.mult, ALU.mult), "lat_ready")
            v(stt(ckv, ckv, col("kv_g"), rst[:, 1, :], ALU.mult, ALU.mult), "lat_ready")
            gemv_col(1)

            def index_scores(qb):
                w = P if qb == 0 else T
                for n in range(8 * qb, 8 * qb + 8):
                    dve.wait_ge(S("proj_ev"), AFTER["ix", n])
                    v(stt(score[:, qb, 0:w], rel[:, n % 2, 0:w], wi[:, qb, n % 8:n % 8 + 1], score[:, qb, 0:w],
                          ALU.mult, ALU.add), "idx_acc")

            def top(qb):
                sc = score[:, qb, 0:P if qb == 0 else T]
                m = aconst[:, qb, 0:P if qb == 0 else T]
                v(stt(sc, sc, IDX_SCALE, m, ALU.mult, ALU.add))
                for _ in range(TOPK // 8):
                    v(nc.vector.max(top8, sc))
                    v(nc.vector.match_replace(sc, top8, sc, TAKEN))
                v(ts(m, sc, -2.0e38, MASKED, ALU.is_gt, ALU.mult))

            def masked(gi):
                qb, w, buf = gi // 2, P if gi < 2 else T, pbuf[gi % 2]
                dve.wait_ge(S("lg_mm"), gi + 1)
                if gi >= 2:
                    dve.wait_ge(S("pT_mm"), (1, 2)[gi - 2])
                v(stt(buf[:, :, 0:w], psum[3][:].rearrange("p a (b s) -> p (a b) s", b=2)[:, :, 0:w], ATT_SCALE,
                      selb[:, qb, 0:w].unsqueeze(1).to_broadcast([P, 4, w]), ALU.mult, ALU.add), "lg_used")
                v(nc.vector.tensor_reduce(mx[gi % 2], buf[:, :, 0:w], AX, ALU.max))
                v(nc.vector.tensor_scalar_mul(mx[gi % 2], mx[gi % 2], -1.0), "max_ready")

            def normalized(gi):
                w, buf = P if gi < 2 else T, pbuf[gi % 2]
                dve.wait_ge(S("exp_done"), 4 * (gi + 1))
                v(nc.vector.reciprocal(rsum, ssum[:, 4 * (gi % 2):4 * (gi % 2) + 4]))
                v(tt(buf[:, :, 0:w], buf[:, :, 0:w], rsum.unsqueeze(2).to_broadcast([P, 4, w]), ALU.mult), "p_ready")

            index_scores(0)
            dve.wait_ge(S("att_in"), 32)
            top(0)
            index_scores(1)
            masked(0)
            masked(1)
            dve.wait_ge(S("cstat_mm"), 1)
            for c in range(2):
                v(stt(cacc[:, c, :], bank(0)[:, 0:T], -1.0 / 256, cacc[:, c, :], ALU.mult, ALU.add))
            normalized(0)
            top(1)
            normalized(1)
            masked(2)
            v(tt(csq, cacc, cacc, ALU.mult), "csq_ready")
            gemv_col(2)
            masked(3)
            normalized(2)
            normalized(3)
            dve.wait_ge(S("cvar_root"), 1)
            v(nc.vector.reciprocal(rst[:, 1, :], rst[:, 1, :]))
            v(tt(cacc, cacc, rst[:, 1, :].unsqueeze(1).to_broadcast([P, 2, T]), ALU.mult), "cnorm_ready")
            gemv_col(3)

            def residual(n, gate, after=lambda m: None):
                for m in range(KD):
                    dve.wait_ge(S("res_mm"), KD * n + m + 1)
                    v(stt(x[:, m, :], bank(6 + m % 2)[:, 0:T], gate[:, m:m + 1], x[:, m, :], ALU.mult, ALU.add),
                      "res_used")
                    add_square((1, 3, 4)[n], m)
                    after(m)

            residual(0, mod1[:, 16:24], lambda m: gemv_col(4) if m == 4 else None)

            inverse(1)
            scaled(h2, 1, gain[:, 1, :])
            gemv_col(5)
            lg = rt[:, 0:72].rearrange("p (t e) -> p t e", t=TT)
            glog, elog = lg[:, :, 0:4], lg[:, :, 4:36].rearrange("p t (g e) -> p t g e", g=4)
            gex = rt[:, 72:80].rearrange("p (t g) -> p t g", t=TT)
            goh = rt[:, 80:88].rearrange("p (t g) -> p t g", t=TT)
            gmax, gp, pri = rt[:, 88:90], rt[:, 90:92], rt[:, 92:94]
            esel = rt[:, 96:112].rearrange("p (t e) -> p t e", t=TT)
            oh = [rt[:, 112 + 16 * i:128 + 16 * i].rearrange("p (t e) -> p t e", t=TT) for i in range(2)]
            emax = [rt[:, 144:146], rt[:, 146:148]]
            gap, den, wg = rt[:, 160:162], rt[:, 162:164], [rt[:, 164:166], rt[:, 166:168]]
            tmp8 = rt[:, 176:192].rearrange("p (t e) -> p t e", t=TT)
            asg = rt[:, 192:256].rearrange("p (t g e) -> p t g e", t=TT, g=4)
            gat = rt[:, 256:320].rearrange("p (t g e) -> p t g e", t=TT, g=4)
            tmp32 = rt[:, 320:384].rearrange("p (t g e) -> p t g e", t=TT, g=4)
            cnt = rt[:, 384:416]
            acc1 = rt[:, 416:424]

            def wide(a, n):
                return a.unsqueeze(2).to_broadcast([P, TT, n])

            def first_max(src, top, out_oh, n):
                v(nc.vector.tensor_reduce(top, src, AX, ALU.max))
                v(tt(out_oh, src, wide(top, n), ALU.is_equal))
                v(tt(out_oh, out_oh, cst("prio")[:, 0:n].unsqueeze(1).to_broadcast([P, TT, n]), ALU.mult))
                v(nc.vector.tensor_reduce(pri, out_oh, AX, ALU.max))
                v(tt(out_oh, out_oh, wide(pri, n), ALU.is_equal))

            dve.wait_ge(S("router_mm"), 1)
            v(tt(lg, bank(1)[:, 0:72].rearrange("p (t e) -> p t e", t=TT),
                 col("rbias", 0, 36).unsqueeze(1).to_broadcast([P, TT, 36]), ALU.add))
            first_max(glog, gmax, goh, 4)
            v(tt(gex, glog, wide(gmax, 4), ALU.subtract), "router_in")
            v(tt(tmp32, elog, goh.unsqueeze(3).to_broadcast([P, TT, 4, 8]), ALU.mult))
            v(tt(esel, tmp32[:, :, 0, :], tmp32[:, :, 1, :], ALU.add))
            v(tt(esel, esel, tmp32[:, :, 2, :], ALU.add))
            v(tt(esel, esel, tmp32[:, :, 3, :], ALU.add))
            first_max(esel, emax[0], oh[0], 8)
            v(stt(tmp8, oh[0], MASKED, esel, ALU.mult, ALU.add))
            first_max(tmp8, emax[1], oh[1], 8)
            v(tt(gap, emax[1], emax[0], ALU.subtract), "router_in")
            v(tt(tmp8, oh[0], oh[1], ALU.add))
            v(tt(asg, goh.unsqueeze(3).to_broadcast([P, TT, 4, 8]), tmp8.unsqueeze(2).to_broadcast([P, TT, 4, 8]),
                 ALU.mult), "asg_ready")
            dve.wait_ge(S("router_exp"), 1)
            v(nc.vector.tensor_reduce(gp, gex, AX, ALU.add))
            v(nc.vector.reciprocal(gp, gp))
            dve.wait_ge(S("router_exp"), 2)
            v(nc.vector.tensor_scalar_add(den, gap, 1.0))
            v(nc.vector.reciprocal(den, den))
            v(tt(wg[0], den, gp, ALU.mult))
            v(tt(wg[1], wg[0], gap, ALU.mult))
            v(tt(oh[0], oh[0], wide(wg[0], 8), ALU.mult))
            v(tt(oh[1], oh[1], wide(wg[1], 8), ALU.mult))
            v(tt(oh[0], oh[0], oh[1], ALU.add))
            v(tt(gat, goh.unsqueeze(3).to_broadcast([P, TT, 4, 8]), oh[0].unsqueeze(2).to_broadcast([P, TT, 4, 8]),
                 ALU.mult))
            dve.wait_ge(S("rank_mm"), 1)
            a2, g2 = rt[:, 192:256].rearrange("p (t e) -> p t e", t=TT), rt[:, 256:320].rearrange("p (t e) -> p t e", t=TT)
            rk = rt[:, 320:384].rearrange("p (t e) -> p t e", t=TT)
            v(stt(rk, bank(5)[:, 0:64].rearrange("p (t e) -> p t e", t=TT), 1.0, a2, ALU.add, ALU.mult))
            v(nc.vector.tensor_copy(gate_s.rearrange("p t (s e) -> p t s e", s=4),
                                    g2.unsqueeze(2).to_broadcast([P, TT, 4, E])))
            for s in range(4):
                v(nc.vector.tensor_scalar_add(rank_s[:, :, E * s:E * s + E], rk, -1.0 - CAP * s))
            v(nc.vector.reduce_max(acc1[:, 0:1], bank(5)[:, 64:96], AX))
            for s in range(1, 4):
                v(ts(acc1[:, s:s + 1], acc1[:, 0:1], CAP * s + 0.5, None, ALU.is_gt))
            v(stt(acc1[:, 1:2], acc1[:, 1:2], 1.0, acc1[:, 2:3], ALU.add, ALU.add))
            v(tt(acc1[:, 1:2], acc1[:, 1:2], acc1[:, 3:4], ALU.add))
            v(nc.vector.tensor_copy(sweeps[:], acc1[:, 1:2]), "sweeps_ready")
            dve.sem_inc(S("moe_add"), 4)

            def dve_group(g):
                dve.wait_ge(S("gath_mm"), g * 10 + 1)
                for j in range(4):
                    for t in range(TT):
                        nc.vector.tensor_tensor(
                            s_oh[:, t, 2 * j * CAP:(2 * j + 2) * CAP].rearrange("p (e s) -> p e s", e=2),
                            rank_s[:, t, bass.ds(g * 8 + 2 * j, 2)].unsqueeze(2).to_broadcast([P, 2, CAP]),
                            cst("iota").unsqueeze(1).to_broadcast([P, 2, CAP]), ALU.is_equal).then_inc(S("onehot"), 1)
                dve.wait_ge(S("onehot"), g * 8 + 8)
                for t in range(TT):
                    nc.vector.tensor_tensor(
                        s_gt[:, t, :].rearrange("p (e s) -> p e s", e=EG),
                        s_oh[:, t, :].rearrange("p (e s) -> p e s", e=EG),
                        gate_s[:, t, bass.ds(g * 8, 8)].unsqueeze(2).to_broadcast([P, EG, CAP]),
                        ALU.mult).then_inc(S("gated"), 1)
                for j in range(4):
                    dve.wait_ge(S("up_mm"), g * 8 + (AHEAD + 2 * j + 2))
                    dve.wait_ge(S("sil_ready"), g * 4 + (j + 1))
                    nc.vector.tensor_tensor(hid, sil, bank(1), ALU.mult).then_inc(S("hid_ready"), 1)
                    for c in range(4):
                        dve.wait_ge(S("comb_mm"), g * 16 + (4 * j + c + 1))
                        dve.wait_ge(S("moe_add"), g * 16 + (4 * j + c + 4))
                        for q in range(2):
                            m = 2 * c + q
                            ins = nc.vector.scalar_tensor_tensor(
                                x[:, m, :], bank(4 + c % 2)[:, q * T:q * T + T], mod1[:, 40 + m:41 + m], x[:, m, :],
                                ALU.mult, ALU.add)
                        ins.then_inc(S("moe_add"), 1)

            dve.wait_ge(S("mod_ready"), 24)
            n_sw = dve.value_load(sweeps[0:1, 0:1], min_val=1, max_val=4)
            with dve.Fori(0, 4) as g:
                dve_group(g)
            with dve.If(n_sw > 1):
                with dve.Fori(4, n_sw * 4) as g:
                    dve_group(g)
            for k in range(1, KD):
                dve.wait_ge(S("sqx_ready"), 2 * k + 2)
                so_far = sq_xn[:, 0, :, :] if k == 1 else xsq[2][:, 0:2, :]
                v(tt(xsq[2][:, 0:2, :], so_far, sq_xn[:, k, :, :], ALU.add), "sq_ready" if k == KD - 1 else "dve_step")

            dve.wait_ge(S("root_ready"), 6)
            v(nc.vector.reciprocal(rcol[:, 0:2], rcol[:, 0:2]))
            v(tt(rcol[:, 4:6], rcol[:, 0:2], rcol[:, 0:2], ALU.mult))
            dve.wait_ge(S("msn_mm"), 1)
            for t in range(TT):
                v(tt(rcol[:, 2 + t:3 + t], rcol[:, 4 + t:5 + t], bank(1 + t)[:, 0:1], ALU.mult),
                  "ms3_in" if t else "dve_step")
            v(tt(gnf, gain[:, 2, :], col("nf", 0, 8), ALU.mult))
            dve.wait_ge(S("root3_ready"), 1)
            v(nc.vector.reciprocal(rcol[:, 2:4], rcol[:, 2:4]))
            v(tt(rcol[:, 2:4], rcol[:, 2:4], rcol[:, 0:2], ALU.mult), "rcol_ready")
            scaled(g_h, 2, gnf)
            for k in range(KD):
                d(stt(x[:, k, :], x[:, k, :], col("nf", k), bank(0)[:, T:2 * T], ALU.mult, ALU.mult), "x_normed")
            v(nc.vector.memset(raw[:, :, 0:3], 0.0), "raw_pad")
            v(nc.vector.memset(scp[:, :, 0:2], 0.0))
            def qkv_conv(m):
                dve.wait_ge(S("proj2_ev"), m + 1)
                for j in range(4):
                    src, k = raw[:, m, j:j + T], col("gconv", 4 * m + j)
                    if j == 0:
                        v(nc.vector.tensor_scalar_mul(qkv[:, m, :], src, k))
                    else:
                        v(stt(qkv[:, m, :], src, k, qkv[:, m, :], ALU.mult, ALU.add),
                          "gconv_done" if j == 3 else "dve_step")

            def short_conv(i):
                dve.wait_ge(S("proj2_ev"), PROJ2.index(("h", i)) + 1)
                v(tt(scp[:, i, 2:2 + T], scp[:, i, 2:2 + T], scc[:, i, :], ALU.mult))
                o = g_y[:, 4 + i, :]
                v(nc.vector.tensor_scalar_mul(o, scp[:, i, 0:T], col("sconv", 3 * i)))
                v(stt(o, scp[:, i, 1:1 + T], col("sconv", 3 * i + 1), o, ALU.mult, ALU.add))
                v(stt(o, scp[:, i, 2:2 + T], col("sconv", 3 * i + 2), o, ALU.mult, ALU.add))
                v(tt(o, o, scb[:, i, :], ALU.mult), "y2_ready")

            ab = dl[:, 0:16].rearrange("p (t c) -> p t c", t=TT)
            ap, sp_, am = [dl[:, o:o + 8].rearrange("p (t h) -> p t h", t=TT) for o in (16, 24, 32)]
            be = dl[:, 40:48].rearrange("p (t h) -> p t h", t=TT)
            na = dl[:, 48:52]
            gg = dl[:, 56:64].rearrange("p (t h) -> p t h", t=TT)
            dve.wait_ge(S("ab_ready"), 1)
            v(tt(ap, ab[:, :, 0:4], col("dt", 0, 4).unsqueeze(1).to_broadcast([P, TT, 4]), ALU.add))
            v(nc.vector.tensor_scalar_mul(sp_, ap, -1.0))
            v(tt(sp_, sp_, ap, ALU.min))
            v(nc.vector.tensor_scalar_max(am, ap, 0.0))
            v(nc.vector.tensor_copy(be, ab[:, :, 4:8]), "sp_in")
            qkv_conv(0)
            dve.wait_ge(S("sp_exp"), 4)
            v(tt(sp_, sp_, am, ALU.add))
            v(nc.vector.tensor_scalar_mul(na, na, -1.0))
            v(tt(gg, sp_, na.unsqueeze(1).to_broadcast([P, TT, 4]), ALU.mult), "g_ready")
            v(nc.vector.tensor_scalar_add(be, be, 1.0))
            v(nc.vector.reciprocal(be, be))
            qkv_conv(1)
            dve.wait_ge(S("gcum_mm"), 1)
            G, GL = dl[:, 64:72], dl[:, 72:80]
            v(nc.vector.tensor_copy(G, bank(6)[:, 0:8]))
            v(tt(GL, bank(6)[:, 8:16], G, ALU.subtract), "gcol_ready")
            eG, eGL, beta = dl[:, 80:88], dl[:, 88:96], dl[:, 40:48]
            nbe, rq, rk, brk = dl[:, 96:104], dl[:, 104:112], dl[:, 112:120], dl[:, 120:128]
            for m in range(2, 8):
                qkv_conv(m)
            for t in range(TT):
                dve.wait_ge(S("unit_mm"), GROW + t + 1)
                dve.wait_ge(S("expg_ready"), t + 1)
                for hd in range(GH):
                    u = 4 * t + hd
                    v(stt(dec[:, u, :], bank(2 + t)[:, hd * P:hd * P + P], G[:, u:u + 1], mask_c, ALU.subtract, ALU.add),
                      "dec_arg" if hd == 3 else "dve_step")
            for i in range(2):
                dve.wait_ge(S("qkv_ready"), 4 * i + 4)
                k = slice(4 * i, 4 * i + 4)
                v(tt(sq8[:, k, :], qkv[:, k, :], qkv[:, k, :], ALU.mult), "sq8_ready")
            qkv_conv(8)
            qkv_conv(9)
            dve.wait_ge(S("qk_root"), 1)
            v(nc.vector.reciprocal(dl[:, 104:120], dl[:, 104:120]))
            v(nc.vector.tensor_scalar_mul(rq, rq, float(128 ** -0.5)))
            v(tt(brk, beta, rk, ALU.mult), "brk_ready")
            dve.wait_ge(S("gexp_ready"), 1)
            v(tt(nbe, brk, eG, ALU.mult))
            v(nc.vector.tensor_scalar_mul(nbe, nbe, -1.0))
            v(tt(eGL, eGL, rk, ALU.mult))
            for t in range(TT):
                us = slice(4 * t, 4 * t + 4)
                dve.wait_ge(S("dec_ready"), t + 1)
                v(tt(dec[:, us, :], dec[:, us, :], rk[:, us].unsqueeze(2).to_broadcast([P, 4, P]), ALU.mult))
            for t in range(TT):
                dve.wait_ge(S("unit_mm"), KTOK + t + 1)
                for hd in range(GH):
                    u = 4 * t + hd
                    src = bank(6 + t)[:, hd * P:hd * P + P]
                    v(nc.vector.tensor_scalar_mul(kbe[:, u, :], src, nbe[:, u:u + 1]))
                    v(nc.vector.tensor_scalar_mul(kdec[:, u, :], src, eGL[:, u:u + 1]), "k_used")
            for t in range(TT):
                us = slice(4 * t, 4 * t + 4)
                dve.wait_ge(S("unit_mm"), KK + t + 1)
                v(tt(lt[:, us, :], bank(4 + t).rearrange("p (h c) -> p h c", h=4), dec[:, us, :], ALU.mult), "kk_used")
            qkv_conv(10)
            qkv_conv(11)
            for t in range(TT):
                us = slice(4 * t, 4 * t + 4)
                dve.wait_ge(S("unit_mm"), BROW + t + 1)
                v(tt(lt[:, us, :], lt[:, us, :], bank(2 + t).rearrange("p (h c) -> p h c", h=4), ALU.mult),
                  "lt_ready" if t == 1 else "dve_step")
            for t in range(TT):
                us = slice(4 * t, 4 * t + 4)
                v(tt(ttm[:, us, :], lt[:, us, :], gcon[:, 3, :].unsqueeze(1).to_broadcast([P, 4, P]), ALU.mult))
                v(tt(ttm[:, us, :], ident.unsqueeze(1).to_broadcast([P, 4, P]), ttm[:, us, :], ALU.subtract), "ttm_ready")
            for t in range(TT):
                dve.wait_ge(S("unit_mm"), VTOK + t + 1)
                for hd in range(GH):
                    u = 4 * t + hd
                    v(nc.vector.tensor_scalar_mul(vb[:, u, :], bank(6 + t)[:, hd * P:hd * P + P], beta[:, u:u + 1]),
                      "v_used")
            for t in range(TT):
                us = slice(4 * t, 4 * t + 4)
                dve.wait_ge(S("unit_mm"), KQ + t + 1)
                v(tt(attn_t[:, us, :], bank(4 + t).rearrange("p (h c) -> p h c", h=4), dec[:, us, :], ALU.mult),
                  "attn_ready")
            for lv in range(1, LEVELS):
                for t in range(TT):
                    us = slice(4 * t, 4 * t + 4)
                    if lv == 1:
                        dve.wait_ge(S("tm0_ready"), t + 1)
                    if lv < LEVELS - 1:
                        dve.wait_ge(S("merge_t_mm"), TT * (lv - 1) + t + 1)
                        v(tt(tm[:, us, :], tm[:, us, :], bank(4 + t).rearrange("p (h c) -> p h c", h=4), ALU.subtract),
                          "tm_ready")
                    dve.wait_ge(S("merge_tt_mm"), TT * (lv - 1) + t + 1)
                    v(tt(ttm[:, us, :], ttm[:, us, :], bank(2 + t).rearrange("p (h c) -> p h c", h=4), ALU.subtract),
                      "ttm_ready")
            for t in range(TT):
                for hd in range(GH):
                    v(tt(qkv[:, hd, t * P:t * P + P], qkv[:, hd, t * P:t * P + P], expg[:, 4 * t + hd, :], ALU.mult),
                      "qdec_ready")
            for n in range(NCH - 1):
                dve.wait_ge(S("state_mm"), n + 1)
                dve.wait_ge(S("out_mm"), n + 1)
                for hd in range(GH):
                    src = bank(6 + n % 2)[:, hd * P:hd * P + P]
                    if n == 0:
                        v(nc.vector.tensor_copy(state[:, hd, :], src), "state_ready")
                    else:
                        u = 4 * (n // 2) + hd
                        last = 64 * (n % 2) + 63
                        v(stt(state[:, hd, :], state[:, hd, :], expg[:, u, last:last + 1], src, ALU.mult, ALU.add),
                          "state_ready")
                if n > 0:
                    short_conv(n - 1)
            dve.wait_ge(S("o_ready"), NCH)
            v(tt(o_sq, o_t, o_t, ALU.mult), "osq_ready")
            short_conv(2)
            fac = dl[:, 128:136]
            dve.wait_ge(S("osum_mm"), 1)
            v(tt(fac, bank(7)[:, 0:8], rq, ALU.mult))
            v(tt(fac, fac, rq, ALU.mult), "o_ms")
            dve.wait_ge(S("o_root"), 1)
            v(nc.vector.reciprocal(fac, fac))
            v(tt(fac, fac, rq, ALU.mult), "fac_ready")
            dve.wait_ge(S("fac_mm"), 1)
            for i in range(2):
                k = slice(2 * i, 2 * i + 2)
                v(stt(o_t[:, k, :], o_t[:, k, :], col("gnorm"), bank(2 + i).rearrange("p (a t) -> p a t", a=2),
                      ALU.mult, ALU.mult))
                v(tt(g_y[:, k, :], o_t[:, k, :], zg[:, k, :], ALU.mult), "y2_ready")
            dve.sem_inc(S("delta_done"), 1)
            short_conv(3)
            dve.wait_ge(S("x_normed"), KD)
            residual(1, mod2[:, 16:24])
            inverse(3)
            scaled(f_h, 3, gain[:, 3, :])
            for f in range(NFF):
                dve.wait_ge(S("sff_ready"), f + 1)
                dve.wait_ge(S("ff_up_mm"), f + 1)
                v(tt(hff[:, f, :], sff[:, (f // 2) % 2, f % 2, :], bank(2 * (f % 2) + 3)[:, 0:T], ALU.mult), "hff_ready")
            residual(2, mod2[:, 40:48])
            inverse(4)
            scaled(f_h, 4, col("nfb", 0, 8), "out_ready")

        @block.tensor
        def _(pe):
            mm = nc.tensor.matmul

            def sums(n):
                pe.wait_ge(S("sq_ready"), n + 1)
                for t in range(TT):
                    last = mm(bank(STAT[t])[:, 0:1], xsq[n][:, 0, t * P:t * P + P], ones[:, 0:1], start=True, stop=True)
                last.then_inc(S("ms_mm"), 1)

            def spread(cols_at, to, inc=True):
                for t in range(TT):
                    last = mm(bank(0)[:, to + t * P:to + t * P + P], rcol[:, cols_at + t:cols_at + t + 1].to_broadcast([P, P]),
                              ident, start=True, stop=True)
                if inc:
                    last.then_inc(S("rrow_mm"), 1)

            def gemv(r):
                c = cact[:, r // 3, :]
                pe.wait_ge(S("cact_ready"), 2)
                if r > 0:
                    pe.wait_ge(S("modrow_ready"), r)
                for k in range(KD):
                    n = PASS[r][k // 4]
                    s = PRE_SLOT[n]
                    if k % 4 == 0:
                        pe.wait_ge(S(f"loaded{s}"), landed(n))
                    w = ring[:, s, :].rearrange("p (k n) -> p k n", k=4)[:, k % 4, :]
                    for j in range(4):
                        last = mm(bank(1)[32 * j:32 * j + 32, :], c[:, k:k + 1].to_broadcast([P, 32]),
                                  w[:, 512 * j:512 * j + 512], start=k == 0, stop=k == KD - 1)
                last.then_inc(S("gemv_mm"), 1)

            def gemv_t(r):
                pe.wait_ge(S("modrow_ready"), r + 1)
                if r > 0:
                    pe.wait_ge(S("mod_ready"), 4 * r)
                for s in range(4):
                    last = nc.tensor.transpose(bank(2)[:, s * P:s * P + P], modrow[r][:, s * P:s * P + P], ident)
                last.then_inc(S("modT_mm"), 1)

            sums(0)
            gemv(0)
            pe.wait_ge(S("small_in"), 32)
            gemv_t(0)
            pe.wait_ge(S("rcol_ready"), 1)
            spread(0, 0)

            WB = 776
            def z_chunk(i, s, width, at):
                w = ring[:, s, 0:KD * width].rearrange("p (k n) -> p k n", k=KD)
                for k in range(KD):
                    if i == 0:
                        pe.wait_ge(S("h_ready"), k + 1)
                    last = mm(bank(3 + i % 2)[:, 0:T], w[:, k, at:at + P], h[:, k, :], start=k == 0, stop=k == KD - 1)
                return last

            def step(i):
                kind, n = SERIES[i]
                if i >= 2:
                    pe.wait_ge(S("proj_ev"), i - 1)
                b = bank(3 + i % 2)
                if kind in ("a", "g", "p"):
                    last = z_chunk(i, 2, WB, P * ({"a": 0, "g": 2, "p": 4}[kind] + n))
                elif kind in ("lat", "ki", "qi"):
                    last = z_chunk(i, 3, 1024, P * ({"ki": 0, "qi": 1, "lat": 5}[kind] + n))
                elif kind == "wi":
                    wb = ring[:, 2, 0:KD * WB].rearrange("p (k n) -> p k n", k=KD)
                    for t in range(TT):
                        for k in range(KD):
                            last = mm(b[:, 8 * t:8 * t + 8], h[:, k, t * P:t * P + P], wb[:, k, 768:776],
                                      start=k == 0, stop=k == KD - 1)
                elif kind == "ix":
                    qb, hd = n // 8, n % 8
                    w, q = P if qb == 0 else T, slice(64 * (hd % 2), 64 * (hd % 2) + 64)
                    pe.wait_ge(S("proj_ev"), AFTER["qi", hd // 2])
                    last = mm(b[:, 0:w], qi[q, hd // 2, qb * P:qb * P + P], ki[q, 0:w], start=True, stop=True)
                elif kind == "q":
                    pe.wait_ge(S("lat_ready"), 3)
                    for k in range(2):
                        last = mm(b[:, 0:T], uq[:, k, n * P:n * P + P], cq[:, k, :], start=k == 0, stop=k == 1)
                elif kind == "qa":
                    q = slice(64 * (n % 2), 64 * (n % 2) + 64)
                    pe.wait_ge(S("proj_ev"), AFTER["q", n // 2])
                    last = mm(b[:, 0:T], uk[q, n // 2, :], qT[q, n // 2, :], start=True, stop=True)
                else:
                    for t in range(TT):
                        last = nc.tensor.transpose(b[:, t * P:t * P + P], ckv[:, t * P:t * P + P], ident)
                last.then_inc(S("proj_mm"), 1)

            pe.wait_ge(S("loaded2"), 16)
            for i in range(AFTER["wi", 0]):
                step(i)
            pe.wait_ge(S("loaded3"), 16)
            for i in range(AFTER["wi", 0], AFTER["ki", 0]):
                step(i)
            pe.wait_ge(S("lat_sq"), 1)
            for c in range(2):
                mm(bank(0)[:, 0:T], ones[:], rel[:, c, :], start=c == 0, stop=c == 1)
            mm(bank(0)[:, T:2 * T], ones[:], rel[:, 2, :], start=True, stop=True).then_inc(S("lat_mm"), 1)
            gemv(1)
            for i in range(AFTER["ki", 0], AFTER["qi", 0]):
                step(i)
            gemv_t(1)
            for i in range(AFTER["qi", 0], AFTER["qi", 3]):
                step(i)
            pe.wait_ge(S("att_in"), 32)
            for i in range(AFTER["qi", 3], AFTER["ct", 0]):
                step(i)

            def logits(gi):
                qb, hh, w = gi // 2, gi % 2, P if gi < 2 else T
                pe.wait_ge(S("proj_ev"), AFTER["qa", 7])
                if gi > 0:
                    pe.wait_ge(S("lg_used"), gi)
                for j in range(4):
                    last = mm(psum[3][:, j // 2, (j % 2) * T:(j % 2) * T + w],
                              qabs[:, 4 * hh + j, qb * P:qb * P + P], ckv[:, 0:w], start=True, stop=True)
                last.then_inc(S("lg_mm"), 1)

            def context(gi):
                nst = 1 if gi < 2 else 2
                pe.wait_ge(S("p_ready"), gi + 1)
                for st in range(nst):
                    n = (0, 1, 2, 4)[gi] + st
                    if n > 0:
                        pe.wait_ge(S("pT_ready"), n)
                    for j in range(4):
                        last = nc.tensor.transpose(bank(5)[:, j * P:j * P + P],
                                                   pbuf[gi % 2][:, j, st * P:st * P + P], ident)
                    last.then_inc(S("pT_mm"), 1)
                if gi > 0:
                    pe.wait_ge(S("ctx_ready"), gi)
                for st in range(nst):
                    pe.wait_ge(S("pT_ready"), (0, 1, 2, 4)[gi] + st + 1)
                    last = mm(bank(4), ctok[:, st, :], pT[:, st, :], start=st == 0, stop=st == nst - 1)
                last.then_inc(S("ctx_mm"), 1)

            gemv(2)
            for i in range(AFTER["ct", 0], len(SERIES)):
                step(i)
            logits(0)
            pe.wait_ge(S("conv_step0"), CONV_W)
            pe.wait_ge(S("conv_step1"), CONV_W)
            pe.wait_ge(S("lat_root"), 2)
            for c in range(2):
                last = mm(bank(0)[:, 0:T], ones[:], cacc[:, c, :], start=c == 0, stop=c == 1)
            last.then_inc(S("cstat_mm"), 1)
            gemv_t(2)
            logits(1)
            for gi in range(4):
                context(gi)
                if gi < 2:
                    logits(gi + 2)
                if gi == 0:
                    gemv(3)
                if gi == 1:
                    pe.wait_ge(S("csq_ready"), 1)
                    for c in range(2):
                        last = mm(bank(0)[:, T:2 * T], ones[:], csq[:, c, :], start=c == 0, stop=c == 1)
                    last.then_inc(S("cstat_mm"), 1)
            gemv_t(3)
            pe.wait_ge(S("ctx_ready"), 4)
            pe.wait_ge(S("ctx_ready"), 4)
            for c in range(4):
                for j in range(2):
                    hd = 2 * c + j
                    last = mm(bank(3 + c // 2)[64 * j:64 * j + 64, (c % 2) * T:(c % 2) * T + T],
                              uv[:, 64 * hd:64 * hd + 64], ctxT[:, hd, :], start=True, stop=True)
                if c % 2:
                    last.then_inc(S("o_mm"), 1)
            pe.wait_ge(S("dpool_ready"), 1)
            pe.wait_ge(S("pT_ready"), 6)
            for gq in range(4):
                q = slice(64 * (gq % 2), 64 * (gq % 2) + 64)
                last = mm(bank(5)[q, (gq // 2) * T:(gq // 2) * T + T], pw[q, gq // 2, :], dpool[q, gq // 2, :],
                          start=True, stop=True)
            last.then_inc(S("pool_mm"), 1)
            def out_product(n, w, src, nk, norm, after=lambda m: None):
                for m in range(KD):
                    if m >= 2:
                        pe.wait_ge(S("res_used"), KD * n + m - 1)
                    for k in range(nk):
                        last = mm(bank(6 + m % 2)[:, 0:T], w(k)[:, m * P:m * P + P], src[:, k, :],
                                  start=k == 0, stop=k == nk - 1)
                    last.then_inc(S("res_mm"), 1)
                    after(m)
                sums(norm)
                pe.wait_ge(S("rcol_ready"), norm + 1)
                spread(0, 0)

            def passes_4_5(m):
                if m == 1:
                    gemv_t(4)
                if m == 6:
                    gemv(5)
                if m == 7:
                    gemv_t(5)

            gemv(4)
            pe.wait_ge(S(f"loaded{PRE_SLOT[8]}"), landed(8))
            pe.wait_ge(S("y1_ready"), 6)
            wo = ring[:, PRE_SLOT[8], :].rearrange("p (k n) -> p k n", k=KD)
            out_product(0, lambda k: wo[:, k, :], y, KD, 1, passes_4_5)

            pe.wait_ge(S("h_ready"), 2 * KD)
            for t in range(TT):
                for k in range(KD):
                    last = mm(bank(1)[:, 36 * t:36 * t + 36], h2[:, k, t * P:t * P + P], rw[:, k, :],
                              start=k == 0, stop=k == KD - 1)
            last.then_inc(S("router_mm"), 1)
            pe.wait_ge(S("mod_ready"), 24)
            for i in range(4):
                t, half = i // 2, i % 2
                if i >= 2:
                    pe.wait_ge(S("htok_ready"), i - 1)
                for q in range(4):
                    last = nc.tensor.transpose(bank(2 + i % 2)[:, q * P:q * P + P],
                                               h2[:, 4 * half + q, t * P:t * P + P], ident)
                last.then_inc(S("htok_mm"), 1)
            pe.wait_ge(S("asg_ready"), 1)
            asg = [rt[:, 192 + E * t:192 + E * t + E] for t in range(TT)]
            mm(bank(5)[:, 0:32], cst("tri"), asg[0], start=True, stop=True)
            mm(bank(5)[:, 32:64], cst("tri"), asg[1], start=True, stop=False)
            mm(bank(5)[:, 32:64], ones[:], asg[0], start=False, stop=True)
            mm(bank(5)[:, 64:96], ones[:], asg[0], start=True, stop=False)
            mm(bank(5)[:, 64:96], ones[:], asg[1], start=False, stop=True).then_inc(S("rank_mm"), 1)
            pe.wait_ge(S("htok_ready"), 4)
            pe.wait_ge(S("sweeps_ready"), 1)
            pe.sem_inc(S("gath_ev"), 2)
            pe.sem_inc(S("gath_mm"), 1)
            pe.sem_inc(S("up_mm"), AHEAD)
            pe.sem_inc(S("down_mm"), AHEAD)
            n_sw_ap = sweeps[0:1, 0:1]

            def pe_group(g):
                def slot(n):
                    s = EXP_SLOT[n % SLOTS]
                    return s, g * 48 + 16 * (PRE[s] + n // SLOTS + 1)

                def gather(i):
                    pe.wait_ge(S("gath_ev"), g * 10 + (i + 1))
                    b = bank(GATH[i % 2])
                    if i in (4, 5):
                        pe.wait_ge(S("gated"), g * 2 + 2)
                        for q in range(2):
                            for t in range(TT):
                                last = nc.tensor.transpose(
                                    b[:, q * T + t * P:q * T + t * P + P],
                                    s_gt[:, t, (2 * (i - 4) + q) * P:(2 * (i - 4) + q) * P + P], ident)
                    else:
                        j = (0, 1, None, 2, 3)[i // 2]
                        pe.wait_ge(S("onehot"), g * 8 + (2 * j + 2))
                        for q in range(4):
                            k = 4 * (i % 2) + q
                            for t in range(TT):
                                last = mm(b[:, q * P:q * P + P], htok[:, t, k * P:k * P + P],
                                          s_oh[:, t, j * P:j * P + P], start=t == 0, stop=t == 1)
                    last.then_inc(S("gath_mm"), 1)

                for i in range(2):
                    gather(i)
                for j in range(4):
                    pe.wait_ge(S("gath_ev"), g * 10 + ((1, 3, 7, 9)[j] + 3))
                    for i in range(2):
                        s, at = slot(3 * j + i)
                        pe.wait_ge(S(f"loaded{s}"), at)
                        w = ring[:, s, :].rearrange("p (a k f) -> p a k f", a=2, k=KD)
                        for k in range(KD):
                            for e in range(2):
                                lo = (2 * j + e) * CAP
                                last = mm(bank(i)[64 * e:64 * e + 64, :], hsel[:, k, lo:lo + CAP], w[:, e, k, :],
                                          start=k == 0, stop=k == KD - 1)
                        last.then_inc(S("up_mm"), 1)
                    for i in ((2, 3, 4, 5), (6, 7), (8, 9), ())[j]:
                        gather(i)
                    pe.wait_ge(S("hid_ready"), g * 4 + (j + 1))
                    for k in range(KF):
                        last = nc.tensor.transpose(bank(6)[:, k * P:k * P + P], hid[:, k * P:k * P + P], ident)
                    last.then_inc(S("hidT_mm"), 1)
                    s, at = slot(3 * j + 2)
                    pe.wait_ge(S("hidT_ready"), g * 4 + (j + 1))
                    pe.wait_ge(S(f"loaded{s}"), at)
                    w = ring[:, s, :].rearrange("p (a k n) -> p a k n", a=2, k=KF)
                    for half in range(2):
                        if half:
                            pe.wait_ge(S("gath_ev"), g * 10 + ((5, 7, 9, 9)[j] + 3))
                        for k in range(KF):
                            for e in range(2):
                                last = mm(bank(2 + half)[64 * e:64 * e + 64, :], hidT[:, k, 64 * e:64 * e + 64],
                                          w[:, e, k, half * 512:half * 512 + 512], start=k == 0, stop=k == KF - 1)
                        last.then_inc(S("down_mm"), 1)
                    for c in range(4):
                        pe.wait_ge(S("y_ready"), g * 8 + (2 * j + c // 2 + 1))
                        pe.wait_ge(S("moe_add"), g * 16 + (4 * j + c + 3))
                        for q in range(2):
                            m = 2 * c + q
                            last = mm(bank(4 + c % 2)[:, q * T:q * T + T], yex[:, m * P:m * P + P], gT[:, j, :],
                                      start=True, stop=True)
                        last.then_inc(S("comb_mm"), 1)

            n_sw = pe.value_load(n_sw_ap, min_val=1, max_val=4)
            with pe.Fori(0, 4) as g:
                pe_group(g)
            with pe.If(n_sw > 1):
                with pe.Fori(4, n_sw * 4) as g:
                    pe_group(g)

            def post(j):
                s = POST_SLOT[j]
                pe.wait_ge(S(f"loaded_b{s}"), 16 * POST_SLOT[:j + 1].count(s))
                return s, ring[:, s, :]

            sums(2)
            for t in range(TT):
                last = mm(bank(1 + t)[:, 0:1], xsq[2][:, 1, t * P:t * P + P], ones[:, 0:1], start=True, stop=True)
            last.then_inc(S("msn_mm"), 1)
            pe.wait_ge(S("rcol_ready"), 3)
            spread(0, T, False)
            spread(2, 0)
            pe.wait_ge(S("h_ready"), 3 * KD)
            def proj2(i):
                kind, n = PROJ2[i]
                j = "qkvzbch".index(kind)
                width = 1024 if j < 6 else 512
                s, w = post(j // 2)
                w = w[:, 0:KD * width].rearrange("p (k n) -> p k n", k=KD)
                at = 512 * (j % 2) + n * P
                if i >= 2:
                    pe.wait_ge(S("proj2_ev"), i - 1)
                if i == 0:
                    pe.wait_ge(S("x_normed"), KD)
                for k in range(KD):
                    last = mm(bank(PROJ2_BANK[i])[:, 0:T], w[:, k, at:at + P], g_h[:, k, :], start=k == 0,
                              stop=k == KD - 1)
                last.then_inc(S("proj2_mm"), 1)

            def units(outs, product, banks):
                for t in range(TT):
                    for wait in outs:
                        pe.wait_ge(S(wait[0]), wait[1][t])
                    for hd in range(GH):
                        last = product(t, hd, bank(banks + t)[:, hd * P:hd * P + P])
                    last.then_inc(S("unit_mm"), 1)

            def k_(t, hd):
                return qkv[:, 4 + hd, t * P:t * P + P]

            abw = col("abw", 0, 64).rearrange("p (k n) -> p k n", k=KD)
            for t in range(TT):
                for k in range(KD):
                    last = mm(bank(2)[:, 8 * t:8 * t + 8], g_h[:, k, t * P:t * P + P], abw[:, k, :],
                              start=k == 0, stop=k == KD - 1)
            last.then_inc(S("ab_mm"), 1)
            proj2(0)
            proj2(1)
            pe.wait_ge(S("g_ready"), 1)
            pe.wait_ge(S("gcon_in"), 16)
            mm(bank(6)[:, 0:8], U_c, dl[:, 56:64], start=True, stop=True)
            mm(bank(6)[:, 8:16], ones_c, dl[:, 56:64], start=True, stop=True).then_inc(S("gcum_mm"), 1)
            for i in range(2, 8):
                proj2(i)
            pe.wait_ge(S("ab_ready"), 1)
            units([], lambda t, hd, b: mm(b, dl[:, 56 + 4 * t + hd:57 + 4 * t + hd].to_broadcast([P, P]), U_c,
                                          start=True, stop=True), 2)
            proj2(8)
            pe.wait_ge(S("qkv_ready"), 8)
            pe.wait_ge(S("gcol_ready"), 1)
            units([], lambda t, hd, b: nc.tensor.transpose(b, k_(t, hd), ident), 6)
            proj2(9)
            pe.wait_ge(S("sq8_ready"), 2)
            for i in range(2):
                for t in range(TT):
                    for hd in range(GH):
                        o = 8 * i + 4 * t + hd
                        last = mm(bank(4)[:, o:o + 1], sq8[:, 4 * i + hd, t * P:t * P + P], ones[:, 0:1], start=True,
                                  stop=True)
            last.then_inc(S("qk_mm"), 1)
            proj2(10)
            pe.wait_ge(S("qk_root"), 1)
            units([], lambda t, hd, b: mm(b, k_(t, hd), k_(t, hd), start=True, stop=True), 4)
            proj2(11)
            pe.wait_ge(S("brk_ready"), 1)
            units([("expg_ready", (1, 2)), ("dec_arg", (1, 2))],
                  lambda t, hd, b: mm(b, dl[:, 120 + 4 * t + hd:121 + 4 * t + hd].to_broadcast([P, P]), ident,
                                      start=True, stop=True), 2)
            proj2(12)
            pe.wait_ge(S("qkv_ready"), 12)
            units([("k_used", (4, 8))],
                  lambda t, hd, b: nc.tensor.transpose(b, qkv[:, 8 + hd, t * P:t * P + P], ident), 6)
            proj2(13)
            units([("kk_used", (1, 2))],
                  lambda t, hd, b: mm(b, k_(t, hd), qkv[:, hd, t * P:t * P + P], start=True, stop=True), 4)
            proj2(14)
            proj2(15)
            for t in range(TT):
                pe.wait_ge(S("attn_ready"), t + 1)
                pe.wait_ge(S("ttm_ready"), t + 1)
                for hd in range(GH):
                    last = nc.tensor.transpose(bank(4 + t)[:, hd * P:hd * P + P], ttm[:, 4 * t + hd, :], ident)
                last.then_inc(S("merge0_mm"), 1)
            pe.wait_ge(S("proj2_ev"), 16)
            for lv in range(1, LEVELS):
                for t in range(TT):
                    pe.wait_ge(S("lm_ready"), TT * (lv - 1) + t + 1)
                    if lv == 1:
                        pe.wait_ge(S("tm0_ready"), t + 1)
                    else:
                        pe.wait_ge(S("tm_ready"), TT * (lv - 2) + t + 1)
                    for hd in range(GH):
                        u = 4 * t + hd
                        last = mm(bank(t)[:, hd * P:hd * P + P], lm[:, u, :], tm[:, u, :], start=True, stop=True)
                    last.then_inc(S("merge_p_mm"), 1)
                for t in range(TT):
                    pe.wait_ge(S("pm_ready"), TT * (lv - 1) + t + 1)
                    pe.wait_ge(S("ttm_ready"), TT * (lv - 1) + t + 1)
                    if lv < LEVELS - 1:
                        for hd in range(GH):
                            u = 4 * t + hd
                            last = mm(bank(4 + t)[:, hd * P:hd * P + P], ttm[:, u, :], pm[:, u, :], start=True,
                                      stop=True)
                        last.then_inc(S("merge_t_mm"), 1)
                    for hd in range(GH):
                        u = 4 * t + hd
                        last = mm(bank(2 + t)[:, hd * P:hd * P + P], pm[:, u, :], ttm[:, u, :], start=True, stop=True)
                    last.then_inc(S("merge_tt_mm"), 1)
            for t in range(TT):
                pe.wait_ge(S("ttm_ready"), TT * (LEVELS - 1) + t + 1)
                for hd in range(GH):
                    u = 4 * t + hd
                    last = mm(bank(4 + t)[:, hd * P:hd * P + P], kbe[:, u, :], ttm[:, u, :], start=True, stop=True)
                last.then_inc(S("wt_mm"), 1)
            pe.wait_ge(S("v_used"), 8)
            proj2(16)
            pe.wait_ge(S("wt_ready"), 2)
            pe.wait_ge(S("qdec_ready"), 8)
            for n in range(NCH):
                t, o = n // 2, 64 * (n % 2)
                q = slice(o, o + 64)
                if n >= 1:
                    pe.wait_ge(S("state_ready"), 4 * n)
                if n >= 2:
                    pe.wait_ge(S("o_ready"), n - 1)
                for hd in range(GH):
                    u = 4 * t + hd
                    dst = bank(n % 2)[q, hd * P:hd * P + P]
                    last = mm(dst, ttm[q, u, o:o + 64], vb[q, u, :], start=True, stop=n == 0)
                    if n > 0:
                        last = mm(dst, wtn[:, u, o:o + 64], state[:, hd, :], start=False, stop=True)
                last.then_inc(S("vnew_mm"), 1)
                proj2(17 + 2 * n)
                pe.wait_ge(S("vnew_ready"), n + 1)
                if n < NCH - 1:
                    for hd in range(GH):
                        u = 4 * t + hd
                        last = mm(bank(6 + n % 2)[:, hd * P:hd * P + P], kdec[q, u, :], vnew[q, hd, :], start=True,
                                  stop=True)
                    last.then_inc(S("state_mm"), 1)
                for hd in range(GH):
                    u = 4 * t + hd
                    dst = bank(2 + n % 2)[:, 64 * hd:64 * hd + 64]
                    last = mm(dst, vnew[q, hd, :], attn_t[q, u, o:o + 64], start=True, stop=n == 0)
                    if n > 0:
                        last = mm(dst, state[:, hd, :], qkv[:, hd, 64 * n:64 * n + 64], start=False, stop=True)
                last.then_inc(S("out_mm"), 1)
                proj2(18 + 2 * n)
            proj2(25)
            pe.wait_ge(S("osq_ready"), 1)
            for t in range(TT):
                for hd in range(GH):
                    o = 4 * t + hd
                    last = mm(bank(7)[:, o:o + 1], o_sq[:, hd, t * P:t * P + P], ones[:, 0:1], start=True, stop=True)
            last.then_inc(S("osum_mm"), 1)
            proj2(26)
            pe.wait_ge(S("fac_ready"), 1)
            pe.wait_ge(S("o_ready"), NCH)
            for hd in range(GH):
                for t in range(TT):
                    o, to = 128 + 4 * t + hd, (hd % 2) * T + t * P
                    last = mm(bank(2 + hd // 2)[:, to:to + P], dl[:, o:o + 1].to_broadcast([P, P]), ident,
                              start=True, stop=True)
            last.then_inc(S("fac_mm"), 1)
            proj2(27)
            pe.wait_ge(S("y2_ready"), 6)
            s, w = post(4)
            wo2 = w.rearrange("p (k n) -> p k n", k=KD)
            out_product(1, lambda k: wo2[:, k, :], g_y, KD, 3)
            pe.wait_ge(S("h_ready"), 4 * KD)
            for f in range(NFF):
                j, i = 5 + f // 4, f % 4
                half = 512 if j < 10 else 256
                if i == 0:
                    s, w = post(j)
                    w = w[:, 0:KD * 2 * half].rearrange("p (k n) -> p k n", k=KD)
                if f >= 2:
                    pe.wait_ge(S("hff_ready"), f - 1)
                for b, off, name in ((2 * (f % 2) + 2, 0, "ff_gate_mm"), (2 * (f % 2) + 3, half, "ff_up_mm")):
                    for k in range(KD):
                        last = mm(bank(b)[:, 0:T], w[:, k, off + i * P:off + i * P + P], f_h[:, k, :], start=k == 0,
                                  stop=k == KD - 1)
                    last.then_inc(S(name), 1)
            down = [post(11 + j)[1].rearrange("p (k n) -> p k n", k=KD) for j in range(3)]
            pe.wait_ge(S("hff_ready"), NFF)
            out_product(2, lambda k: down[k // 8][:, k % 8, :], hff, NFF, 4)


def _tiles(w):
    r, n = w.shape
    return np.ascontiguousarray(w.reshape(r // P, P, n).transpose(1, 0, 2)).reshape(P, (r // P) * n)


def _cols(v):
    return v.reshape(-1, P).T


def _constants():
    i = np.arange(P)
    const = np.zeros((P, NCONST), np.float32)
    const[:, CONST["ident"][0]:CONST["ident"][1]] = np.eye(P)
    const[:, CONST["tri"][0]:CONST["tri"][1]] = i[:, None] < i[None, :]
    const[:, CONST["iota"][0]:CONST["iota"][1]] = np.arange(CAP)
    const[:, CONST["prio"][0]:CONST["prio"][1]] = 8 - np.arange(8)
    aconst = np.zeros((P, 4, T), np.float32)
    s = np.arange(T)
    for qb in range(2):
        aconst[:, qb] = np.where((s[None, :] // CHUNK) <= ((qb * P + i[:, None]) // CHUNK), 0.0, MASKED)
    for c in range(2):
        for half in range(2):
            w = (2, 4, 8, 16)[2 * c + half]
            aconst[64 * half:64 * half + 64, 2 + c] = 1.0 / np.minimum(s + 1, w)
    g = np.zeros((P, 3 + LEVELS, P), np.float32)
    same = (i[:, None] // CHUNK) == (i[None, :] // CHUNK)
    g[:, 0] = same & (i[:, None] <= i[None, :])
    g[:, 1] = same
    g[:, 2] = np.where(same & (i[:, None] <= i[None, :]), 0.0, MASKED)
    for lv in range(LEVELS):
        b = 1 << lv
        pair = (i[:, None] // (2 * b)) == (i[None, :] // (2 * b))
        g[:, 3 + lv] = pair & ((i[:, None] // b) % 2 == 0) & ((i[None, :] // b) % 2 == 1)
    return const, aconst, g


def kernel(**inp):
    from concourse import bacc
    from concourse.bass_utils import run_bass_kernel_spmd

    inp = {k: np.asarray(v) for k, v in inp.items()}
    C = np.ascontiguousarray

    def passes(w):
        return C(w.reshape(2, 4, P, 3, 2048).transpose(3, 0, 2, 1, 4)).reshape(6, P, SLOT)

    win = inp["w_in"][0]
    ki = win[:, 1408:1472]
    wa = np.concatenate([ki, ki, win[:, 896:1408], win[:, 512:896]], axis=1)
    wb = np.concatenate([win[:, 0:512], win[:, 1480:1736], win[:, 1472:1480]], axis=1)
    w2 = inp["w_in_2"][0]
    gate, up, down = inp["w_gate_2"][0], inp["w_up_2"][0], inp["w_down_2"][0]
    ffu = np.stack([_tiles(np.concatenate([gate[:, 512 * i:512 * i + 512], up[:, 512 * i:512 * i + 512]], axis=1))
                    for i in range(5)])
    vectors = [_cols(inp["c"][0]), _cols(inp["c_2"][0]), _cols(inp["mod_b"][0]), _cols(inp["b_ada_2"][0]),
               _cols(inp["norm1_g"][0]), _cols(inp["norm2_g"][0]), _cols(inp["final_g"]), _cols(inp["norm1_w_2"][0]),
               _cols(inp["norm2_w_2"][0]), _cols(inp["norm_f_w_2"]), _cols(inp["conv_b"][0]),
               _cols(inp["conv_ln_g"][0]), _cols(inp["conv_ln_b"][0]), _cols(inp["q_norm_g"][0]),
               _cols(inp["kv_norm_g"][0]), _cols(inp["pool_scale"][0]),
               inp["conv_k"][0].reshape(CONV_W, 2, P).transpose(2, 1, 0).reshape(P, 2 * CONV_W),
               inp["conv_qkv_w_2"][0].reshape(4, 12, P).transpose(2, 1, 0).reshape(P, 48),
               inp["conv_short_w_2"][0].reshape(3, 4, P).transpose(2, 1, 0).reshape(P, 12),
               _cols(inp["gdn_norm_w_2"][0]),
               np.broadcast_to(inp["router_g_b"][0].reshape(1, 4), (P, 4)),
               np.broadcast_to(inp["router_e_b"][0].reshape(1, 32), (P, 32)),
               np.broadcast_to(inp["A_log_2"][0].reshape(1, 4), (P, 4)),
               np.broadcast_to(inp["dt_bias_2"][0].reshape(1, 4), (P, 4)), _tiles(w2[:, 2048:2056])]
    pool_w = inp["pool_w"][0].reshape(2, 2, 64, 64).transpose(1, 2, 0, 3).reshape(P, 128)
    router = np.concatenate([inp["router_g_w"][0], inp["router_e_w"][0].reshape(D, E)], axis=1)
    uk = inp["w_uk"][0].transpose(1, 2, 0).reshape(4, P, P).transpose(1, 0, 2).reshape(P, 512)
    smallw = [_tiles(inp["w_uq"][0].reshape(256, 512)), uk, inp["w_uv"][0].reshape(P, 512), pool_w, _tiles(router)]
    const, aconst, gconst = _constants()

    def experts(w):
        e, r, n = w.shape
        return C(w.reshape(e, r // P, P, n).transpose(0, 2, 1, 3)).reshape(e, P, (r // P) * n)

    arrays = {
        "xT": C(inp["x"][0].T.reshape(KD, P, T).transpose(1, 0, 2)),
        "mod_w": passes(inp["mod_w"][0]), "ada_w": passes(inp["w_ada_2"][0]),
        "winA": _tiles(wa), "winB": _tiles(wb), "wout": _tiles(inp["w_out"][0]),
        "ew1": experts(inp["exp_w1"][0]), "ew3": experts(inp["exp_w3"][0]), "ew2": experts(inp["exp_w2"][0]),
        "w2A": _tiles(w2[:, 0:1024]), "w2B": _tiles(w2[:, 1024:2048]), "w2C": _tiles(w2[:, 2056:3080]),
        "w2D": _tiles(w2[:, 3080:3592]),
        "wout2": _tiles(inp["w_out_2"][0]),
        "ffu": ffu, "ffu_last": _tiles(np.concatenate([gate[:, 2560:], up[:, 2560:]], axis=1)),
        "ffd": np.stack([_tiles(down[0:1024]), _tiles(down[1024:2048])]), "ffd_last": _tiles(down[2048:]),
        "cols_d": C(np.concatenate(vectors, axis=1)), "small_d": C(np.concatenate(smallw, axis=1)),
        "const_d": const, "aconst_d": aconst, "gconst_d": gconst,
    }
    nc = bacc.Bacc("TRN2", target_bir_lowering=False, num_devices=1)
    aps = {k: nc.dram_tensor("in_" + k, a.shape, mybir.dt.from_np(a.dtype), kind="ExternalInput").ap()
           for k, a in arrays.items()}
    out = nc.dram_tensor("out_dram", (P, KD, T), mybir.dt.float32, kind="ExternalOutput").ap()
    program(nc, out=out, **aps)
    r = run_bass_kernel_spmd(nc, [{"in_" + k: a for k, a in arrays.items()}], core_ids=[0])
    got = r.results[0]["out_dram"]
    return np.ascontiguousarray(got.transpose(1, 0, 2).reshape(D, T).T).reshape(1, T, D)
```

```python
import itertools
from contextlib import ExitStack

import concourse.bass as bass
import numpy as np
from concourse import mybir

P = 128
D = 1024
KD = D // P
T = 256
TT = T // P
EPS = 1e-6
CONV_W = 31
HEADS, HD = 8, 64
TOPK = 64
IDX_SCALE = float((8 * 64) ** -0.5)
ATT_SCALE = float(HD ** -0.5)
CHUNK = 64
E, EG, F = 32, 8, 512
KF = F // P
CAP = 64
MASKED = -1.0e30
TAKEN = -3.0e38
GH = 4
NCH = T // CHUNK
FF = 2816
NFF = FF // P
LEVELS = 6

SLOTS, SLOT = 4, 8192
PRE_LOADS = 15
PRE = [(PRE_LOADS - s + SLOTS - 1) // SLOTS for s in range(SLOTS)]

COLS = {}
_n = 0
for _name, _w in (("c", 8), ("c2", 8), ("mod_b", 48), ("ada_b", 48), ("n1", 8), ("n2", 8), ("nf", 8),
                  ("n1b", 8), ("n2b", 8), ("nfb", 8), ("conv_b", 2), ("ln_g", 2), ("ln_b", 2),
                  ("q_g", 2), ("kv_g", 1), ("pool_s", 2), ("conv_k", 2 * CONV_W), ("gconv", 48),
                  ("sconv", 12), ("gnorm", 1), ("rbias", 36), ("a_log", 4), ("dt", 4), ("abw", 64)):
    COLS[_name] = (_n, _n + _w)
    _n += _w
NCOL = _n
SMALL = {}
_n = 0
for _name, _w in (("uq", 1024), ("uk", 512), ("uv", 512), ("pw", 128), ("rw", 288)):
    SMALL[_name] = (_n, _n + _w)
    _n += _w
NSMALL = _n
CONST = {}
_n = 0
for _name, _w in (("ident", 128), ("tri", 128), ("iota", 64), ("prio", 8)):
    CONST[_name] = (_n, _n + _w)
    _n += _w
NCONST = _n


def program(nc, xT, mod_w, ada_w, winA, winB, wout, ew1, ew3, ew2, w2A, w2B, w2C, w2D, wout2,
            ffu, ffu_last, ffd, ffd_last, cols_d, small_d, const_d, aconst_d, gconst_d, out):
    fp32, fp32r = mybir.dt.float32, mybir.dt.float32r
    i32 = mybir.dt.int32
    ACT = mybir.ActivationFunctionType
    ALU = mybir.AluOpType
    AX = mybir.AxisListType.X

    with ExitStack() as ctx:
        def sb(name, shape, dt=fp32):
            return ctx.enter_context(nc.sbuf_tensor(name, shape, dt))

        sems, count = {}, {}

        def S(name):
            if name not in sems:
                sems[name] = ctx.enter_context(nc.semaphore(name))
                count[name] = 0
            return sems[name]

        for s in range(SLOTS):
            S(f"loaded{s}"), S(f"loaded_b{s}")

        ring_at = -(-nc.sbuf_base // 32) * 32
        ring = sb("ring", [P, SLOTS, SLOT])
        ring_r = {s: nc.alloc_sbuf_tensor_at(f"ring_rounded{s}", [P, SLOT // 2], fp32r,
                                             offset=ring_at + 4 * SLOT * s) for s in (1, 3)}
        x = sb("x_res", [P, KD, T])
        cols = sb("cols", [P, NCOL])
        const = sb("const", [P, NCONST])
        ones = sb("ones", [P, P])
        zero = sb("zero", [P, 1])
        one = sb("one", [P, 1])
        eps = sb("eps", [P, 1])
        mod1 = sb("mod1", [P, 48])
        mod2 = sb("mod2", [P, 48])
        gain = sb("gain", [P, 4, KD])
        cact = sb("cact", [P, 2, 8])
        sweeps = sb("sweeps", [P, 1], i32)
        small = sb("smalls", [P, 64])
        rst = sb("rst", [P, 2, T])
        ARENA = 16444
        arena_at = -(-nc.sbuf_base // 32) * 32
        arena = sb("arena", [P, ARENA])
        arena_r = nc.alloc_sbuf_tensor_at("arena_rounded", [P, ARENA], fp32r, offset=arena_at)
        psum = [ctx.enter_context(nc.psum_tensor(f"bank{i}", [P, 2, 512], fp32)) for i in range(4)]

        def bank(i):
            return psum[i // 2][:, i % 2, :]

        def view(off, *shape, of=None):
            n = 1
            for d in shape:
                n *= d
            assert off + n <= ARENA, (off, shape)
            v = (arena if of is None else of)[:, off:off + n]
            if len(shape) == 2:
                v = v.rearrange("p (a b) -> p a b", a=shape[0])
            if len(shape) == 3:
                v = v.rearrange("p (a b c) -> p a b c", a=shape[0], b=shape[1])
            return v

        def rounded(off, *shape):
            return view(off, *shape, of=arena_r)

        def col(name, i=0, n=1):
            a = COLS[name][0] + i
            return cols[:, a:a + n]

        def cst(name):
            return const[:, CONST[name][0]:CONST[name][1]]

        ident = cst("ident")

        PRE_SLOT = [0, 1, 2, 3, 0, 1, 2, 0, 1, 3, 2, 0, 3, 2, 0]
        EXP_SLOT = [3, 2, 0, 1]
        POST_SLOT = [3, 2, 0, 1, 2, 0, 3, 1, 2, 0, 1, 2, 0, 1]
        PRE = [PRE_SLOT.count(s) for s in range(SLOTS)]
        PASS = [(0, 1), (4, 5), (6, 7), (9, 10), (11, 12), (13, 14)]

        def landed(n):
            return 16 * PRE_SLOT[:n + 1].count(PRE_SLOT[n])

        h = view(0, KD, T)
        qabs = view(0, HEADS, T)
        ctxT = view(2048, HEADS, T)
        aval = view(2048, 2, T)
        cgate = view(2560, 2, T)
        smallw = view(4096, NSMALL)
        uq = smallw[:, 0:1024].rearrange("p (k n) -> p k n", k=2)
        uk = smallw[:, 1024:1536].rearrange("p (k n) -> p k n", k=4)
        uv = smallw[:, 1536:2048]
        pw = smallw[:, 2048:2176].rearrange("p (g n) -> p g n", g=2)
        rw = smallw[:, 2176:2464].rearrange("p (k n) -> p k n", k=KD)
        z_att = view(6560, 8, T)
        ki, qi, cq, ckv = z_att[:, 0, :], z_att[:, 1:5, :], z_att[:, 5:7, :], z_att[:, 7, :]
        rel = view(8608, 3, T)
        qT = view(9376, 4, T)
        UPW, PPW = T + CONV_W - 1, T + 16
        psums = view(10400, 2, 2 * PPW)
        upad = view(11488, 2, UPW)
        ppad = view(12060, 2, PPW)
        y = view(12604, KD, T)
        ctok = view(14652, TT, P)
        score = view(14908, TT, T)
        aconst = view(15420, 4, T)
        selb = aconst
        pbuf = [view(6816, 4, T), view(9376, 4, T)]
        pT = view(12604 + 512, 2, 512)
        modrow = [view(12604 + 1536, 512)] * 4 + [view(8608, 512)] * 2
        cacc = y[:, 0:2, :]
        csq = view(11488, 2, T)
        dpool = cq
        wi = small[:, 0:16].rearrange("p (t h) -> p t h", t=TT)
        top8, ssum, rsum = small[:, 16:24], small[:, 28:36], small[:, 36:40]
        mx = [small[:, 24:28], small[:, 40:44]]

        htok = view(0, TT, D)
        s_oh = view(2048, TT, EG * CAP)
        s_gt = view(3072, TT, EG * CAP)
        gT = view(4096, 4, T)
        hsel = view(7168, KD, EG * CAP)
        h2 = view(11264, KD, T)
        sil, hid = view(11264, 512), view(11776, 512)
        hidT = view(12288, KF, P)
        yex = view(12800, D)
        rt = view(13824, 512)
        rank_s = view(14336, TT, 4 * E)
        gate_s = view(14592, TT, 4 * E)
        sq_xn = view(0, KD, 2, T)

        g_hi, g_lo = rounded(0, KD, T), rounded(2048, KD, T)
        g_in = view(2048, KD, T)
        g_y, y_lo = view(4096, KD, T), rounded(4096, KD, T)
        qkv = view(6144, 12, T)
        raw = view(9216, 12, T + 3)
        zg = view(12324, 4, T)
        gcon = view(13348, 3 + LEVELS, P)
        dl = view(14500, 144)
        scb, scc = view(14644, 2, T), view(15156, 2, T)
        scp = view(15668, 2, T + 2)
        y_hi = [rounded(o, 4, T) for o in (7168, 11264)]
        SCR = POST_SLOT[0]

        def scr(i):
            v = ring[:, SCR, 1024 * i:1024 * (i + 1)]
            return v.rearrange("p (u c) -> p u c", u=8)
        dec, lt, expg, attn_t, tm, ttm, pm, lm = [scr(i) for i in range(8)]
        sq8 = view(9216, 8, T)
        kdec, vb, kbe = view(9216, 8, P), view(10240, 8, P), view(14644, 8, P)
        wtn = lm
        state, vnew = tm[:, 0:4, :], tm[:, 4:8, :]
        o_t, o_sq = [ring[:, SCR, 1024 * i:1024 * (i + 1)].rearrange("p (h c) -> p h c", h=GH) for i in range(2)]
        f_hi, f_lo, f_in = g_hi, g_lo, g_in
        hf_hi, hf_lo = rounded(4096, NFF, T), rounded(9728, NFF, T)
        hff = view(9728, NFF, T)
        sff = view(15360, 2, 2, T)
        f_h = view(0, KD, T)
        U_c, ones_c, mask_c = gcon[:, 0, :], gcon[:, 1, :], gcon[:, 2, :]

        rcol = small[:, 44:52]
        gnf = small[:, 52:60]
        xsq = [view(12604, 3, T)] + [view(15676, 3, T)] * 4
        GATH = (7, 3)
        STAT = (0, 5)

        block = ctx.enter_context(nc.Block())

        SERIES = [("a", 0), ("a", 1), ("g", 0), ("g", 1), ("p", 0), ("p", 1), ("wi", 0)]
        SERIES += [("lat", i) for i in range(3)] + [("ki", 0)] + [("qi", i) for i in range(4)]
        SERIES += [("ix", 0), ("ix", 1), ("q", 0), ("ix", 2), ("q", 1), ("ix", 3), ("q", 2), ("ix", 4), ("q", 3)]
        SERIES += [("ix", 5), ("ix", 6), ("ix", 7), ("ct", 0)]
        SERIES += [(kind, i + d) for i in range(8) for kind, d in (("qa", 0), ("ix", 8))]
        AFTER = {step: i + 1 for i, step in enumerate(SERIES)}
        GROW, KTOK, KK, BROW, VTOK, KQ = 0, 2, 4, 6, 8, 10
        PROJ2 = [(kind, i) for kind in "qkvz" for i in range(4)] + [(kind, i) for i in range(4) for kind in "bch"]
        PROJ2_BANK = [(i + 1) % 2 for i in range(16)] + [7] + [4 + i % 2 for i in range(17, 28)]

        PIECES, USED = [], []
        for i, (kind, n) in enumerate(PROJ2):
            j = "qkvzbch".index(kind)
            PIECES.append((j // 2, 512 * (j % 2) + n * P, KD, 1024 if j < 6 else 512))
            USED.append(("proj2_mm", i + 1))
        MIX2 = len(PIECES)
        for m in range(KD):
            PIECES.append((4, m * P, KD, D))
            USED.append(("res_mm", KD + m + 1))
        UP2 = len(PIECES)
        for f in range(NFF):
            half = 512 if f < 20 else 256
            for part in range(2):
                PIECES.append(((5, 7, 8, 9, 10, 6)[f // 4], part * half + f % 4 * P, KD, 2 * half))
                USED.append((("ff_gate_mm", "ff_up_mm")[part], f + 1))
        DOWN2 = len(PIECES)
        for m in range(KD):
            for j in range(3):
                PIECES.append((11 + j, m * P, (KD, KD, NFF - 2 * KD)[j], D))
                USED.append(("down_part", 2 * m + j + 1) if j < 2 else ("res_mm", 2 * KD + m + 1))

        def post_place(j):
            s = POST_SLOT[j]
            return ring[:, s, SLOT // 2:SLOT] if j in (3, 6) else ring[:, s, :]

        def piece(p):
            j, at, n, width = PIECES[p]
            w = post_place(j)[:, 0:n * width].rearrange("p (k n) -> p k n", k=n)[:, :, at:at + P]
            o = 2048 * (p % 2)
            parts = ring_r[1 if p < UP2 else 3][:, o:o + 2 * n * P]
            return w, parts[:, 0:n * P].rearrange("p (k n) -> p k n", k=n), \
                parts[:, n * P:2 * n * P].rearrange("p (k n) -> p k n", k=n)

        AHEAD = 8

        @block.sync
        def _(sp):
            sp.dma_start(x[:], xT).then_inc(S("x_in"), 16)
            sp.dma_start(cols[:], cols_d).then_inc(S("small_in"), 16)
            sp.dma_start(const[:], const_d).then_inc(S("small_in"), 16)
            pre = [(mod_w[0], SLOT, None), (mod_w[1], SLOT, None), (winB, winB.shape[1], None), (winA, SLOT, None),
                   (mod_w[2], SLOT, ("gemv_mm", 1)), (mod_w[3], SLOT, ("gemv_mm", 1)),
                   (mod_w[4], SLOT, ("proj_mm", AFTER["wi", 0])), (mod_w[5], SLOT, ("gemv_mm", 2)),
                   (wout, SLOT, ("gemv_mm", 2)), (ada_w[0], SLOT, ("proj_mm", AFTER["qi", 3])),
                   (ada_w[1], SLOT, ("gemv_mm", 3)), (ada_w[2], SLOT, ("gemv_mm", 3)),
                   (ada_w[3], SLOT, ("gemv_mm", 4)), (ada_w[4], SLOT, ("gemv_mm", 4)),
                   (ada_w[5], SLOT, ("gemv_mm", 5))]
            for n, (src, width, used) in enumerate(pre):
                s = PRE_SLOT[n]
                if used:
                    sp.wait_ge(S(used[0]), used[1])
                sp.dma_start(ring[:, s, 0:width], src).then_inc(S(f"loaded{s}"), 16)
                if n == 2:
                    sp.dma_start(aconst[:], aconst_d).then_inc(S("att_in"), 16)
                    sp.dma_start(smallw[:], small_d).then_inc(S("att_in"), 16)

            def expert_used(g8, n):
                if n % 3 < 2:
                    sp.wait_ge(S("up_mm"), g8 + (AHEAD + 2 * (n // 3) + n % 3 + 1))
                else:
                    sp.wait_ge(S("down_mm"), g8 + (AHEAD + 2 * (n // 3) + 2))

            def expert_load(e8, n):
                s = EXP_SLOT[n % SLOTS]
                w = (ew1, ew3, ew2)[n % 3]
                pair = w[bass.ds(e8 + 2 * (n // 3), 2), :, :]
                sp.dma_start(ring[:, s, :].rearrange("p (a f) -> p a f", a=2),
                             pair.rearrange("a p f -> p a f")).then_inc(S(f"loaded{s}"), 16)

            for n, used in enumerate([("gemv_mm", 5), ("gemv_mm", 6), ("gemv_mm", 6), ("res_mm", KD)]):
                sp.wait_ge(S(used[0]), used[1])
                expert_load(0, n)
            with sp.Fori(0, 3) as g:
                for n in range(SLOTS, 12 + SLOTS):
                    expert_used(g * 8, n - SLOTS)
                    expert_load(g * 8 + 8 * (n // 12), n % 12)
            for n in range(SLOTS, 12):
                expert_used(3 * 8, n - SLOTS)
                expert_load(3 * 8, n)
            sp.wait_ge(S("sweeps_ready"), 1)
            n_sw = sp.value_load(sweeps[0:1, 0:1], min_val=1, max_val=4)
            with sp.If(n_sw > 1):
                with sp.Fori(4, n_sw * 4) as g:
                    for n in range(12):
                        expert_used(g * 8, n - SLOTS)
                        expert_load((g % 4) * 8, n)
            post = [(w2A, SLOT), (w2B, SLOT), (w2C, SLOT), (w2D, w2D.shape[1]), (wout2, SLOT), (ffu[0], SLOT),
                    (ffu_last, SLOT // 2)] + [(ffu[i], SLOT) for i in range(1, 5)]
            post += [(ffd[i], SLOT) for i in range(2)] + [(ffd_last, 6 * D)]
            free = [("w_lo", 16), ("w_lo", MIX2 - 1), ("delta_done", 1), ("res_mm", 2 * KD), ("w_lo", UP2)]
            free += [("w_lo", UP2 + 8 * i) for i in range(1, 6)]
            for j, (src, width) in enumerate(post):
                if j < SLOTS:
                    expert_used(n_sw * 32, j - SLOTS)
                else:
                    sp.wait_ge(S(free[j - SLOTS][0]), free[j - SLOTS][1])
                sp.dma_start(post_place(j)[:, 0:width], src).then_inc(S(f"loaded_b{POST_SLOT[j]}"), 16)
            for i in range(KD // 2):
                sp.wait_ge(S("out_ready"), 2 * i + 2)
                sp.dma_start(out[:, 2 * i:2 * i + 2, :], f_h[:, 2 * i:2 * i + 2, :]).then_inc(S("stored"), 16)
            sp.wait_ge(S("stored"), 16 * (KD // 2))

        @block.gpsimd
        def _(pool):
            def p(ins, name="pool_step"):
                ins.then_inc(S(name), 1)
                count[name] += 1
                pool.wait_ge(S(name), count[name])

            p(nc.gpsimd.memset(ppad[:, :, 0:16], 0.0), "pool_pad")
            pool.wait_ge(S("proj_ev"), AFTER["p", 1])
            s_a = psums[:, 0, :].rearrange("p (c t) -> p c t", c=2)
            s_b = psums[:, 1, :].rearrange("p (c t) -> p c t", c=2)
            p(nc.gpsimd.memset(psums, 0.0))
            p(nc.gpsimd.tensor_tensor(s_a[:, :, 1:PPW], ppad[:, :, 1:PPW], ppad[:, :, 0:PPW - 1], ALU.add))
            p(nc.gpsimd.tensor_tensor(s_b[:, :, 3:PPW], s_a[:, :, 3:PPW], s_a[:, :, 1:PPW - 2], ALU.add))
            p(nc.gpsimd.tensor_tensor(s_a[:, 1, 7:PPW], s_b[:, 1, 7:PPW], s_b[:, 1, 3:PPW - 4], ALU.add))
            p(nc.gpsimd.tensor_tensor(s_b[:, 1, 15:PPW], s_a[:, 1, 15:PPW], s_a[:, 1, 7:PPW - 8], ALU.add))
            pool.wait_ge(S("proj_mm"), AFTER["q", 3])
            pool.wait_ge(S("att_in"), 32)
            for c in range(2):
                for half, sums in ((0, s_a), (64, s_b)):
                    q = slice(half, half + 64)
                    p(nc.gpsimd.tensor_tensor(dpool[q, c, :], sums[q, c, 16:PPW], aconst[q, 2 + c, :], ALU.mult))
                    p(nc.gpsimd.tensor_tensor(dpool[q, c, :], dpool[q, c, :], ppad[q, c, 16:PPW], ALU.subtract),
                      "dpool_ready" if (c, half) == (1, 64) else "pool_step")

            for lv in range(1, LEVELS):
                for t in range(TT):
                    pool.wait_ge(S("lt_ready"), 1)
                    if lv > 1:
                        pool.wait_ge(S("merge_p_mm"), TT * (lv - 2) + t + 1)
                    nc.gpsimd.tensor_tensor(lm[:, 4 * t:4 * t + 4, :], lt[:, 4 * t:4 * t + 4, :],
                                            gcon[:, 3 + lv, :].unsqueeze(1).to_broadcast([P, 4, P]),
                                            ALU.mult).then_inc(S("lm_ready"), 1)

        @block.scalar
        def _(act):
            def a(ins, name):
                ins.then_inc(S(name), 1)
                count[name] += 1

            act.wait_ge(S("small_in"), 32)
            act.wait_ge(S("init"), 1)
            a(nc.scalar.activation(cact[:, 0, :], col("c", 0, 8), ACT.Silu, bias=zero[:]), "cact_ready")
            a(nc.scalar.activation(cact[:, 1, :], col("c2", 0, 8), ACT.Silu, bias=zero[:]), "cact_ready")

            def root(src, dst, n, mm, at, out_name):
                act.wait_ge(S(mm), at)
                a(nc.scalar.activation(dst, src, ACT.Sqrt, scale=1.0 / n, bias=eps[:]), out_name)

            def norm_root(n):
                act.wait_ge(S("ms_mm"), n + 1)
                for t in range(TT):
                    a(nc.scalar.activation(rcol[:, t:t + 1], bank(STAT[t])[:, 0:1], ACT.Sqrt, scale=1.0 / D,
                                           bias=eps[:]), "root_ready")

            def shifted(dst, n, mod, shift):
                for k in range(KD):
                    act.wait_ge(S("scaled"), 8 * n + k + 1)
                    a(nc.scalar.activation(dst[:, k, :], dst[:, k, :], ACT.Identity,
                                           bias=mod[:, shift * 8 + k:shift * 8 + k + 1]), "h_ready")

            def gemv_row(r):
                act.wait_ge(S("gemv_mm"), r + 1)
                if r > 0:
                    act.wait_ge(S("modT_mm"), r)
                a(nc.scalar.activation(modrow[r], bank(1), ACT.Copy), "modrow_ready")

            norm_root(0)
            gemv_row(0)
            shifted(h, 0, mod1, 0)

            def step_out(i):
                act.wait_ge(S("proj_mm"), i + 1)
                src = bank(3 + i % 2)
                kind, n = SERIES[i]
                func, kw = ACT.Copy, {}
                if kind == "a":
                    dst = aval[:, n, :]
                elif kind == "g":
                    dst, func, kw = cgate[:, n, :], ACT.Sigmoid, {"bias": zero[:]}
                elif kind == "p":
                    act.wait_ge(S("pool_pad"), 1)
                    dst = ppad[:, n, 16:PPW]
                elif kind == "wi":
                    dst = small[:, 0:16]
                elif kind in ("lat", "ki", "qi"):
                    dst = z_att[:, {"lat": 5, "ki": 0, "qi": 1}[kind] + n, :]
                elif kind == "ix":
                    if n >= 2:
                        act.wait_ge(S("idx_acc"), n - 1)
                    dst, func = rel[:, n % 2, 0:P if n < 8 else T], ACT.Relu
                elif kind == "q":
                    dst = qT[:, n, :]
                elif kind == "qa":
                    dst = qabs[:, n, :]
                else:
                    dst = ctok.rearrange("p t c -> p (t c)")
                a(nc.scalar.activation(dst, src[:, 0:dst.shape[1]], func, **kw), "proj_ev")

            for i in range(AFTER["ki", 0]):
                step_out(i)
            act.wait_ge(S("lat_mm"), 1)
            a(nc.scalar.activation(rst[:, 0, :], bank(0)[:, 0:T], ACT.Sqrt, scale=1.0 / 256, bias=eps[:]), "lat_root")
            a(nc.scalar.activation(rst[:, 1, :], bank(0)[:, T:2 * T], ACT.Sqrt, scale=1.0 / 128, bias=eps[:]), "lat_root")
            gemv_row(1)
            for i in range(AFTER["ki", 0], AFTER["ct", 0]):
                step_out(i)
            gemv_row(2)
            for i in range(AFTER["ct", 0], len(SERIES)):
                step_out(i)

            def exps(gi):
                w = P if gi < 2 else T
                act.wait_ge(S("max_ready"), gi + 1)
                for j in range(4):
                    a(nc.scalar.activation(pbuf[gi % 2][:, j, 0:w], pbuf[gi % 2][:, j, 0:w], ACT.Exp,
                                           bias=mx[gi % 2][:, j:j + 1],
                                           accum_out=ssum[:, 4 * (gi % 2) + j:4 * (gi % 2) + j + 1]), "exp_done")

            def pt_out(gi):
                for st in range(1 if gi < 2 else 2):
                    n = (0, 1, 2, 4)[gi] + st
                    act.wait_ge(S("pT_mm"), n + 1)
                    if gi > 0:
                        act.wait_ge(S("ctx_mm"), gi)
                    a(nc.scalar.activation(pT[:, st, :], bank(5), ACT.Copy), "pT_ready")

            def ctx_out(gi):
                act.wait_ge(S("ctx_mm"), gi + 1)
                if gi == 0:
                    act.wait_ge(S("u_ready"), 1)
                qb, hh = gi // 2, gi % 2
                a(nc.scalar.activation(ctxT[:, 4 * hh:4 * hh + 4, qb * P:qb * P + P],
                                       bank(4).rearrange("p (h q) -> p h q", h=4), ACT.Copy), "ctx_ready")

            exps(0)
            for gi in range(4):
                if gi < 3:
                    exps(gi + 1)
                if gi == 2:
                    root(bank(0)[:, T:2 * T], rst[:, 1, :], 256, "cstat_mm", 2, "cvar_root")
                if gi == 1:
                    gemv_row(3)
                pt_out(gi)
                ctx_out(gi)
            for c in range(2):
                act.wait_ge(S("o_mm"), c + 1)
                a(nc.scalar.activation(y[:, 2 + 2 * c:4 + 2 * c, :],
                                       bank(3 + c).rearrange("p (a t) -> p a t", a=2), ACT.Copy), "y1_ready")
            act.wait_ge(S("pool_mm"), 1)
            for c in range(2):
                a(nc.scalar.activation(y[:, 6 + c, :], bank(5)[:, c * T:c * T + T], ACT.Copy, scale=col("pool_s", c)),
                  "y1_ready")
            act.wait_ge(S("cnorm_ready"), 1)
            for c in range(2):
                a(nc.scalar.activation(y[:, c, :], cacc[:, c, :], ACT.Silu, scale=col("ln_g", c), bias=col("ln_b", c)),
                  "y1_ready")

            gemv_row(4)
            gemv_row(5)
            norm_root(1)
            shifted(h2, 1, mod1, 3)
            for i in range(4):
                act.wait_ge(S("htok_mm"), i + 1)
                t, half = i // 2, i % 2
                a(nc.scalar.activation(htok[:, t, half * 512:half * 512 + 512], bank(2 + i % 2), ACT.Copy), "htok_ready")
            act.wait_ge(S("router_in"), 1)
            a(nc.scalar.activation(rt[:, 72:80], rt[:, 72:80], ACT.Exp, bias=zero[:]), "router_exp")
            act.wait_ge(S("router_in"), 2)
            a(nc.scalar.activation(rt[:, 160:162], rt[:, 160:162], ACT.Exp, bias=zero[:]), "router_exp")

            def act_group(g):
                def gathered(i):
                    act.wait_ge(S("gath_mm"), g * 10 + (i + 2))
                    src = bank(GATH[i % 2])
                    if i in (4, 5):
                        dst, src = gT[:, 2 * (i - 4):2 * (i - 4) + 2, :], src.rearrange("p (j t) -> p j t", j=2)
                    else:
                        j = (0, 1, None, 2, 3)[i // 2]
                        dst = hsel[:, 4 * (i % 2):4 * (i % 2) + 4, j * P:j * P + P]
                        src = src.rearrange("p (k s) -> p k s", k=4)
                    nc.scalar.activation(dst, src, ACT.Copy).then_inc(S("gath_ev"), 1)

                for i in range(2):
                    gathered(i)
                for j in range(4):
                    act.wait_ge(S("up_mm"), g * 8 + (AHEAD + 2 * j + 1))
                    nc.scalar.activation(sil, bank(0), ACT.Silu, bias=zero[:]).then_inc(S("sil_ready"), 1)
                    for i in ((2, 3, 4, 5), (6, 7), (8, 9), ())[j]:
                        gathered(i)
                    act.wait_ge(S("hidT_mm"), g * 4 + (j + 1))
                    nc.scalar.activation(hidT[:], bank(6).rearrange("p (k s) -> p k s", k=KF),
                                         ACT.Copy).then_inc(S("hidT_ready"), 1)
                    for half in range(2):
                        act.wait_ge(S("down_mm"), g * 8 + (AHEAD + 2 * j + half + 1))
                        nc.scalar.activation(yex[:, half * 512:half * 512 + 512], bank(2 + half),
                                             ACT.Copy).then_inc(S("y_ready"), 1)

            act.wait_ge(S("sweeps_ready"), 1)
            n_sw = act.value_load(sweeps[0:1, 0:1], min_val=1, max_val=4)
            with act.Fori(0, 4) as g:
                act_group(g)
            with act.If(n_sw > 1):
                with act.Fori(4, n_sw * 4) as g:
                    act_group(g)

            split = itertools.count()

            def w_hi():
                p = next(split)
                w, hi, _ = piece(p)
                s = POST_SLOT[PIECES[p][0]]
                act.wait_ge(S(f"loaded_b{s}"), 16 * POST_SLOT[:PIECES[p][0] + 1].count(s))
                if p >= 2:
                    act.wait_ge(S(USED[p - 2][0]), USED[p - 2][1])
                if p == UP2:
                    act.wait_ge(S("delta_done"), 1)
                a(nc.scalar.activation(hi, w, ACT.Copy), "w_hi")

            def shifted_parts(n, mod, shift):
                for k in range(KD):
                    act.wait_ge(S("scaled"), 8 * n + k + 1)
                    b = mod[:, shift * 8 + k:shift * 8 + k + 1]
                    ins = nc.scalar.activation(g_hi[:, k, :], g_in[:, k, :], ACT.Identity, bias=b)
                    if n == 2:
                        ins = nc.scalar.activation(g_in[:, k, :], g_in[:, k, :], ACT.Identity, bias=b)
                    a(ins, "h_ready")

            for k in range(KD):
                if k % 2 == 0:
                    act.wait_ge(S("moe_add"), n_sw * 64 + (k // 2 + 1))
                a(nc.scalar.activation(sq_xn[:, k, 0, :], x[:, k, :], ACT.Square, bias=zero[:]), "sqx_ready")
                a(nc.scalar.activation(sq_xn[:, k, 1, :], x[:, k, :], ACT.Square, bias=zero[:], scale=col("nf", k)),
                  "sqx_ready")
            act.dma_start(gcon[:], gconst_d).then_inc(S("gcon_in"), 16)
            norm_root(2)
            act.wait_ge(S("ms3_in"), 1)
            a(nc.scalar.activation(rcol[:, 2:4], rcol[:, 2:4], ACT.Sqrt, scale=1.0 / D, bias=eps[:]), "root3_ready")
            w_hi()
            w_hi()
            shifted_parts(2, mod2, 0)

            def proj_out(i):
                act.wait_ge(S("proj2_mm"), i + 1)
                kind, n = PROJ2[i]
                func, kw = ACT.Copy, {}
                if kind in "qkv":
                    if i == 0:
                        act.wait_ge(S("raw_pad"), 1)
                    nc.scalar.activation(qkv[:, i, :], bank(PROJ2_BANK[i])[:, 0:T], ACT.Copy,
                                         scale=col("gconv", 4 * i + 3))
                    dst = raw[:, i, 3:3 + T]
                elif kind == "z":
                    dst, func, kw = zg[:, n, :], ACT.Silu, {"bias": zero[:]}
                else:
                    if n >= 2:
                        act.wait_ge(S("short_done"), n - 1)
                    dst = {"b": scb[:, n % 2, :], "c": scc[:, n % 2, :], "h": scp[:, n % 2, 2:2 + T]}[kind]
                a(nc.scalar.activation(dst, bank(PROJ2_BANK[i])[:, 0:T], func, **kw), "proj2_ev")
                w_hi()

            def conv_silu(m):
                for i in range(m, m + 4):
                    act.wait_ge(S("gconv_done"), i + 1)
                    a(nc.scalar.activation(qkv[:, i, :], qkv[:, i, :], ACT.Silu, bias=zero[:]), "qkv_ready")

            act.wait_ge(S("ab_mm"), KD)
            for t in range(TT):
                a(nc.scalar.activation(dl[:, 8 * t:8 * t + 8], bank(2 + t)[:, 0:8], ACT.Copy), "ab_ready")
            proj_out(0)
            proj_out(1)
            act.wait_ge(S("sp_in"), 1)
            a(nc.scalar.activation(dl[:, 24:32], dl[:, 24:32], ACT.Exp, bias=zero[:]), "sp_exp")
            a(nc.scalar.activation(dl[:, 40:48], dl[:, 40:48], ACT.Exp, bias=zero[:], scale=-1.0), "sp_exp")
            a(nc.scalar.activation(dl[:, 48:52], col("a_log", 0, 4), ACT.Exp, bias=zero[:]), "sp_exp")
            act.wait_ge(S("sp_exp"), 3)
            a(nc.scalar.activation(dl[:, 24:32], dl[:, 24:32], ACT.Ln, bias=one[:]), "sp_exp")
            for i in range(2, 8):
                proj_out(i)
            act.wait_ge(S("gcol_ready"), 1)
            a(nc.scalar.activation(dl[:, 80:96], dl[:, 64:80], ACT.Exp, bias=zero[:]), "gexp_ready")
            act.wait_ge(S("w_lo"), 8)
            for t in range(TT):
                act.wait_ge(S("unit_mm"), GROW + t + 1)
                a(nc.scalar.activation(expg[:, 4 * t:4 * t + 4, :], bank(2 + t).rearrange("p (h c) -> p h c", h=4),
                                       ACT.Exp, bias=zero[:]), "expg_ready")
            proj_out(8)
            conv_silu(0)
            conv_silu(4)
            for t in range(TT):
                act.wait_ge(S("dec_arg"), t + 1)
                a(nc.scalar.activation(dec[:, 4 * t:4 * t + 4, :], dec[:, 4 * t:4 * t + 4, :], ACT.Exp,
                                       bias=zero[:]), "dec_ready")
            proj_out(9)
            act.wait_ge(S("qk_mm"), 1)
            a(nc.scalar.activation(dl[:, 104:120], bank(4)[:, 0:16], ACT.Sqrt, bias=eps[:]), "qk_root")
            proj_out(10)
            act.wait_ge(S("k_scales"), 1)
            for t in range(TT):
                act.wait_ge(S("k_used"), 4 * t + 4)
                for hd in range(GH):
                    u = 4 * t + hd
                    ins = nc.scalar.activation(kdec[:, u, :], bank(6 + t)[:, hd * P:hd * P + P], ACT.Copy,
                                               scale=dl[:, 88 + u:89 + u])
                a(ins, "kdec_ready")
            proj_out(11)
            conv_silu(8)
            proj_out(12)
            for t in range(TT):
                act.wait_ge(S("unit_mm"), VTOK + t + 1)
                for hd in range(GH):
                    u = 4 * t + hd
                    ins = nc.scalar.activation(vb[:, u, :], bank(6 + t)[:, hd * P:hd * P + P], ACT.Copy,
                                               scale=dl[:, 40 + u:41 + u])
                a(ins, "v_used")
            for i in range(13, 16):
                proj_out(i)
            for t in range(TT):
                act.wait_ge(S("merge0_mm"), t + 1)
                a(nc.scalar.activation(tm[:, 4 * t:4 * t + 4, :], bank(4 + t).rearrange("p (h c) -> p h c", h=4),
                                       ACT.Copy), "tm0_ready")
            for lv in range(1, LEVELS):
                for t in range(TT):
                    act.wait_ge(S("merge_p_mm"), TT * (lv - 1) + t + 1)
                    a(nc.scalar.activation(pm[:, 4 * t:4 * t + 4, :], bank(t).rearrange("p (h c) -> p h c", h=4),
                                           ACT.Copy), "pm_ready")
            for t in range(TT):
                act.wait_ge(S("wt_mm"), t + 1)
                a(nc.scalar.activation(wtn[:, 4 * t:4 * t + 4, :], bank(4 + t).rearrange("p (h c) -> p h c", h=4),
                                       ACT.Copy), "wt_ready")
            proj_out(16)
            for n in range(NCH):
                q = slice(64 * (n % 2), 64 * (n % 2) + 64)
                act.wait_ge(S("vnew_mm"), n + 1)
                if n >= 2:
                    act.wait_ge(S("out_mm"), n - 1)
                    act.wait_ge(S("state_mm"), n - 1)
                a(nc.scalar.activation(vnew[q], bank(n % 2)[q].rearrange("p (h c) -> p h c", h=4), ACT.Copy),
                  "vnew_ready")
                proj_out(17 + 2 * n)
                act.wait_ge(S("out_mm"), n + 1)
                a(nc.scalar.activation(o_t[:, :, 64 * n:64 * n + 64],
                                       bank(2 + n % 2)[:, 0:256].rearrange("p (h c) -> p h c", h=4), ACT.Copy), "o_ready")
                proj_out(18 + 2 * n)
            proj_out(25)
            proj_out(26)
            act.wait_ge(S("o_ms"), 1)
            a(nc.scalar.activation(dl[:, 128:136], dl[:, 128:136], ACT.Sqrt, bias=eps[:], scale=1.0 / 128), "o_root")
            proj_out(27)
            for m in range(KD - 1):
                w_hi()
            norm_root(3)
            w_hi()
            shifted_parts(3, mod2, 3)
            for f in range(NFF):
                act.wait_ge(S("ff_gate_mm"), f + 1)
                if f >= 4:
                    act.wait_ge(S("hff_used"), f - 3)
                a(nc.scalar.activation(sff[:, (f // 2) % 2, f % 2, :], bank(2 * (f % 2) + 2)[:, 0:T], ACT.Silu,
                                       bias=zero[:]), "sff_ready")
                w_hi()
                w_hi()
            for p in range(DOWN2 + 2, len(PIECES)):
                w_hi()
            norm_root(4)

        @block.vector
        def _(dve):
            def v(ins, name="dve_step"):
                ins.then_inc(S(name), 1)
                count[name] += 1
                dve.wait_ge(S(name), count[name])

            tt, stt, ts = nc.vector.tensor_tensor, nc.vector.scalar_tensor_tensor, nc.vector.tensor_scalar

            nc.vector.memset(zero[:], 0.0).then_inc(S("dve_step"), 1)
            nc.vector.memset(one[:], 1.0).then_inc(S("dve_step"), 1)
            nc.vector.memset(eps[:], EPS).then_inc(S("dve_step"), 1)
            nc.vector.memset(ones[:], 1.0).then_inc(S("dve_step"), 1)
            nc.vector.memset(upad[:, :, 0:CONV_W - 1], 0.0).then_inc(S("dve_step"), 1)
            count["dve_step"] += 5
            dve.wait_ge(S("dve_step"), 5)
            v(nc.vector.memset(score[:], 0.0), "init")

            def d(ins, name):
                ins.then_inc(S(name), 1)
                count[name] += 1

            def add_square(n, k):
                total, sq = xsq[n][:, 0, :], xsq[n][:, 2, :]
                if k == 0:
                    v(tt(total, x[:, k, :], x[:, k, :], ALU.mult))
                else:
                    v(tt(sq, x[:, k, :], x[:, k, :], ALU.mult))
                    v(tt(total, total, sq, ALU.add), "sq_ready" if k == KD - 1 else "dve_step")

            def inverse(n):
                dve.wait_ge(S("root_ready"), 2 * n + 2)
                v(nc.vector.reciprocal(rcol[:, 0:2], rcol[:, 0:2]), "rcol_ready")

            def scaled(dst, n, gains, name="scaled"):
                dve.wait_ge(S("rrow_mm"), n + 1)
                for k in range(KD):
                    d(stt(dst[:, k, :], x[:, k, :], gains[:, k:k + 1], bank(0)[:, 0:T], ALU.mult, ALU.mult), name)

            def gemv_col(r):
                mod, bias, rr = (mod1, "mod_b", r) if r < 3 else (mod2, "ada_b", r - 3)
                dve.wait_ge(S("modT_mm"), r + 1)
                for j in range(4):
                    o = slice(16 * rr + 4 * j, 16 * rr + 4 * j + 4)
                    v(tt(mod[:, o], bank(2).rearrange("p (s q) -> p s q", s=4)[:, :, 32 * j],
                         col(bias, 16 * rr + 4 * j, 4), ALU.add), "mod_ready")
                if rr != 1:
                    n = 2 * (r // 3) + rr // 2
                    sc = mod[:, 8:16] if rr == 0 else mod[:, 32:40]
                    v(stt(gain[:, n, :], sc, 1.0, col(("n1", "n2", "n1b", "n2b")[n], 0, 8), ALU.add, ALU.mult))

            dve.wait_ge(S("x_in"), 16)
            for k in range(KD):
                add_square(0, k)
            inverse(0)
            dve.wait_ge(S("small_in"), 32)
            gemv_col(0)
            scaled(h, 0, gain[:, 0, :])
            dve.wait_ge(S("proj_ev"), AFTER["g", 1])
            v(tt(upad[:, :, CONV_W - 1:UPW], aval, cgate, ALU.mult), "u_ready")

            def conv(lo, hi):
                for j in range(lo, hi):
                    for c in range(2):
                        src, k = upad[:, c, j:j + T], col("conv_k", c * CONV_W + j)
                        if j == 0:
                            d(ts(cacc[:, c, :], src, k, col("conv_b", c), ALU.mult, ALU.add), f"conv_step{c}")
                        else:
                            dve.wait_ge(S(f"conv_step{c}"), j)
                            d(stt(cacc[:, c, :], src, k, cacc[:, c, :], ALU.mult, ALU.add), f"conv_step{c}")

            conv(0, 24)
            dve.wait_ge(S("proj_ev"), AFTER["lat", 2])
            v(tt(rel[:, 0:2, :], cq, cq, ALU.mult))
            v(tt(rel[:, 2, :], ckv, ckv, ALU.mult), "lat_sq")
            conv(24, CONV_W)
            dve.wait_ge(S("lat_root"), 2)
            v(nc.vector.reciprocal(rst[:, 0, :], rst[:, 0, :]))
            v(nc.vector.reciprocal(rst[:, 1, :], rst[:, 1, :]))
            for c in range(2):
                v(stt(cq[:, c, :], cq[:, c, :], col("q_g", c), rst[:, 0, :], ALU.mult, ALU.mult), "lat_ready")
            v(stt(ckv, ckv, col("kv_g"), rst[:, 1, :], ALU.mult, ALU.mult), "lat_ready")
            gemv_col(1)

            def index_scores(qb):
                w = P if qb == 0 else T
                for n in range(8 * qb, 8 * qb + 8):
                    dve.wait_ge(S("proj_ev"), AFTER["ix", n])
                    v(stt(score[:, qb, 0:w], rel[:, n % 2, 0:w], wi[:, qb, n % 8:n % 8 + 1], score[:, qb, 0:w],
                          ALU.mult, ALU.add), "idx_acc")

            def top(qb):
                sc = score[:, qb, 0:P if qb == 0 else T]
                m = aconst[:, qb, 0:P if qb == 0 else T]
                v(stt(sc, sc, IDX_SCALE, m, ALU.mult, ALU.add))
                for _ in range(TOPK // 8):
                    v(nc.vector.max(top8, sc))
                    v(nc.vector.match_replace(sc, top8, sc, TAKEN))
                v(ts(m, sc, -2.0e38, MASKED, ALU.is_gt, ALU.mult))

            def masked(gi):
                qb, w, buf = gi // 2, P if gi < 2 else T, pbuf[gi % 2]
                dve.wait_ge(S("lg_mm"), gi + 1)
                if gi >= 2:
                    dve.wait_ge(S("pT_mm"), (1, 2)[gi - 2])
                v(stt(buf[:, :, 0:w], psum[3][:].rearrange("p a (b s) -> p (a b) s", b=2)[:, :, 0:w], ATT_SCALE,
                      selb[:, qb, 0:w].unsqueeze(1).to_broadcast([P, 4, w]), ALU.mult, ALU.add), "lg_used")
                v(nc.vector.tensor_reduce(mx[gi % 2], buf[:, :, 0:w], AX, ALU.max))
                v(nc.vector.tensor_scalar_mul(mx[gi % 2], mx[gi % 2], -1.0), "max_ready")

            def normalized(gi):
                w, buf = P if gi < 2 else T, pbuf[gi % 2]
                dve.wait_ge(S("exp_done"), 4 * (gi + 1))
                v(nc.vector.reciprocal(rsum, ssum[:, 4 * (gi % 2):4 * (gi % 2) + 4]))
                v(tt(buf[:, :, 0:w], buf[:, :, 0:w], rsum.unsqueeze(2).to_broadcast([P, 4, w]), ALU.mult), "p_ready")

            index_scores(0)
            dve.wait_ge(S("att_in"), 32)
            top(0)
            index_scores(1)
            masked(0)
            masked(1)
            dve.wait_ge(S("cstat_mm"), 1)
            for c in range(2):
                v(stt(cacc[:, c, :], bank(0)[:, 0:T], -1.0 / 256, cacc[:, c, :], ALU.mult, ALU.add))
            normalized(0)
            top(1)
            normalized(1)
            masked(2)
            v(tt(csq, cacc, cacc, ALU.mult), "csq_ready")
            gemv_col(2)
            masked(3)
            normalized(2)
            normalized(3)
            dve.wait_ge(S("cvar_root"), 1)
            v(nc.vector.reciprocal(rst[:, 1, :], rst[:, 1, :]))
            v(tt(cacc, cacc, rst[:, 1, :].unsqueeze(1).to_broadcast([P, 2, T]), ALU.mult), "cnorm_ready")
            gemv_col(3)

            def residual(n, gate, after=lambda m: None, before=lambda m: None):
                for m in range(KD):
                    before(m)
                    dve.wait_ge(S("res_mm"), KD * n + m + 1)
                    v(stt(x[:, m, :], bank(6 + m % 2)[:, 0:T], gate[:, m:m + 1], x[:, m, :], ALU.mult, ALU.add),
                      "res_used")
                    add_square((1, 3, 4)[n], m)
                    after(m)

            residual(0, mod1[:, 16:24], lambda m: gemv_col(4) if m == 2 else gemv_col(5) if m == 6 else None)

            inverse(1)
            scaled(h2, 1, gain[:, 1, :])
            lg = rt[:, 0:72].rearrange("p (t e) -> p t e", t=TT)
            glog, elog = lg[:, :, 0:4], lg[:, :, 4:36].rearrange("p t (g e) -> p t g e", g=4)
            gex = rt[:, 72:80].rearrange("p (t g) -> p t g", t=TT)
            goh = rt[:, 80:88].rearrange("p (t g) -> p t g", t=TT)
            gmax, gp, pri = rt[:, 88:90], rt[:, 90:92], rt[:, 92:94]
            esel = rt[:, 96:112].rearrange("p (t e) -> p t e", t=TT)
            oh = [rt[:, 112 + 16 * i:128 + 16 * i].rearrange("p (t e) -> p t e", t=TT) for i in range(2)]
            emax = [rt[:, 144:146], rt[:, 146:148]]
            gap, den, wg = rt[:, 160:162], rt[:, 162:164], [rt[:, 164:166], rt[:, 166:168]]
            tmp8 = rt[:, 176:192].rearrange("p (t e) -> p t e", t=TT)
            asg = rt[:, 192:256].rearrange("p (t g e) -> p t g e", t=TT, g=4)
            gat = rt[:, 256:320].rearrange("p (t g e) -> p t g e", t=TT, g=4)
            tmp32 = rt[:, 320:384].rearrange("p (t g e) -> p t g e", t=TT, g=4)
            acc1 = rt[:, 416:424]

            def wide(a, n):
                return a.unsqueeze(2).to_broadcast([P, TT, n])

            def first_max(src, top, out_oh, n):
                v(nc.vector.tensor_reduce(top, src, AX, ALU.max))
                v(tt(out_oh, src, wide(top, n), ALU.is_equal))
                v(tt(out_oh, out_oh, cst("prio")[:, 0:n].unsqueeze(1).to_broadcast([P, TT, n]), ALU.mult))
                v(nc.vector.tensor_reduce(pri, out_oh, AX, ALU.max))
                v(tt(out_oh, out_oh, wide(pri, n), ALU.is_equal))

            dve.wait_ge(S("router_mm"), 1)
            for t in range(TT):
                v(tt(lg[:, t, :], bank((1, 4)[t])[:, 0:36], col("rbias", 0, 36), ALU.add))
            first_max(glog, gmax, goh, 4)
            v(tt(gex, glog, wide(gmax, 4), ALU.subtract), "router_in")
            v(tt(tmp32, elog, goh.unsqueeze(3).to_broadcast([P, TT, 4, 8]), ALU.mult))
            v(tt(esel, tmp32[:, :, 0, :], tmp32[:, :, 1, :], ALU.add))
            v(tt(esel, esel, tmp32[:, :, 2, :], ALU.add))
            v(tt(esel, esel, tmp32[:, :, 3, :], ALU.add))
            first_max(esel, emax[0], oh[0], 8)
            v(stt(tmp8, oh[0], MASKED, esel, ALU.mult, ALU.add))
            first_max(tmp8, emax[1], oh[1], 8)
            v(tt(gap, emax[1], emax[0], ALU.subtract), "router_in")
            v(tt(tmp8, oh[0], oh[1], ALU.add))
            v(tt(asg, goh.unsqueeze(3).to_broadcast([P, TT, 4, 8]), tmp8.unsqueeze(2).to_broadcast([P, TT, 4, 8]),
                 ALU.mult), "asg_ready")
            dve.wait_ge(S("router_exp"), 1)
            v(nc.vector.tensor_reduce(gp, gex, AX, ALU.add))
            v(nc.vector.reciprocal(gp, gp))
            dve.wait_ge(S("router_exp"), 2)
            v(nc.vector.tensor_scalar_add(den, gap, 1.0))
            v(nc.vector.reciprocal(den, den))
            v(tt(wg[0], den, gp, ALU.mult))
            v(tt(wg[1], wg[0], gap, ALU.mult))
            v(tt(oh[0], oh[0], wide(wg[0], 8), ALU.mult))
            v(tt(oh[1], oh[1], wide(wg[1], 8), ALU.mult))
            v(tt(oh[0], oh[0], oh[1], ALU.add))
            v(tt(gat, goh.unsqueeze(3).to_broadcast([P, TT, 4, 8]), oh[0].unsqueeze(2).to_broadcast([P, TT, 4, 8]),
                 ALU.mult))
            dve.wait_ge(S("rank_mm"), 1)
            a2, g2 = [rt[:, o:o + 64].rearrange("p (t e) -> p t e", t=TT) for o in (192, 256)]
            rk = rt[:, 320:384].rearrange("p (t e) -> p t e", t=TT)
            v(stt(rk, bank(5)[:, 0:64].rearrange("p (t e) -> p t e", t=TT), 1.0, a2, ALU.add, ALU.mult))
            v(nc.vector.tensor_copy(gate_s.rearrange("p t (s e) -> p t s e", s=4),
                                    g2.unsqueeze(2).to_broadcast([P, TT, 4, E])))
            for s in range(4):
                v(nc.vector.tensor_scalar_add(rank_s[:, :, E * s:E * s + E], rk, -1.0 - CAP * s))
            v(nc.vector.reduce_max(acc1[:, 0:1], bank(5)[:, 64:96], AX))
            for s in range(1, 4):
                v(ts(acc1[:, s:s + 1], acc1[:, 0:1], CAP * s + 0.5, None, ALU.is_gt))
            v(stt(acc1[:, 1:2], acc1[:, 1:2], 1.0, acc1[:, 2:3], ALU.add, ALU.add))
            v(tt(acc1[:, 1:2], acc1[:, 1:2], acc1[:, 3:4], ALU.add))
            v(nc.vector.tensor_copy(sweeps[:], acc1[:, 1:2]), "sweeps_ready")
            dve.sem_inc(S("moe_add"), 4)

            def dve_group(g):
                dve.wait_ge(S("gath_mm"), g * 10 + 1)
                for j in range(4):
                    for t in range(TT):
                        nc.vector.tensor_tensor(
                            s_oh[:, t, 2 * j * CAP:(2 * j + 2) * CAP].rearrange("p (e s) -> p e s", e=2),
                            rank_s[:, t, bass.ds(g * 8 + 2 * j, 2)].unsqueeze(2).to_broadcast([P, 2, CAP]),
                            cst("iota").unsqueeze(1).to_broadcast([P, 2, CAP]), ALU.is_equal).then_inc(S("onehot"), 1)
                dve.wait_ge(S("onehot"), g * 8 + 8)
                for t in range(TT):
                    nc.vector.tensor_tensor(
                        s_gt[:, t, :].rearrange("p (e s) -> p e s", e=EG),
                        s_oh[:, t, :].rearrange("p (e s) -> p e s", e=EG),
                        gate_s[:, t, bass.ds(g * 8, 8)].unsqueeze(2).to_broadcast([P, EG, CAP]),
                        ALU.mult).then_inc(S("gated"), 1)
                for j in range(4):
                    dve.wait_ge(S("up_mm"), g * 8 + (AHEAD + 2 * j + 2))
                    dve.wait_ge(S("sil_ready"), g * 4 + (j + 1))
                    nc.vector.tensor_tensor(hid, sil, bank(1), ALU.mult).then_inc(S("hid_ready"), 1)
                    for c in range(4):
                        dve.wait_ge(S("comb_mm"), g * 16 + (4 * j + c + 1))
                        dve.wait_ge(S("moe_add"), g * 16 + (4 * j + c + 4))
                        for q in range(2):
                            m = 2 * c + q
                            ins = nc.vector.scalar_tensor_tensor(
                                x[:, m, :], bank(4 + c % 2)[:, q * T:q * T + T], mod1[:, 40 + m:41 + m], x[:, m, :],
                                ALU.mult, ALU.add)
                        ins.then_inc(S("moe_add"), 1)

            dve.wait_ge(S("mod_ready"), 24)
            n_sw = dve.value_load(sweeps[0:1, 0:1], min_val=1, max_val=4)
            with dve.Fori(0, 4) as g:
                dve_group(g)
            with dve.If(n_sw > 1):
                with dve.Fori(4, n_sw * 4) as g:
                    dve_group(g)
            for k in range(1, KD):
                dve.wait_ge(S("sqx_ready"), 2 * k + 2)
                so_far = sq_xn[:, 0, :, :] if k == 1 else xsq[2][:, 0:2, :]
                v(tt(xsq[2][:, 0:2, :], so_far, sq_xn[:, k, :, :], ALU.add), "sq_ready" if k == KD - 1 else "dve_step")

            dve.wait_ge(S("root_ready"), 6)
            v(nc.vector.reciprocal(rcol[:, 0:2], rcol[:, 0:2]))
            v(tt(rcol[:, 4:6], rcol[:, 0:2], rcol[:, 0:2], ALU.mult))
            dve.wait_ge(S("msn_mm"), 1)
            for t in range(TT):
                v(tt(rcol[:, 2 + t:3 + t], rcol[:, 4 + t:5 + t], bank(1 + t)[:, 0:1], ALU.mult),
                  "ms3_in" if t else "dve_step")
            v(tt(gnf, gain[:, 2, :], col("nf", 0, 8), ALU.mult))
            dve.wait_ge(S("root3_ready"), 1)
            v(nc.vector.reciprocal(rcol[:, 2:4], rcol[:, 2:4]))
            v(tt(rcol[:, 2:4], rcol[:, 2:4], rcol[:, 0:2], ALU.mult), "rcol_ready")
            split = itertools.count()

            def w_lo():
                p = next(split)
                w, hi, lo = piece(p)
                dve.wait_ge(S("w_hi"), p + 1)
                d(tt(lo, w, hi.bitcast(fp32), ALU.subtract), "w_lo")

            def parts(value, hi, lo, name):
                v(nc.vector.tensor_copy(hi, value))
                v(tt(lo, value, hi.bitcast(fp32), ALU.subtract), name)

            def input_parts(n):
                for k in range(KD):
                    dve.wait_ge(S("h_ready"), n * KD + k + 1)
                    hi = g_hi[:, k, :].bitcast(fp32)
                    if n == 2:
                        dve.wait_ge(S("ab_mm"), k + 1)
                        d(tt(g_lo[:, k, :], g_in[:, k, :], hi, ALU.subtract), "parts_ready")
                    else:
                        d(stt(g_lo[:, k, :], g_in[:, k, :], mod2[:, 24 + k:25 + k], hi, ALU.add, ALU.subtract),
                          "parts_ready")

            scaled(g_in, 2, gnf)
            w_lo()
            input_parts(2)
            for k in range(KD):
                d(stt(x[:, k, :], x[:, k, :], col("nf", k), bank(0)[:, T:2 * T], ALU.mult, ALU.mult), "x_normed")
            w_lo()
            v(nc.vector.memset(raw[:, :, 0:3], 0.0), "raw_pad")
            v(nc.vector.memset(scp[:, :, 0:2], 0.0))
            def qkv_conv(m, ahead=True):
                if ahead:
                    w_lo()
                dve.wait_ge(S("proj2_ev"), m + 1)
                for j in range(3):
                    src, k = raw[:, m, j:j + T], col("gconv", 4 * m + j)
                    v(stt(qkv[:, m, :], src, k, qkv[:, m, :], ALU.mult, ALU.add),
                      "gconv_done" if j == 2 else "dve_step")

            def short_conv(i):
                dve.wait_ge(S("proj2_ev"), PROJ2.index(("h", i)) + 1)
                b, c, p = scb[:, i % 2, :], scc[:, i % 2, :], scp[:, i % 2, :]
                v(tt(p[:, 2:2 + T], p[:, 2:2 + T], c, ALU.mult))
                o = g_y[:, 4 + i, :]
                v(nc.vector.tensor_scalar_mul(o, p[:, 0:T], col("sconv", 3 * i)))
                v(stt(o, p[:, 1:1 + T], col("sconv", 3 * i + 1), o, ALU.mult, ALU.add))
                v(stt(o, p[:, 2:2 + T], col("sconv", 3 * i + 2), o, ALU.mult, ALU.add))
                v(tt(o, o, b, ALU.mult), "short_done")
                parts(o, y_hi[1][:, i, :], y_lo[:, 4 + i, :], "y2_ready")

            ab = dl[:, 0:16].rearrange("p (t c) -> p t c", t=TT)
            ap, sp_, am = [dl[:, o:o + 8].rearrange("p (t h) -> p t h", t=TT) for o in (16, 24, 32)]
            be = dl[:, 40:48].rearrange("p (t h) -> p t h", t=TT)
            na = dl[:, 48:52]
            gg = dl[:, 56:64].rearrange("p (t h) -> p t h", t=TT)
            dve.wait_ge(S("ab_ready"), 2)
            v(tt(ap, ab[:, :, 0:4], col("dt", 0, 4).unsqueeze(1).to_broadcast([P, TT, 4]), ALU.add))
            v(nc.vector.tensor_scalar_mul(sp_, ap, -1.0))
            v(tt(sp_, sp_, ap, ALU.min))
            v(nc.vector.tensor_scalar_max(am, ap, 0.0))
            v(nc.vector.tensor_copy(be, ab[:, :, 4:8]), "sp_in")
            qkv_conv(0)
            qkv_conv(1)
            dve.wait_ge(S("sp_exp"), 4)
            v(tt(sp_, sp_, am, ALU.add))
            v(nc.vector.tensor_scalar_mul(na, na, -1.0))
            v(tt(gg, sp_, na.unsqueeze(1).to_broadcast([P, TT, 4]), ALU.mult), "g_ready")
            v(nc.vector.tensor_scalar_add(be, be, 1.0))
            v(nc.vector.reciprocal(be, be))
            for m in range(2, 5):
                qkv_conv(m)
            dve.wait_ge(S("gcum_mm"), 1)
            G, GL = dl[:, 64:72], dl[:, 72:80]
            v(nc.vector.tensor_copy(G, bank(6)[:, 0:8]))
            v(tt(GL, bank(6)[:, 8:16], G, ALU.subtract), "gcol_ready")
            eG, eGL, beta = dl[:, 80:88], dl[:, 88:96], dl[:, 40:48]
            nbe, rq, rk, brk = dl[:, 96:104], dl[:, 104:112], dl[:, 112:120], dl[:, 120:128]
            for m in range(5, 8):
                qkv_conv(m)
            for t in range(TT):
                dve.wait_ge(S("unit_mm"), GROW + t + 1)
                dve.wait_ge(S("expg_ready"), t + 1)
                for hd in range(GH):
                    u = 4 * t + hd
                    v(stt(dec[:, u, :], bank(2 + t)[:, hd * P:hd * P + P], G[:, u:u + 1], mask_c, ALU.subtract, ALU.add),
                      "dec_arg" if hd == 3 else "dve_step")
            w_lo()
            for i in range(2):
                dve.wait_ge(S("qkv_ready"), 4 * i + 4)
                k = slice(4 * i, 4 * i + 4)
                v(tt(sq8[:, k, :], qkv[:, k, :], qkv[:, k, :], ALU.mult), "sq8_ready")
            qkv_conv(8, ahead=False)
            qkv_conv(9)
            dve.wait_ge(S("qk_root"), 1)
            v(nc.vector.reciprocal(dl[:, 104:120], dl[:, 104:120]))
            v(nc.vector.tensor_scalar_mul(rq, rq, float(128 ** -0.5)))
            v(tt(brk, beta, rk, ALU.mult), "brk_ready")
            dve.wait_ge(S("gexp_ready"), 1)
            v(tt(nbe, brk, eG, ALU.mult))
            v(nc.vector.tensor_scalar_mul(nbe, nbe, -1.0))
            v(tt(eGL, eGL, rk, ALU.mult), "k_scales")
            for t in range(TT):
                us = slice(4 * t, 4 * t + 4)
                dve.wait_ge(S("dec_ready"), t + 1)
                v(tt(dec[:, us, :], dec[:, us, :], rk[:, us].unsqueeze(2).to_broadcast([P, 4, P]), ALU.mult))
            for t in range(TT):
                dve.wait_ge(S("unit_mm"), KTOK + t + 1)
                for hd in range(GH):
                    u = 4 * t + hd
                    src = bank(6 + t)[:, hd * P:hd * P + P]
                    d(nc.vector.tensor_scalar_mul(kbe[:, u, :], src, nbe[:, u:u + 1]), "k_used")
            for t in range(TT):
                us = slice(4 * t, 4 * t + 4)
                dve.wait_ge(S("unit_mm"), KK + t + 1)
                v(tt(lt[:, us, :], bank(4 + t).rearrange("p (h c) -> p h c", h=4), dec[:, us, :], ALU.mult), "kk_used")
            qkv_conv(10)
            qkv_conv(11)
            for t in range(TT):
                us = slice(4 * t, 4 * t + 4)
                dve.wait_ge(S("unit_mm"), BROW + t + 1)
                v(tt(lt[:, us, :], lt[:, us, :], bank(2 + t).rearrange("p (h c) -> p h c", h=4), ALU.mult),
                  "lt_ready" if t == 1 else "dve_step")
            for t in range(TT):
                us = slice(4 * t, 4 * t + 4)
                v(tt(ttm[:, us, :], lt[:, us, :], gcon[:, 3, :].unsqueeze(1).to_broadcast([P, 4, P]), ALU.mult))
                v(tt(ttm[:, us, :], ident.unsqueeze(1).to_broadcast([P, 4, P]), ttm[:, us, :], ALU.subtract), "ttm_ready")
            w_lo()
            w_lo()
            for t in range(TT):
                us = slice(4 * t, 4 * t + 4)
                dve.wait_ge(S("unit_mm"), KQ + t + 1)
                v(tt(attn_t[:, us, :], bank(4 + t).rearrange("p (h c) -> p h c", h=4), dec[:, us, :], ALU.mult),
                  "attn_ready")
            w_lo()
            w_lo()
            for lv in range(1, LEVELS):
                for t in range(TT):
                    us = slice(4 * t, 4 * t + 4)
                    if lv == 1:
                        dve.wait_ge(S("tm0_ready"), t + 1)
                    if lv < LEVELS - 1:
                        dve.wait_ge(S("merge_t_mm"), TT * (lv - 1) + t + 1)
                        v(tt(tm[:, us, :], tm[:, us, :], bank(4 + t).rearrange("p (h c) -> p h c", h=4), ALU.subtract),
                          "tm_ready")
                    dve.wait_ge(S("merge_tt_mm"), TT * (lv - 1) + t + 1)
                    v(tt(ttm[:, us, :], ttm[:, us, :], bank(2 + t).rearrange("p (h c) -> p h c", h=4), ALU.subtract),
                      "ttm_ready")
            for t in range(TT):
                for hd in range(GH):
                    v(tt(qkv[:, hd, t * P:t * P + P], qkv[:, hd, t * P:t * P + P], expg[:, 4 * t + hd, :], ALU.mult),
                      "qdec_ready")
            w_lo()
            for n in range(NCH - 1):
                w_lo()
                dve.wait_ge(S("state_mm"), n + 1)
                dve.wait_ge(S("out_mm"), n + 1)
                for hd in range(GH):
                    src = bank(6 + n % 2)[:, hd * P:hd * P + P]
                    if n == 0:
                        v(nc.vector.tensor_copy(state[:, hd, :], src), "state_ready")
                    else:
                        u = 4 * (n // 2) + hd
                        last = 64 * (n % 2) + 63
                        v(stt(state[:, hd, :], state[:, hd, :], expg[:, u, last:last + 1], src, ALU.mult, ALU.add),
                          "state_ready")
                w_lo()
                if n > 0:
                    short_conv(n - 1)
            w_lo()
            dve.wait_ge(S("o_ready"), NCH)
            v(tt(o_sq, o_t, o_t, ALU.mult), "osq_ready")
            w_lo()
            short_conv(2)
            w_lo()
            for i in range(2):
                k = slice(2 * i, 2 * i + 2)
                v(stt(o_t[:, k, :], o_t[:, k, :], col("gnorm"), zg[:, k, :], ALU.mult, ALU.mult))
            fac = dl[:, 128:136]
            dve.wait_ge(S("osum_mm"), 1)
            v(tt(fac, bank(7)[:, 0:8], rq, ALU.mult))
            v(tt(fac, fac, rq, ALU.mult), "o_ms")
            dve.wait_ge(S("o_root"), 1)
            v(nc.vector.reciprocal(fac, fac))
            v(tt(fac, fac, rq, ALU.mult), "fac_ready")
            w_lo()
            short_conv(3)
            w_lo()
            dve.wait_ge(S("fac_mm"), 1)
            for i in range(2):
                k = slice(2 * i, 2 * i + 2)
                v(tt(g_y[:, k, :], o_t[:, k, :], bank(2 + i).rearrange("p (a t) -> p a t", a=2), ALU.mult))
                parts(g_y[:, k, :], y_hi[0][:, k, :], y_lo[:, k, :], "y2_ready")
            dve.sem_inc(S("delta_done"), 1)
            dve.wait_ge(S("x_normed"), KD)
            residual(1, mod2[:, 16:24], before=lambda m: w_lo() if m < KD - 1 else None)
            inverse(3)
            scaled(f_in, 3, gain[:, 3, :])
            input_parts(3)
            w_lo()
            for f in range(NFF):
                w_lo()
                dve.wait_ge(S("sff_ready"), f + 1)
                dve.wait_ge(S("ff_up_mm"), f + 1)
                v(tt(hff[:, f, :], sff[:, (f // 2) % 2, f % 2, :], bank(2 * (f % 2) + 3)[:, 0:T], ALU.mult), "hff_used")
                parts(hff[:, f, :], hf_hi[:, f, :], hf_lo[:, f, :], "hff_ready")
                w_lo()
            residual(2, mod2[:, 40:48],
                     before=lambda m: [w_lo() for p in range(DOWN2 + 3 * m + 2, min(DOWN2 + 3 * m + 5, len(PIECES)))])
            inverse(4)
            scaled(f_h, 4, col("nfb", 0, 8), "out_ready")

        @block.tensor
        def _(pe):
            mm = nc.tensor.matmul

            def sums(n):
                pe.wait_ge(S("sq_ready"), n + 1)
                for t in range(TT):
                    last = mm(bank(STAT[t])[:, 0:1], xsq[n][:, 0, t * P:t * P + P], ones[:, 0:1], start=True, stop=True)
                last.then_inc(S("ms_mm"), 1)

            def spread(cols_at, to, inc=True):
                for t in range(TT):
                    last = mm(bank(0)[:, to + t * P:to + t * P + P],
                              rcol[:, cols_at + t:cols_at + t + 1].to_broadcast([P, P]), ident, start=True, stop=True)
                if inc:
                    last.then_inc(S("rrow_mm"), 1)

            def gemv(r):
                c = cact[:, r // 3, :]
                pe.wait_ge(S("cact_ready"), 2)
                if r > 0:
                    pe.wait_ge(S("modrow_ready"), r)
                for k in range(KD):
                    n = PASS[r][k // 4]
                    s = PRE_SLOT[n]
                    if k % 4 == 0:
                        pe.wait_ge(S(f"loaded{s}"), landed(n))
                    w = ring[:, s, :].rearrange("p (k n) -> p k n", k=4)[:, k % 4, :]
                    for j in range(4):
                        last = mm(bank(1)[32 * j:32 * j + 32, :], c[:, k:k + 1].to_broadcast([P, 32]),
                                  w[:, 512 * j:512 * j + 512], start=k == 0, stop=k == KD - 1)
                last.then_inc(S("gemv_mm"), 1)

            def gemv_t(r):
                pe.wait_ge(S("modrow_ready"), r + 1)
                if r > 0:
                    pe.wait_ge(S("mod_ready"), 4 * r)
                for s in range(4):
                    last = nc.tensor.transpose(bank(2)[:, s * P:s * P + P], modrow[r][:, s * P:s * P + P], ident)
                last.then_inc(S("modT_mm"), 1)

            sums(0)
            gemv(0)
            pe.wait_ge(S("small_in"), 32)
            gemv_t(0)
            pe.wait_ge(S("rcol_ready"), 1)
            spread(0, 0)

            WB = 776
            def z_chunk(i, s, width, at):
                w = ring[:, s, 0:KD * width].rearrange("p (k n) -> p k n", k=KD)
                for k in range(KD):
                    if i == 0:
                        pe.wait_ge(S("h_ready"), k + 1)
                    last = mm(bank(3 + i % 2)[:, 0:T], w[:, k, at:at + P], h[:, k, :], start=k == 0, stop=k == KD - 1)
                return last

            def step(i):
                kind, n = SERIES[i]
                if i >= 2:
                    pe.wait_ge(S("proj_ev"), i - 1)
                b = bank(3 + i % 2)
                if kind in ("a", "g", "p"):
                    last = z_chunk(i, 2, WB, P * ({"a": 0, "g": 2, "p": 4}[kind] + n))
                elif kind in ("lat", "ki", "qi"):
                    last = z_chunk(i, 3, 1024, P * ({"ki": 0, "qi": 1, "lat": 5}[kind] + n))
                elif kind == "wi":
                    wb = ring[:, 2, 0:KD * WB].rearrange("p (k n) -> p k n", k=KD)
                    for t in range(TT):
                        for k in range(KD):
                            last = mm(b[:, 8 * t:8 * t + 8], h[:, k, t * P:t * P + P], wb[:, k, 768:776],
                                      start=k == 0, stop=k == KD - 1)
                elif kind == "ix":
                    qb, hd = n // 8, n % 8
                    w, q = P if qb == 0 else T, slice(64 * (hd % 2), 64 * (hd % 2) + 64)
                    pe.wait_ge(S("proj_ev"), AFTER["qi", hd // 2])
                    last = mm(b[:, 0:w], qi[q, hd // 2, qb * P:qb * P + P], ki[q, 0:w], start=True, stop=True)
                elif kind == "q":
                    pe.wait_ge(S("lat_ready"), 3)
                    for k in range(2):
                        last = mm(b[:, 0:T], uq[:, k, n * P:n * P + P], cq[:, k, :], start=k == 0, stop=k == 1)
                elif kind == "qa":
                    q = slice(64 * (n % 2), 64 * (n % 2) + 64)
                    pe.wait_ge(S("proj_ev"), AFTER["q", n // 2])
                    last = mm(b[:, 0:T], uk[q, n // 2, :], qT[q, n // 2, :], start=True, stop=True)
                else:
                    for t in range(TT):
                        last = nc.tensor.transpose(b[:, t * P:t * P + P], ckv[:, t * P:t * P + P], ident)
                last.then_inc(S("proj_mm"), 1)

            pe.wait_ge(S("loaded2"), 16)
            for i in range(AFTER["wi", 0]):
                step(i)
            pe.wait_ge(S("loaded3"), 16)
            for i in range(AFTER["wi", 0], AFTER["ki", 0]):
                step(i)
            pe.wait_ge(S("lat_sq"), 1)
            for c in range(2):
                mm(bank(0)[:, 0:T], ones[:], rel[:, c, :], start=c == 0, stop=c == 1)
            mm(bank(0)[:, T:2 * T], ones[:], rel[:, 2, :], start=True, stop=True).then_inc(S("lat_mm"), 1)
            gemv(1)
            for i in range(AFTER["ki", 0], AFTER["qi", 0]):
                step(i)
            gemv_t(1)
            for i in range(AFTER["qi", 0], AFTER["qi", 3]):
                step(i)
            pe.wait_ge(S("att_in"), 32)
            for i in range(AFTER["qi", 3], AFTER["ct", 0]):
                step(i)

            def logits(gi):
                qb, hh, w = gi // 2, gi % 2, P if gi < 2 else T
                pe.wait_ge(S("proj_ev"), AFTER["qa", 7])
                if gi > 0:
                    pe.wait_ge(S("lg_used"), gi)
                for j in range(4):
                    last = mm(psum[3][:, j // 2, (j % 2) * T:(j % 2) * T + w],
                              qabs[:, 4 * hh + j, qb * P:qb * P + P], ckv[:, 0:w], start=True, stop=True)
                last.then_inc(S("lg_mm"), 1)

            def context(gi):
                nst = 1 if gi < 2 else 2
                pe.wait_ge(S("p_ready"), gi + 1)
                for st in range(nst):
                    n = (0, 1, 2, 4)[gi] + st
                    if n > 0:
                        pe.wait_ge(S("pT_ready"), n)
                    for j in range(4):
                        last = nc.tensor.transpose(bank(5)[:, j * P:j * P + P],
                                                   pbuf[gi % 2][:, j, st * P:st * P + P], ident)
                    last.then_inc(S("pT_mm"), 1)
                if gi > 0:
                    pe.wait_ge(S("ctx_ready"), gi)
                for st in range(nst):
                    pe.wait_ge(S("pT_ready"), (0, 1, 2, 4)[gi] + st + 1)
                    last = mm(bank(4), ctok[:, st, :], pT[:, st, :], start=st == 0, stop=st == nst - 1)
                last.then_inc(S("ctx_mm"), 1)

            gemv(2)
            for i in range(AFTER["ct", 0], len(SERIES)):
                step(i)
            logits(0)
            pe.wait_ge(S("conv_step0"), CONV_W)
            pe.wait_ge(S("conv_step1"), CONV_W)
            pe.wait_ge(S("lat_root"), 2)
            for c in range(2):
                last = mm(bank(0)[:, 0:T], ones[:], cacc[:, c, :], start=c == 0, stop=c == 1)
            last.then_inc(S("cstat_mm"), 1)
            gemv_t(2)
            logits(1)
            for gi in range(4):
                context(gi)
                if gi < 2:
                    logits(gi + 2)
                if gi == 0:
                    gemv(3)
                if gi == 1:
                    pe.wait_ge(S("csq_ready"), 1)
                    for c in range(2):
                        last = mm(bank(0)[:, T:2 * T], ones[:], csq[:, c, :], start=c == 0, stop=c == 1)
                    last.then_inc(S("cstat_mm"), 1)
            gemv_t(3)
            pe.wait_ge(S("ctx_ready"), 4)
            pe.wait_ge(S("ctx_ready"), 4)
            for c in range(4):
                for j in range(2):
                    hd = 2 * c + j
                    last = mm(bank(3 + c // 2)[64 * j:64 * j + 64, (c % 2) * T:(c % 2) * T + T],
                              uv[:, 64 * hd:64 * hd + 64], ctxT[:, hd, :], start=True, stop=True)
                if c % 2:
                    last.then_inc(S("o_mm"), 1)
            pe.wait_ge(S("dpool_ready"), 1)
            pe.wait_ge(S("pT_ready"), 6)
            for gq in range(4):
                q = slice(64 * (gq % 2), 64 * (gq % 2) + 64)
                last = mm(bank(5)[q, (gq // 2) * T:(gq // 2) * T + T], pw[q, gq // 2, :], dpool[q, gq // 2, :],
                          start=True, stop=True)
            last.then_inc(S("pool_mm"), 1)
            def out_product(n, w, src, nk, norm, after=lambda m: None):
                for m in range(KD):
                    if m >= 2:
                        pe.wait_ge(S("res_used"), KD * n + m - 1)
                    for k in range(nk):
                        last = mm(bank(6 + m % 2)[:, 0:T], w(k)[:, m * P:m * P + P], src[:, k, :],
                                  start=k == 0, stop=k == nk - 1)
                    last.then_inc(S("res_mm"), 1)
                    after(m)
                sums(norm)
                pe.wait_ge(S("rcol_ready"), norm + 1)
                spread(0, 0)

            def passes_4_5(m):
                if m == 1:
                    gemv_t(4)
                if m == 2:
                    gemv(5)
                if m == 5:
                    gemv_t(5)

            gemv(4)
            pe.wait_ge(S(f"loaded{PRE_SLOT[8]}"), landed(8))
            pe.wait_ge(S("y1_ready"), 6)
            wo = ring[:, PRE_SLOT[8], :].rearrange("p (k n) -> p k n", k=KD)
            out_product(0, lambda k: wo[:, k, :], y, KD, 1, passes_4_5)

            for k in range(KD):
                pe.wait_ge(S("h_ready"), KD + k + 1)
                for t in range(TT):
                    last = mm(bank((1, 4)[t])[:, 0:36], h2[:, k, t * P:t * P + P], rw[:, k, :],
                              start=k == 0, stop=k == KD - 1)
            last.then_inc(S("router_mm"), 1)
            pe.wait_ge(S("mod_ready"), 24)
            for i in range(4):
                t, half = i // 2, i % 2
                if i >= 2:
                    pe.wait_ge(S("htok_ready"), i - 1)
                for q in range(4):
                    last = nc.tensor.transpose(bank(2 + i % 2)[:, q * P:q * P + P],
                                               h2[:, 4 * half + q, t * P:t * P + P], ident)
                last.then_inc(S("htok_mm"), 1)
            pe.wait_ge(S("asg_ready"), 1)
            asg = [rt[:, 192 + E * t:192 + E * t + E] for t in range(TT)]
            mm(bank(5)[:, 0:32], cst("tri"), asg[0], start=True, stop=True)
            mm(bank(5)[:, 32:64], cst("tri"), asg[1], start=True, stop=False)
            mm(bank(5)[:, 32:64], ones[:], asg[0], start=False, stop=True)
            mm(bank(5)[:, 64:96], ones[:], asg[0], start=True, stop=False)
            mm(bank(5)[:, 64:96], ones[:], asg[1], start=False, stop=True).then_inc(S("rank_mm"), 1)
            pe.wait_ge(S("htok_ready"), 4)
            pe.wait_ge(S("sweeps_ready"), 1)
            pe.sem_inc(S("gath_ev"), 2)
            pe.sem_inc(S("gath_mm"), 1)
            pe.sem_inc(S("up_mm"), AHEAD)
            pe.sem_inc(S("down_mm"), AHEAD)

            def pe_group(g):
                def slot(n):
                    s = EXP_SLOT[n % SLOTS]
                    return s, g * 48 + 16 * (PRE[s] + n // SLOTS + 1)

                def gather(i):
                    pe.wait_ge(S("gath_ev"), g * 10 + (i + 1))
                    b = bank(GATH[i % 2])
                    if i in (4, 5):
                        pe.wait_ge(S("gated"), g * 2 + 2)
                        for q in range(2):
                            for t in range(TT):
                                last = nc.tensor.transpose(
                                    b[:, q * T + t * P:q * T + t * P + P],
                                    s_gt[:, t, (2 * (i - 4) + q) * P:(2 * (i - 4) + q) * P + P], ident)
                    else:
                        j = (0, 1, None, 2, 3)[i // 2]
                        pe.wait_ge(S("onehot"), g * 8 + (2 * j + 2))
                        for q in range(4):
                            k = 4 * (i % 2) + q
                            for t in range(TT):
                                last = mm(b[:, q * P:q * P + P], htok[:, t, k * P:k * P + P],
                                          s_oh[:, t, j * P:j * P + P], start=t == 0, stop=t == 1)
                    last.then_inc(S("gath_mm"), 1)

                for i in range(2):
                    gather(i)
                for j in range(4):
                    pe.wait_ge(S("gath_ev"), g * 10 + ((1, 3, 7, 9)[j] + 3))
                    for i in range(2):
                        s, at = slot(3 * j + i)
                        pe.wait_ge(S(f"loaded{s}"), at)
                        w = ring[:, s, :].rearrange("p (a k f) -> p a k f", a=2, k=KD)
                        for k in range(KD):
                            for e in range(2):
                                lo = (2 * j + e) * CAP
                                last = mm(bank(i)[64 * e:64 * e + 64, :], hsel[:, k, lo:lo + CAP], w[:, e, k, :],
                                          start=k == 0, stop=k == KD - 1)
                        last.then_inc(S("up_mm"), 1)
                    for i in ((2, 3, 4, 5), (6, 7), (8, 9), ())[j]:
                        gather(i)
                    pe.wait_ge(S("hid_ready"), g * 4 + (j + 1))
                    for k in range(KF):
                        last = nc.tensor.transpose(bank(6)[:, k * P:k * P + P], hid[:, k * P:k * P + P], ident)
                    last.then_inc(S("hidT_mm"), 1)
                    s, at = slot(3 * j + 2)
                    pe.wait_ge(S("hidT_ready"), g * 4 + (j + 1))
                    pe.wait_ge(S(f"loaded{s}"), at)
                    w = ring[:, s, :].rearrange("p (a k n) -> p a k n", a=2, k=KF)
                    for half in range(2):
                        if half:
                            pe.wait_ge(S("gath_ev"), g * 10 + ((5, 7, 9, 9)[j] + 3))
                        for k in range(KF):
                            for e in range(2):
                                last = mm(bank(2 + half)[64 * e:64 * e + 64, :], hidT[:, k, 64 * e:64 * e + 64],
                                          w[:, e, k, half * 512:half * 512 + 512], start=k == 0, stop=k == KF - 1)
                        last.then_inc(S("down_mm"), 1)
                    for c in range(4):
                        pe.wait_ge(S("y_ready"), g * 8 + (2 * j + c // 2 + 1))
                        pe.wait_ge(S("moe_add"), g * 16 + (4 * j + c + 3))
                        for q in range(2):
                            m = 2 * c + q
                            last = mm(bank(4 + c % 2)[:, q * T:q * T + T], yex[:, m * P:m * P + P], gT[:, j, :],
                                      start=True, stop=True)
                        last.then_inc(S("comb_mm"), 1)

            n_sw = pe.value_load(sweeps[0:1, 0:1], min_val=1, max_val=4)
            with pe.Fori(0, 4) as g:
                pe_group(g)
            with pe.If(n_sw > 1):
                with pe.Fori(4, n_sw * 4) as g:
                    pe_group(g)

            sums(2)
            for t in range(TT):
                last = mm(bank(1 + t)[:, 0:1], xsq[2][:, 1, t * P:t * P + P], ones[:, 0:1], start=True, stop=True)
            last.then_inc(S("msn_mm"), 1)
            pe.wait_ge(S("rcol_ready"), 3)
            spread(0, T, False)
            spread(2, 0)
            split = itertools.count()

            def split_product(dst, hi, lo, ks, first=True, last=True, ready=None):
                p = next(split)
                _, w_hi, w_lo = piece(p)
                at = min(ks)
                pe.wait_ge(S("w_hi"), p + 1)
                for k in ks:
                    if ready:
                        pe.wait_ge(S(ready(k)[0]), ready(k)[1])
                    mm(dst, w_hi[:, k - at, :], hi(k), start=first and k == ks[0], stop=False)
                    mm(dst, w_hi[:, k - at, :], lo(k), start=False, stop=False)
                pe.wait_ge(S("w_lo"), p + 1)
                for k in ks:
                    ins = mm(dst, w_lo[:, k - at, :], hi(k), start=False, stop=last and k == ks[-1])
                ins.then_inc(S(USED[p][0]), 1)

            def proj2(i):
                if i >= 2:
                    pe.wait_ge(S("proj2_ev"), i - 1)
                if i == 1:
                    pe.wait_ge(S("x_normed"), KD)
                split_product(bank(PROJ2_BANK[i])[:, 0:T], lambda k: g_hi[:, k, :], lambda k: g_lo[:, k, :], range(KD),
                              ready=(lambda k: ("parts_ready", k + 1)) if i == 0 else None)

            def units(outs, product, banks):
                for t in range(TT):
                    for wait in outs:
                        pe.wait_ge(S(wait[0]), wait[1][t])
                    for hd in range(GH):
                        last = product(t, hd, bank(banks + t)[:, hd * P:hd * P + P])
                    last.then_inc(S("unit_mm"), 1)

            def k_(t, hd):
                return qkv[:, 4 + hd, t * P:t * P + P]

            abw = col("abw", 0, 64).rearrange("p (k n) -> p k n", k=KD)
            for k in range(KD):
                pe.wait_ge(S("h_ready"), 2 * KD + k + 1)
                for t in range(TT):
                    last = mm(bank(2 + t)[:, 0:8], g_in[:, k, t * P:t * P + P], abw[:, k, :], start=k == 0,
                              stop=k == KD - 1)
                last.then_inc(S("ab_mm"), 1)
            for i in range(5):
                proj2(i)
            pe.wait_ge(S("g_ready"), 1)
            pe.wait_ge(S("gcon_in"), 16)
            mm(bank(6)[:, 0:8], U_c, dl[:, 56:64], start=True, stop=True)
            mm(bank(6)[:, 8:16], ones_c, dl[:, 56:64], start=True, stop=True).then_inc(S("gcum_mm"), 1)
            for i in range(5, 8):
                proj2(i)
            pe.wait_ge(S("ab_ready"), 2)
            units([], lambda t, hd, b: mm(b, dl[:, 56 + 4 * t + hd:57 + 4 * t + hd].to_broadcast([P, P]), U_c,
                                          start=True, stop=True), 2)
            proj2(8)
            proj2(9)
            pe.wait_ge(S("qkv_ready"), 8)
            pe.wait_ge(S("gcol_ready"), 1)
            units([], lambda t, hd, b: nc.tensor.transpose(b, k_(t, hd), ident), 6)
            proj2(10)
            pe.wait_ge(S("sq8_ready"), 2)
            for i in range(2):
                for t in range(TT):
                    for hd in range(GH):
                        o = 8 * i + 4 * t + hd
                        last = mm(bank(4)[:, o:o + 1], sq8[:, 4 * i + hd, t * P:t * P + P], ones[:, 0:1], start=True,
                                  stop=True)
            last.then_inc(S("qk_mm"), 1)
            pe.wait_ge(S("qk_root"), 1)
            units([], lambda t, hd, b: mm(b, k_(t, hd), k_(t, hd), start=True, stop=True), 4)
            proj2(11)
            proj2(12)
            pe.wait_ge(S("brk_ready"), 1)
            units([("expg_ready", (1, 2)), ("dec_arg", (1, 2))],
                  lambda t, hd, b: mm(b, dl[:, 120 + 4 * t + hd:121 + 4 * t + hd].to_broadcast([P, P]), ident,
                                      start=True, stop=True), 2)
            pe.wait_ge(S("qkv_ready"), 12)
            units([("k_used", (4, 8)), ("kdec_ready", (1, 2))],
                  lambda t, hd, b: nc.tensor.transpose(b, qkv[:, 8 + hd, t * P:t * P + P], ident), 6)
            proj2(13)
            units([("kk_used", (1, 2))],
                  lambda t, hd, b: mm(b, k_(t, hd), qkv[:, hd, t * P:t * P + P], start=True, stop=True), 4)
            proj2(14)
            proj2(15)
            for t in range(TT):
                pe.wait_ge(S("attn_ready"), t + 1)
                pe.wait_ge(S("ttm_ready"), t + 1)
                for hd in range(GH):
                    last = nc.tensor.transpose(bank(4 + t)[:, hd * P:hd * P + P], ttm[:, 4 * t + hd, :], ident)
                last.then_inc(S("merge0_mm"), 1)
            pe.wait_ge(S("proj2_ev"), 16)
            for lv in range(1, LEVELS):
                for t in range(TT):
                    pe.wait_ge(S("lm_ready"), TT * (lv - 1) + t + 1)
                    if lv == 1:
                        pe.wait_ge(S("tm0_ready"), t + 1)
                    else:
                        pe.wait_ge(S("tm_ready"), TT * (lv - 2) + t + 1)
                    for hd in range(GH):
                        u = 4 * t + hd
                        last = mm(bank(t)[:, hd * P:hd * P + P], lm[:, u, :], tm[:, u, :], start=True, stop=True)
                    last.then_inc(S("merge_p_mm"), 1)
                for t in range(TT):
                    pe.wait_ge(S("pm_ready"), TT * (lv - 1) + t + 1)
                    pe.wait_ge(S("ttm_ready"), TT * (lv - 1) + t + 1)
                    if lv < LEVELS - 1:
                        for hd in range(GH):
                            u = 4 * t + hd
                            last = mm(bank(4 + t)[:, hd * P:hd * P + P], ttm[:, u, :], pm[:, u, :], start=True,
                                      stop=True)
                        last.then_inc(S("merge_t_mm"), 1)
                    for hd in range(GH):
                        u = 4 * t + hd
                        last = mm(bank(2 + t)[:, hd * P:hd * P + P], pm[:, u, :], ttm[:, u, :], start=True, stop=True)
                    last.then_inc(S("merge_tt_mm"), 1)
            for t in range(TT):
                pe.wait_ge(S("ttm_ready"), TT * (LEVELS - 1) + t + 1)
                for hd in range(GH):
                    u = 4 * t + hd
                    last = mm(bank(4 + t)[:, hd * P:hd * P + P], kbe[:, u, :], ttm[:, u, :], start=True, stop=True)
                last.then_inc(S("wt_mm"), 1)
            pe.wait_ge(S("v_used"), 2)
            proj2(16)
            pe.wait_ge(S("wt_ready"), 2)
            pe.wait_ge(S("qdec_ready"), 8)
            for n in range(NCH):
                t, o = n // 2, 64 * (n % 2)
                q = slice(o, o + 64)
                if n >= 1:
                    pe.wait_ge(S("state_ready"), 4 * n)
                if n >= 2:
                    pe.wait_ge(S("o_ready"), n - 1)
                for hd in range(GH):
                    u = 4 * t + hd
                    dst = bank(n % 2)[q, hd * P:hd * P + P]
                    last = mm(dst, ttm[q, u, o:o + 64], vb[q, u, :], start=True, stop=n == 0)
                    if n > 0:
                        last = mm(dst, wtn[:, u, o:o + 64], state[:, hd, :], start=False, stop=True)
                last.then_inc(S("vnew_mm"), 1)
                proj2(17 + 2 * n)
                pe.wait_ge(S("vnew_ready"), n + 1)
                if n < NCH - 1:
                    for hd in range(GH):
                        u = 4 * t + hd
                        last = mm(bank(6 + n % 2)[:, hd * P:hd * P + P], kdec[q, u, :], vnew[q, hd, :], start=True,
                                  stop=True)
                    last.then_inc(S("state_mm"), 1)
                for hd in range(GH):
                    u = 4 * t + hd
                    dst = bank(2 + n % 2)[:, 64 * hd:64 * hd + 64]
                    last = mm(dst, vnew[q, hd, :], attn_t[q, u, o:o + 64], start=True, stop=n == 0)
                    if n > 0:
                        last = mm(dst, state[:, hd, :], qkv[:, hd, 64 * n:64 * n + 64], start=False, stop=True)
                last.then_inc(S("out_mm"), 1)
                proj2(18 + 2 * n)
            proj2(25)
            proj2(26)
            pe.wait_ge(S("osq_ready"), 1)
            for t in range(TT):
                for hd in range(GH):
                    o = 4 * t + hd
                    last = mm(bank(7)[:, o:o + 1], o_sq[:, hd, t * P:t * P + P], ones[:, 0:1], start=True, stop=True)
            last.then_inc(S("osum_mm"), 1)
            proj2(27)
            pe.wait_ge(S("fac_ready"), 1)
            pe.wait_ge(S("o_ready"), NCH)
            for hd in range(GH):
                for t in range(TT):
                    o, to = 128 + 4 * t + hd, (hd % 2) * T + t * P
                    last = mm(bank(2 + hd // 2)[:, to:to + P], dl[:, o:o + 1].to_broadcast([P, P]), ident,
                              start=True, stop=True)
            last.then_inc(S("fac_mm"), 1)
            def split_out_product(n, pieces, hi, lo, norm, ready=None):
                for m in range(KD):
                    if m >= 2:
                        pe.wait_ge(S("res_used"), KD * n + m - 1)
                    for j, ks in enumerate(pieces):
                        split_product(bank(6 + m % 2)[:, 0:T], hi, lo, ks, j == 0, j == len(pieces) - 1,
                                      ready if m == 0 else None)
                sums(norm)
                pe.wait_ge(S("rcol_ready"), norm + 1)
                spread(0, 0)

            split_out_product(1, [[4, 5, 6, 7, 0, 1, 2, 3]], lambda k: y_hi[k // 4][:, k % 4, :],
                              lambda k: y_lo[:, k, :], 3,
                              lambda k: ("y2_ready", 4 if k >= 4 else 5 + k // 2))
            for f in range(NFF):
                if f >= 2:
                    pe.wait_ge(S("hff_used"), f - 1)
                for b in (2 * (f % 2) + 2, 2 * (f % 2) + 3):
                    split_product(bank(b)[:, 0:T], lambda k: f_hi[:, k, :], lambda k: f_lo[:, k, :], range(KD),
                                  ready=(lambda k: ("parts_ready", KD + k + 1)) if (f, b) == (0, 2) else None)
            pe.wait_ge(S("hff_ready"), NFF)
            split_out_product(2, [range(0, 8), range(8, 16), range(16, NFF)], lambda k: hf_hi[:, k, :],
                              lambda k: hf_lo[:, k, :], 4)


def _tiles(w):
    r, n = w.shape
    return np.ascontiguousarray(w.reshape(r // P, P, n).transpose(1, 0, 2)).reshape(P, (r // P) * n)


def _cols(v):
    return v.reshape(-1, P).T


def _constants():
    i = np.arange(P)
    const = np.zeros((P, NCONST), np.float32)
    const[:, CONST["ident"][0]:CONST["ident"][1]] = np.eye(P)
    const[:, CONST["tri"][0]:CONST["tri"][1]] = i[:, None] < i[None, :]
    const[:, CONST["iota"][0]:CONST["iota"][1]] = np.arange(CAP)
    const[:, CONST["prio"][0]:CONST["prio"][1]] = 8 - np.arange(8)
    aconst = np.zeros((P, 4, T), np.float32)
    s = np.arange(T)
    for qb in range(2):
        aconst[:, qb] = np.where((s[None, :] // CHUNK) <= ((qb * P + i[:, None]) // CHUNK), 0.0, MASKED)
    for c in range(2):
        for half in range(2):
            w = (2, 4, 8, 16)[2 * c + half]
            aconst[64 * half:64 * half + 64, 2 + c] = 1.0 / np.minimum(s + 1, w)
    g = np.zeros((P, 3 + LEVELS, P), np.float32)
    same = (i[:, None] // CHUNK) == (i[None, :] // CHUNK)
    g[:, 0] = same & (i[:, None] <= i[None, :])
    g[:, 1] = same
    g[:, 2] = np.where(same & (i[:, None] <= i[None, :]), 0.0, MASKED)
    for lv in range(LEVELS):
        b = 1 << lv
        pair = (i[:, None] // (2 * b)) == (i[None, :] // (2 * b))
        g[:, 3 + lv] = pair & ((i[:, None] // b) % 2 == 0) & ((i[None, :] // b) % 2 == 1)
    return const, aconst, g


def kernel(**inp):
    from concourse import bacc
    from concourse.bass_utils import run_bass_kernel_spmd

    inp = {k: np.asarray(v) for k, v in inp.items()}
    C = np.ascontiguousarray

    def passes(w):
        return C(w.reshape(2, 4, P, 3, 2048).transpose(3, 0, 2, 1, 4)).reshape(6, P, SLOT)

    win = inp["w_in"][0]
    ki = win[:, 1408:1472]
    wa = np.concatenate([ki, ki, win[:, 896:1408], win[:, 512:896]], axis=1)
    wb = np.concatenate([win[:, 0:512], win[:, 1480:1736], win[:, 1472:1480]], axis=1)
    w2 = inp["w_in_2"][0]
    gate, up, down = inp["w_gate_2"][0], inp["w_up_2"][0], inp["w_down_2"][0]
    ffu = np.stack([_tiles(np.concatenate([gate[:, 512 * i:512 * i + 512], up[:, 512 * i:512 * i + 512]], axis=1))
                    for i in range(5)])
    vectors = [_cols(inp["c"][0]), _cols(inp["c_2"][0]), _cols(inp["mod_b"][0]), _cols(inp["b_ada_2"][0]),
               _cols(inp["norm1_g"][0]), _cols(inp["norm2_g"][0]), _cols(inp["final_g"]), _cols(inp["norm1_w_2"][0]),
               _cols(inp["norm2_w_2"][0]), _cols(inp["norm_f_w_2"]), _cols(inp["conv_b"][0]),
               _cols(inp["conv_ln_g"][0]), _cols(inp["conv_ln_b"][0]), _cols(inp["q_norm_g"][0]),
               _cols(inp["kv_norm_g"][0]), _cols(inp["pool_scale"][0]),
               inp["conv_k"][0].reshape(CONV_W, 2, P).transpose(2, 1, 0).reshape(P, 2 * CONV_W),
               inp["conv_qkv_w_2"][0].reshape(4, 12, P).transpose(2, 1, 0).reshape(P, 48),
               inp["conv_short_w_2"][0].reshape(3, 4, P).transpose(2, 1, 0).reshape(P, 12),
               _cols(inp["gdn_norm_w_2"][0]),
               np.broadcast_to(inp["router_g_b"][0].reshape(1, 4), (P, 4)),
               np.broadcast_to(inp["router_e_b"][0].reshape(1, 32), (P, 32)),
               np.broadcast_to(inp["A_log_2"][0].reshape(1, 4), (P, 4)),
               np.broadcast_to(inp["dt_bias_2"][0].reshape(1, 4), (P, 4)), _tiles(w2[:, 2048:2056])]
    pool_w = inp["pool_w"][0].reshape(2, 2, 64, 64).transpose(1, 2, 0, 3).reshape(P, 128)
    router = np.concatenate([inp["router_g_w"][0], inp["router_e_w"][0].reshape(D, E)], axis=1)
    uk = inp["w_uk"][0].transpose(1, 2, 0).reshape(4, P, P).transpose(1, 0, 2).reshape(P, 512)
    smallw = [_tiles(inp["w_uq"][0].reshape(256, 512)), uk, inp["w_uv"][0].reshape(P, 512), pool_w, _tiles(router)]
    const, aconst, gconst = _constants()

    def experts(w):
        e, r, n = w.shape
        return C(w.reshape(e, r // P, P, n).transpose(0, 2, 1, 3)).reshape(e, P, (r // P) * n)

    arrays = {
        "xT": C(inp["x"][0].T.reshape(KD, P, T).transpose(1, 0, 2)),
        "mod_w": passes(inp["mod_w"][0]), "ada_w": passes(inp["w_ada_2"][0]),
        "winA": _tiles(wa), "winB": _tiles(wb), "wout": _tiles(inp["w_out"][0]),
        "ew1": experts(inp["exp_w1"][0]), "ew3": experts(inp["exp_w3"][0]), "ew2": experts(inp["exp_w2"][0]),
        "w2A": _tiles(w2[:, 0:1024]), "w2B": _tiles(w2[:, 1024:2048]), "w2C": _tiles(w2[:, 2056:3080]),
        "w2D": _tiles(w2[:, 3080:3592]),
        "wout2": _tiles(inp["w_out_2"][0]),
        "ffu": ffu, "ffu_last": _tiles(np.concatenate([gate[:, 2560:], up[:, 2560:]], axis=1)),
        "ffd": np.stack([_tiles(down[0:1024]), _tiles(down[1024:2048])]), "ffd_last": _tiles(down[2048:]),
        "cols_d": C(np.concatenate(vectors, axis=1)), "small_d": C(np.concatenate(smallw, axis=1)),
        "const_d": const, "aconst_d": aconst, "gconst_d": gconst,
    }
    nc = bacc.Bacc("TRN2", target_bir_lowering=False, num_devices=1)
    aps = {k: nc.dram_tensor("in_" + k, a.shape, mybir.dt.from_np(a.dtype), kind="ExternalInput").ap()
           for k, a in arrays.items()}
    out = nc.dram_tensor("out_dram", (P, KD, T), mybir.dt.float32, kind="ExternalOutput").ap()
    program(nc, out=out, **aps)
    r = run_bass_kernel_spmd(nc, [{"in_" + k: a for k, a in arrays.items()}], core_ids=[0])
    got = r.results[0]["out_dram"]
    return np.ascontiguousarray(got.transpose(1, 0, 2).reshape(D, T).T).reshape(1, T, D)
```
